# Optimizing a Trainium2 kernel written in Bass

```python
import functools
import jax, jax.numpy as jnp
from jax import lax
import numpy as np

D_MODEL = 1024
BATCH = 1
SEQ = 256
DEPTH = 1
DEC_BATCH = 8
DEC_SEQ = 1
PAST_LEN = 1024
PAGE_SIZE = 128

D_RNN = 1024
N_LRU_BLOCKS = 4
LRU_BLOCK = D_RNN // N_LRU_BLOCKS
CONV_W = 4
LRU_C = 8.0
HEAD_DIM = 128
HEADS_PER_GROUP = 4
GROUPS = ((128, 1), (512, 4), (2048, 16))
N_GROUPS = len(GROUPS)
N_HEADS = N_GROUPS * HEADS_PER_GROUP
QKV_W = N_HEADS * HEAD_DIM
ATT_OUT = HEADS_PER_GROUP * HEAD_DIM
ROT_DIM = HEAD_DIM // 4
ROPE_THETA = 500000.0
N_EXPERTS = 32
TOP_K = 4
D_FF = 1024
SWIGLU_LIMIT = 7.0
SWIGLU_ALPHA = 1.702
MOE_BLOCK = 128
PLE_DIM = 256
EPS = 1e-6
IN_SIZES = (D_RNN, D_RNN, QKV_W, QKV_W, QKV_W, D_MODEL, D_MODEL)
N_IN = sum(IN_SIZES)

kernel_name = 'hybrid_rglru_dilated_swa_moe_step'

def rmsnorm(x, g):
    xf = x.astype(jnp.float32)
    y = xf * lax.rsqrt(jnp.mean(xf * xf, axis=-1, keepdims=True) + EPS)
    return (y * g.astype(jnp.float32)).astype(x.dtype)

def partial_rope(x, pos):
    half = ROT_DIM // 2
    freqs = jnp.float32(ROPE_THETA) ** (-jnp.arange(half, dtype=jnp.float32) * (2.0 / ROT_DIM))
    ang = pos.astype(jnp.float32)[:, None] * freqs[None, :]
    cos = jnp.cos(ang)[None, :, None, :]
    sin = jnp.sin(ang)[None, :, None, :]
    xf = x.astype(jnp.float32)
    x1 = xf[..., :half]
    x2 = xf[..., half:ROT_DIM]
    out = jnp.concatenate([x1 * cos - x2 * sin, x2 * cos + x1 * sin, xf[..., ROT_DIM:]], axis=-1)
    return out.astype(x.dtype)

def causal_conv(x, buf, w, b):
    T = x.shape[1]
    xp = jnp.concatenate([buf.astype(x.dtype), x], axis=1)
    y = sum(xp[:, k:k + T] * w[k] for k in range(CONV_W)) + b
    return y, xp[:, -(CONV_W - 1):]

def rglru(x, h0, w_a, b_a, w_x, b_x, lam):
    xf = x.astype(jnp.float32)
    xb = xf.reshape(*xf.shape[:-1], N_LRU_BLOCKS, LRU_BLOCK)
    r = jax.nn.sigmoid(jnp.einsum('btnc,ncd->btnd', xb, w_a.astype(jnp.float32)).reshape(xf.shape) + b_a.astype(jnp.float32))
    i = jax.nn.sigmoid(jnp.einsum('btnc,ncd->btnd', xb, w_x.astype(jnp.float32)).reshape(xf.shape) + b_x.astype(jnp.float32))
    log_a = -LRU_C * r * jax.nn.softplus(-lam.astype(jnp.float32))
    a = jnp.exp(log_a)
    u = jnp.sqrt(-jnp.expm1(2.0 * log_a)) * (i * xf)

    def step(h, au):
        a_t, u_t = au
        h = a_t * h + u_t
        return h, h

    h_last, hs = lax.scan(step, h0.astype(jnp.float32), (a.transpose(1, 0, 2), u.transpose(1, 0, 2)))
    return hs.transpose(1, 0, 2).astype(x.dtype), h_last.astype(h0.dtype)

def band_dilated_attention(q, k, v, window, dil):
    B, S, H, D = q.shape
    bl = window // dil
    span = bl * dil
    s_pad = -(-S // span) * span
    nb = s_pad // span

    def blocks(t):
        t = jnp.pad(t, ((0, 0), (0, s_pad - S), (0, 0), (0, 0)))
        t = t.reshape(B, nb * bl, dil, H, D).transpose(0, 2, 1, 3, 4)
        return t.reshape(B, dil, nb, bl, H, D)

    def with_prev(t):
        prev = jnp.pad(t, ((0, 0), (0, 0), (1, 0), (0, 0), (0, 0), (0, 0)))[:, :, :nb]
        return jnp.concatenate([prev, t], axis=3)

    qb = blocks(q).astype(jnp.float32)
    k2 = with_prev(blocks(k)).astype(jnp.float32)
    v2 = with_prev(blocks(v)).astype(jnp.float32)
    s = jnp.einsum('brnqhd,brnkhd->brnhqk', qb, k2) * (HEAD_DIM ** -0.5)
    qi = jnp.arange(bl)[:, None] + bl
    kj = jnp.arange(2 * bl)[None, :]
    rel = qi - kj
    band = (rel >= 0) & (rel <= bl)
    has_prev = (jnp.arange(nb)[:, None, None] > 0) | (kj[None] >= bl)
    mask = band[None] & has_prev
    s = jnp.where(mask[None, None, :, None], s, -jnp.inf)
    lse = jax.nn.logsumexp(s, axis=-1)
    p = jnp.exp(s - lse[..., None])
    o = jnp.einsum('brnhqk,brnkhd->brnqhd', p, v2)
    o = o.reshape(B, dil, nb * bl, H, D).transpose(0, 2, 1, 3, 4).reshape(B, s_pad, H, D)[:, :S]
    lse = lse.transpose(0, 1, 2, 4, 3).reshape(B, dil, nb * bl, H).transpose(0, 2, 1, 3).reshape(B, s_pad, H)[:, :S]
    return o, lse

def gathered_dilated_attention(q, k_all, v_all, n_past, window, dil):
    T = q.shape[1]
    nk = window // dil + 1
    idx = n_past + jnp.arange(T)[:, None] - dil * jnp.arange(nk)[None, :]
    valid = idx >= 0
    idx = jnp.maximum(idx, 0)
    kg = k_all[:, idx].astype(jnp.float32)
    vg = v_all[:, idx].astype(jnp.float32)
    s = jnp.einsum('bthd,btjhd->bthj', q.astype(jnp.float32), kg) * (HEAD_DIM ** -0.5)
    s = jnp.where(valid[None, :, None, :], s, -jnp.inf)
    lse = jax.nn.logsumexp(s, axis=-1)
    p = jnp.exp(s - lse[..., None])
    o = jnp.einsum('bthj,btjhd->bthd', p, vg)
    return o, lse

def combine_groups(outs, lses, dtype):
    o = jnp.stack(outs, axis=0)
    w = jax.nn.softmax(jnp.stack(lses, axis=0), axis=0)
    att = jnp.sum(w[..., None] * o, axis=0)
    B, T = att.shape[:2]
    return att.reshape(B, T, ATT_OUT).astype(dtype)

def attend_prompt(q, k, v):
    S = q.shape[1]
    outs, lses, news = [], [], []
    for g, (window, dil) in enumerate(GROUPS):
        sl = slice(g * HEADS_PER_GROUP, (g + 1) * HEADS_PER_GROUP)
        o, lse = band_dilated_attention(q[:, :, sl], k[:, :, sl], v[:, :, sl], window, dil)
        outs.append(o)
        lses.append(lse)
        wp = min(window, S)
        news.append(jnp.stack([k[:, S - wp:, sl], v[:, S - wp:, sl]], axis=2))
    return combine_groups(outs, lses, q.dtype), news

def attend_sample(q, k, v, caches):
    outs, lses, news = [], [], []
    for g, (window, dil) in enumerate(GROUPS):
        sl = slice(g * HEADS_PER_GROUP, (g + 1) * HEADS_PER_GROUP)
        cache = caches[g]
        wb = cache.shape[1]
        k_all = jnp.concatenate([cache[:, :, 0], k[:, :, sl].astype(cache.dtype)], axis=1)
        v_all = jnp.concatenate([cache[:, :, 1], v[:, :, sl].astype(cache.dtype)], axis=1)
        o, lse = gathered_dilated_attention(q[:, :, sl], k_all, v_all, wb, window, dil)
        outs.append(o)
        lses.append(lse)
        news.append(jnp.stack([k_all[:, -wb:], v_all[:, -wb:]], axis=2))
    return combine_groups(outs, lses, q.dtype), news

def moe(x, w_router, b_router, w_gu, b_gu, w_down, b_down):
    N, D = x.shape
    logits = x.astype(jnp.float32) @ w_router.astype(jnp.float32) + b_router.astype(jnp.float32)
    top_v, top_e = lax.top_k(logits, TOP_K)
    gates = jax.nn.softmax(top_v, axis=-1)
    na = N * TOP_K
    flat_e = top_e.reshape(na)
    order = jnp.argsort(flat_e)
    sorted_e = flat_e[order]
    sorted_tok = order // TOP_K
    counts = jnp.bincount(flat_e, length=N_EXPERTS)
    padded = (counts + MOE_BLOCK - 1) // MOE_BLOCK * MOE_BLOCK
    pad_end = jnp.cumsum(padded)
    pad_start = pad_end - padded
    start = jnp.cumsum(counts) - counts
    dest = pad_start[sorted_e] + jnp.arange(na) - start[sorted_e]
    nb = -(-na // MOE_BLOCK) + N_EXPERTS
    rows = nb * MOE_BLOCK
    row_tok = jnp.full((rows,), N, jnp.int32).at[dest].set(sorted_tok.astype(jnp.int32))
    row_gate = jnp.zeros((rows,), jnp.float32).at[dest].set(gates.reshape(na)[order])
    blk_e = jnp.minimum(jnp.searchsorted(pad_end, jnp.arange(nb) * MOE_BLOCK, side='right'), N_EXPERTS - 1)
    xpad = jnp.concatenate([x, jnp.zeros((1, D), x.dtype)], axis=0)
    xb = xpad[row_tok].reshape(nb, MOE_BLOCK, D)

    def expert_rows(args):
        xblk, e = args
        gu = xblk @ w_gu[e] + b_gu[e]
        gate = jnp.minimum(gu[:, :D_FF], SWIGLU_LIMIT)
        up = jnp.clip(gu[:, D_FF:], -SWIGLU_LIMIT, SWIGLU_LIMIT)
        hmid = (up + 1.0) * (gate * jax.nn.sigmoid(SWIGLU_ALPHA * gate))
        return hmid @ w_down[e] + b_down[e]

    yb = lax.map(expert_rows, (xb, blk_e))
    y = yb.reshape(rows, D) * row_gate[:, None].astype(x.dtype)
    return jnp.zeros((N + 1, D), x.dtype).at[row_tok].add(y)[:N]

def layer(x, ple, conv_buf, h0, pos, attend, lw):
    B, T, _ = x.shape
    h = rmsnorm(x, lw['g_mix'])
    z = h @ lw['w_in']
    xr, gr, q, k, v, g_lru, g_att = jnp.split(z, np.cumsum(IN_SIZES)[:-1].tolist(), axis=-1)
    xc, conv_new = causal_conv(xr, conv_buf, lw['conv_w'], lw['conv_b'])
    yr, h_new = rglru(xc, h0, lw['w_rg_a'], lw['b_rg_a'], lw['w_rg_x'], lw['b_rg_x'], lw['lru_lambda'])
    b_lru = (yr * jax.nn.gelu(gr)) @ lw['w_br_lru']
    q = partial_rope(rmsnorm(q.reshape(B, T, N_HEADS, HEAD_DIM), lw['g_q']), pos)
    k = partial_rope(rmsnorm(k.reshape(B, T, N_HEADS, HEAD_DIM), lw['g_k']), pos)
    v = v.reshape(B, T, N_HEADS, HEAD_DIM)
    att, kv_new = attend(q, k, v)
    b_att = att @ lw['w_br_att']
    merged = jax.nn.sigmoid(g_lru) * b_lru + jax.nn.sigmoid(g_att) * b_att
    x = x + merged @ lw['w_out']
    hf = rmsnorm(x, lw['g_ffn'])
    x = x + moe(hf.reshape(B * T, D_MODEL), lw['w_router'], lw['b_router'], lw['w_gu'], lw['b_gu'], lw['w_down'], lw['b_down']).reshape(B, T, D_MODEL)
    x = x + jax.nn.sigmoid(rmsnorm(x, lw['g_ple']) @ lw['w_ple_gate']) * (ple.astype(x.dtype) @ lw['w_ple'])
    return x, kv_new, conv_new, h_new

def setup_inputs(seed: int = 0) -> dict:
    key = jax.random.key(seed)
    ks = iter(jax.random.split(key, 40))

    def nrm(shape, scale=1.0):
        return jax.random.normal(next(ks), shape, jnp.float32) * scale

    L = DEPTH
    wbs = [min(w, PAST_LEN) for w, _ in GROUPS]
    a0 = jax.random.uniform(next(ks), (L, D_RNN), jnp.float32, 0.9, 0.999)
    s0 = a0 ** (1.0 / LRU_C)
    lru_lambda = jnp.log(s0) - jnp.log1p(-s0)
    return {
        'x_prompt': nrm((BATCH, SEQ, D_MODEL)),
        'x_sample': nrm((DEC_BATCH, DEC_SEQ, D_MODEL)),
        'cache_kv_g0': nrm((L, DEC_BATCH, wbs[0], 2, HEADS_PER_GROUP, HEAD_DIM)),
        'cache_kv_g1': nrm((L, DEC_BATCH, wbs[1], 2, HEADS_PER_GROUP, HEAD_DIM)),
        'cache_kv_g2': nrm((L, DEC_BATCH, wbs[2], 2, HEADS_PER_GROUP, HEAD_DIM)),
        'state_conv': nrm((L, DEC_BATCH, CONV_W - 1, D_RNN)),
        'state_h': nrm((L, DEC_BATCH, D_RNN), 0.5),
        'p_prompt': nrm((L, BATCH, SEQ, PLE_DIM)),
        'p_sample': nrm((L, DEC_BATCH, DEC_SEQ, PLE_DIM)),
        'g_mix': 1.0 + nrm((L, D_MODEL), 0.02),
        'w_in': nrm((L, D_MODEL, N_IN), D_MODEL ** -0.5),
        'conv_w': nrm((L, CONV_W, D_RNN), CONV_W ** -0.5),
        'conv_b': nrm((L, D_RNN), 0.01),
        'w_rg_a': nrm((L, N_LRU_BLOCKS, LRU_BLOCK, LRU_BLOCK), LRU_BLOCK ** -0.5),
        'b_rg_a': nrm((L, D_RNN), 0.01),
        'w_rg_x': nrm((L, N_LRU_BLOCKS, LRU_BLOCK, LRU_BLOCK), LRU_BLOCK ** -0.5),
        'b_rg_x': nrm((L, D_RNN), 0.01),
        'lru_lambda': lru_lambda,
        'g_q': 1.0 + nrm((L, HEAD_DIM), 0.02),
        'g_k': 1.0 + nrm((L, HEAD_DIM), 0.02),
        'w_br_lru': nrm((L, D_RNN, D_MODEL), D_RNN ** -0.5),
        'w_br_att': nrm((L, ATT_OUT, D_MODEL), ATT_OUT ** -0.5),
        'w_out': nrm((L, D_MODEL, D_MODEL), D_MODEL ** -0.5),
        'g_ffn': 1.0 + nrm((L, D_MODEL), 0.02),
        'w_router': nrm((L, D_MODEL, N_EXPERTS), D_MODEL ** -0.5),
        'b_router': nrm((L, N_EXPERTS), 0.01),
        'w_gu': nrm((L, N_EXPERTS, D_MODEL, 2 * D_FF), D_MODEL ** -0.5),
        'b_gu': nrm((L, N_EXPERTS, 2 * D_FF), 0.01),
        'w_down': nrm((L, N_EXPERTS, D_FF, D_MODEL), D_FF ** -0.5),
        'b_down': nrm((L, N_EXPERTS, D_MODEL), 0.01),
        'g_ple': 1.0 + nrm((L, D_MODEL), 0.02),
        'w_ple_gate': nrm((L, D_MODEL, D_MODEL), D_MODEL ** -0.5),
        'w_ple': nrm((L, PLE_DIM, D_MODEL), PLE_DIM ** -0.5),
    }

def reference(x_prompt, x_sample, cache_kv_g0, cache_kv_g1, cache_kv_g2, state_conv, state_h, p_prompt, p_sample,
              g_mix, w_in, conv_w, conv_b, w_rg_a, b_rg_a, w_rg_x, b_rg_x, lru_lambda, g_q, g_k,
              w_br_lru, w_br_att, w_out, g_ffn, w_router, b_router, w_gu, b_gu, w_down, b_down,
              g_ple, w_ple_gate, w_ple):
    B, S, _ = x_prompt.shape
    T = x_sample.shape[1]
    pos_p = jnp.arange(S, dtype=jnp.int32)
    pos_s = PAST_LEN + jnp.arange(T, dtype=jnp.int32)
    xp, xs = x_prompt, x_sample
    kvp = [[], [], []]
    kvs = [[], [], []]
    conv_p, h_p, conv_s, h_s = [], [], [], []
    for l in range(DEPTH):
        lw = dict(g_mix=g_mix[l], w_in=w_in[l], conv_w=conv_w[l], conv_b=conv_b[l], w_rg_a=w_rg_a[l],
                  b_rg_a=b_rg_a[l], w_rg_x=w_rg_x[l], b_rg_x=b_rg_x[l], lru_lambda=lru_lambda[l],
                  g_q=g_q[l], g_k=g_k[l], w_br_lru=w_br_lru[l], w_br_att=w_br_att[l], w_out=w_out[l],
                  g_ffn=g_ffn[l], w_router=w_router[l], b_router=b_router[l], w_gu=w_gu[l], b_gu=b_gu[l],
                  w_down=w_down[l], b_down=b_down[l], g_ple=g_ple[l], w_ple_gate=w_ple_gate[l], w_ple=w_ple[l])
        conv0 = jnp.zeros((B, CONV_W - 1, D_RNN), xp.dtype)
        h0 = jnp.zeros((B, D_RNN), xp.dtype)
        xp, kv_new_p, cp, hp = layer(xp, p_prompt[l], conv0, h0, pos_p, attend_prompt, lw)
        caches = (cache_kv_g0[l], cache_kv_g1[l], cache_kv_g2[l])
        xs, kv_new_s, cs, hs = layer(xs, p_sample[l], state_conv[l], state_h[l], pos_s,
                                     functools.partial(attend_sample, caches=caches), lw)
        for g in range(N_GROUPS):
            kvp[g].append(kv_new_p[g])
            kvs[g].append(kv_new_s[g])
        conv_p.append(cp)
        h_p.append(hp)
        conv_s.append(cs)
        h_s.append(hs)
    return (xp, xs,
            jnp.stack(kvp[0]), jnp.stack(kvp[1]), jnp.stack(kvp[2]), jnp.stack(conv_p), jnp.stack(h_p),
            jnp.stack(kvs[0]), jnp.stack(kvs[1]), jnp.stack(kvs[2]), jnp.stack(conv_s), jnp.stack(h_s))


_drawn_inputs = setup_inputs


def setup_inputs(seed=0):
    import zlib

    import numpy as np

    out = dict(_drawn_inputs(seed))
    spreads = {}
    factors = {'g_mix': 2.785,
     'b_rg_a': 26.754,
     'b_rg_x': 22.699,
     'g_q': 4.609,
     'g_k': 4.121,
     'b_gu': 8.0,
     'b_down': 31.106,
     'g_ple': 200.0,
     'g_ffn': 2.685}
    for name, (base, spread) in spreads.items():
        noise = np.random.default_rng([zlib.crc32(name.encode()), seed]).standard_normal(out[name].shape)
        drawn = base * np.exp(spread * noise) if base else spread * noise
        out[name] = __import__('jax').numpy.asarray(drawn.astype(out[name].dtype))
    for name, factor in factors.items():
        out[name] = (out[name] * factor).astype(out[name].dtype)
    return out
```

```python
from contextlib import ExitStack

import concourse.bass as bass
from concourse import mybir

P = 128
D = 1024
KT = D // P
NP, NS = 256, 8
T = NP + NS
HD = 128
HPG = 4
NG = 3
NHEAD = NG * HPG
E = 32
TOPK = 4
NFEAT = 43
BLK = [(0, 128), (128, 128), (256, NS)]
WB = (128, 512, 1024)
DIL = (1, 4, 16)
SKEYS = (128, 128, 64)
CH = 512
NPIECE = 17
LOOP_A = 8
ZQ, ZK, ZX, ZGR, ZV, ZGL, ZGA = 0, 12, 24, 32, 40, 52, 60
NZ = 68
SCALE = HD ** -0.5
LIMIT, ALPHA, LRU_C = 7.0, 1.702, 8.0
FW, FCB, FBA, FBX, FLAM, FGM, FGF, FGP, FSC, FSH = 0, 4, 5, 6, 7, 8, 9, 10, 11, 35
C_ID, C_ONE, C_TRI, C_MASK0, C_MASK1 = 0, 128, 256, 384, 768
C_IOTA, C_EOFF, C_ETAB, C_TOK, C_VALID, C_EPS, NCST = 1536, 1568, 1600, 1632, 1635, 1638, 1640
CAP = 128
TK_OUT = (0, 32, 80, 128, 176)
VT_OUT = 80
NCHUNK = 3
ROWS = NCHUNK * E * CAP

ALU = mybir.AluOpType
ACT = mybir.ActivationFunctionType
AX = mybir.AxisListType.X
F32 = mybir.dt.float32
I32 = mybir.dt.int32
U32 = mybir.dt.uint32


class Signals:

    def __init__(self, sem):
        self.sq_ok = sem("sq_ok")
        self.ss_sum = sem("ss_sum")
        self.rms_ok = sem("rms_ok")
        self.h_ok = sem("h_ok")
        self.v_in = sem("v_in")
        self.cst_in = sem("cst_in")
        self.x_in = sem("x_in")
        self.rope_in = sem("rope_in")
        self.win0 = sem("win0")
        self.win1 = sem("win1")
        self.win2 = sem("win2")
        self.win3 = sem("win3")
        self.z_done = sem("z_done")
        self.z_evac = sem("z_evac")
        self.sq_qk = sem("sq_qk")
        self.qkn_mm = sem("qkn_mm")
        self.qkn_ev = sem("qkn_ev")
        self.qk_normed = sem("qk_normed")
        self.rot_in = sem("rot_in")
        self.roped = sem("roped")
        self.conv_done = sem("conv_done")
        self.conv_out = sem("conv_out")
        self.wrg_in = sem("wrg_in")
        self.gate_mm = sem("gate_mm")
        self.gate_ev = sem("gate_ev")
        self.kt0_in = sem("kt0_in")
        self.kt1_in = sem("kt1_in")
        self.kt2_in = sem("kt2_in")
        self.ss_mm = sem("ss_mm")
        self.ss_ev = sem("ss_ev")
        self.ss_prod = sem("ss_prod")
        self.ss_rows = sem("ss_rows")
        self.sp_exp = sem("sp_exp")
        self.sp_ready = sem("sp_ready")
        self.st_mm = sem("st_mm")
        self.st_ev = sem("st_ev")
        self.sd_ready = sem("sd_ready")
        self.sb_mm = sem("sb_mm")
        self.sb_ev = sem("sb_ev")
        self.spv_mm = sem("spv_mm")
        self.satt = sem("satt")
        self.tk_mm = sem("tk_mm")
        self.tk_ev = sem("tk_ev")
        self.tk_out = sem("tk_out")
        self.vt_out = sem("vt_out")
        self.h_out = sem("h_out")
        self.at_sc = sem("at_sc")
        self.at_s = sem("at_s")
        self.at_nm = sem("at_nm")
        self.at_e = sem("at_e")
        self.at_p = sem("at_p")
        self.at_t = sem("at_t")
        self.at_pt = sem("at_pt")
        self.at_pv = sem("at_pv")
        self.at_ev = sem("at_ev")
        self.nsp = sem("nsp")
        self.lru_l = sem("lru_l")
        self.lru_th = sem("lru_th")
        self.lru_e = sem("lru_e")
        self.lru_c = sem("lru_c")
        self.lru_s = sem("lru_s")
        self.lru_a = sem("lru_a")
        self.lru_y = sem("lru_y")
        self.lru_yg = sem("lru_yg")
        self.gelu_z = sem("gelu_z")
        self.sig_z = sem("sig_z")
        self.wba_in = sem("wba_in")
        self.wbl_in = sem("wbl_in")
        self.wout_in = sem("wout_in")
        self.ba_mm = sem("ba_mm")
        self.ba_ev = sem("ba_ev")
        self.bl_mm = sem("bl_mm")
        self.bl_ev = sem("bl_ev")
        self.merged = sem("merged")
        self.wo_mm = sem("wo_mm")
        self.wo_ev = sem("wo_ev")
        self.res_in = sem("res_in")
        self.wr_in = sem("wr_in")
        self.lg_mm = sem("lg_mm")
        self.ht_mm = sem("ht_mm")
        self.ht_ev = sem("ht_ev")
        self.ht_out = sem("ht_out")
        self.rk_mm = sem("rk_mm")
        self.rt_exp = sem("rt_exp")
        self.oh_ready = sem("oh_ready")
        self.rt_ready = sem("rt_ready")
        self.tab_z = sem("tab_z")
        self.tab_put = sem("tab_put")
        self.tab_in = sem("tab_in")
        self.cnt_ready = sem("cnt_ready")
        self.xg_in = sem("xg_in")
        self.idx_ok = sem("idx_ok")
        self.brow_in = sem("brow_in")
        self.bc0 = sem("bc0")
        self.bc1 = sem("bc1")
        self.bcd = sem("bcd")
        self.g0_mm = sem("g0_mm")
        self.u0_mm = sem("u0_mm")
        self.g1_mm = sem("g1_mm")
        self.u1_mm = sem("u1_mm")
        self.d0_mm = sem("d0_mm")
        self.d1_mm = sem("d1_mm")
        self.w0 = sem("w0")
        self.w1 = sem("w1")
        self.w2 = sem("w2")
        self.w3 = sem("w3")
        self.w4 = sem("w4")
        self.w5 = sem("w5")
        self.t_mm = sem("t_mm")
        self.t_cp = sem("t_cp")
        self.gmin = sem("gmin")
        self.sig = sem("sig")
        self.h0_ok = sem("h0_ok")
        self.h1_ok = sem("h1_ok")
        self.ps0_rd = sem("ps0_rd")
        self.ps1_rd = sem("ps1_rd")
        self.y_ev = sem("y_ev")
        self.y_out = sem("y_out")
        self.yk0_in = sem("yk0_in")
        self.yk1_in = sem("yk1_in")
        self.yk2_in = sem("yk2_in")
        self.moe_ok = sem("moe_ok")
        self.mt_mm = sem("mt_mm")
        self.mt_ev = sem("mt_ev")
        self.wpg_in = sem("wpg_in")
        self.wpl_in = sem("wpl_in")
        self.pg_mm = sem("pg_mm")
        self.pg_ev = sem("pg_ev")
        self.pl_mm = sem("pl_mm")
        self.pl_ev = sem("pl_ev")
        self.y_ok = sem("y_ok")
        self.out_done = sem("out_done")
        self.kv_copy = sem("kv_copy")
        self.dve = sem("dve")
        self.act = sem("act")
        self.o_w = sem("o_w")
        self.o_idx = sem("o_idx")
        self.o_x = sem("o_x")
        self.o_b = sem("o_b")
        self.o_bc = sem("o_bc")
        self.o_st = sem("o_st")
        self.o_t = sem("o_t")
        self.o_tc = sem("o_tc")
        self.o_gu = sem("o_gu")
        self.o_g = sem("o_g")
        self.o_sig = sem("o_sig")
        self.o_h = sem("o_h")
        self.o_d = sem("o_d")
        self.o_y = sem("o_y")
        self.o_yk = sem("o_yk")
        self.o_add = sem("o_add")
        self.o_dve = sem("o_dve")



def build(nc, a):
    with ExitStack() as ctx:
        def sb(name, shape, dt=F32):
            return ctx.enter_context(nc.sbuf_tensor(name, shape, dt))

        S = Signals(lambda name: ctx.enter_context(nc.semaphore(name)))
        PS = ctx.enter_context(nc.psum_tensor("PS", [P, 8, CH], F32))

        ring = sb("ring", [P, 6, 4096])
        Zb = sb("Zb", [P, NZ * T])
        Z = Zb[:, :].rearrange("p (n t) -> p n t", t=T)
        cst = sb("cst", [P, NCST])
        feat = sb("feat", [P, KT, NFEAT])
        gqk = sb("gqk", [P, 2])
        hT = sb("hT", [P, KT, T])
        xc = sb("xc", [P, KT, T])
        lt = sb("lt", [P, KT, T])
        attT = sb("attT", [P, HPG, T])
        rope = attT[0:32, 0:2, :]
        rstd = sb("rstd", [P, T])
        sm = sb("sm", [P, 64])
        nsp = sb("nsp", [P, 6, KT])
        sct = sb("sct", [P, 96])
        prod = sb("prod", [P, 96])
        srow = sb("srow", [32, 324])
        sdiag = sb("sdiag", [32, 3, 32])
        sptt = sb("sptt", [P, 96])
        brt = sb("brt", [1, E])
        W2 = ring[:, 4:6, :].rearrange("p a n -> p (a n)")
        sq_qk = W2[:, 0:24 * T]
        rot = W2[0:32, 0:24 * T].rearrange("p (n t) -> p n t", t=T)
        vtok = W2[:, 0:3072].rearrange("p (b n) -> p b n", b=2)
        sS = W2[:, 3072:4608].rearrange("p (b n) -> p b n", b=2)
        sPT = W2[:, 4608:6144].rearrange("p (b n) -> p b n", b=2)
        stage = W2[:, 6144:7680]
        wrg = ring[:, 1, :].rearrange("p (a n c d) -> p a n c d", a=2, n=4, c=2)
        kts = [ring[:, 2, :].rearrange("p (s k) -> p s k", s=32), ring[:, 3, :].rearrange("p (s k) -> p s k", s=32),
               ring[:, 0, 0:2048].rearrange("p (s k) -> p s k", s=32)]
        vts = [ring[:, s, :].rearrange("p (b n) -> p b n", b=NS) for s in (1, 2, 3)]
        wba = ring[:, 0, :].rearrange("p (k n) -> p k n", k=4)
        wbl = [ring[:, s, :].rearrange("p (k n) -> p k n", k=4) for s in (1, 2)]
        wout = [ring[:, s, :].rearrange("p (k n) -> p k n", k=4) for s in (3, 0)]
        pos = [0]

        def zb(shape, dt=None):
            n = 1
            for s in shape[1:]:
                n *= s
            v = Zb[0:shape[0], pos[0]:pos[0] + n]
            pos[0] += n
            if dt is not None:
                v = v.bitcast(dt)
            return v if len(shape) == 2 else v.rearrange("p (a n) -> p a n", a=shape[1])

        xg = zb([P, D])
        xgT = [zb([P, KT, P]) for _ in range(2)]
        hm = zb([P, D])
        hmT = zb([P, KT, P])
        sg, ss_, su = zb([P, CH]), zb([P, CH]), zb([P, CH])
        yb = zb([P, D])
        brow = zb([1, 3 * D])
        bg0, bg1, bd = zb([P, 2, CH]), zb([P, 2, CH]), zb([P, D])
        logit = zb([P, 3, E])
        oh = [zb([P, 3, E]) for _ in range(TOPK)]
        route = zb([P, 3, E])
        rtmp, rtab, rrow = zb([P, 3, E]), zb([P, 3, E]), zb([P, 3, E])
        mx, mxi, mif = zb([P, 3, 8]), zb([P, 3, 8], U32), zb([P, 3, 8])
        ge, gs = zb([P, 3, TOPK]), zb([P, 3])
        drow, dtab = zb([P, 3, TOPK]), zb([P, 3, TOPK])
        irow, itab = zb([P, 3 * TOPK], I32), zb([P, 3 * TOPK], I32)
        over, drow2, ge2 = zb([P, 3, TOPK]), zb([P, 3, TOPK]), zb([P, 3, TOPK])
        irow2 = zb([P, 3 * TOPK], I32)
        cmax, most = zb([1, 1]), zb([1, 1], I32)
        tokid = zb([P, 3], I32)
        tab = zb([P, NCHUNK * E], I32)
        idxc = zb([P, 1], I32)
        carried = zb([1, 64])

        assert pos[0] <= NZ * T, pos[0]
        hstage = xg
        wr = hm[:, 0:KT * E].rearrange("p (k n) -> p k n", k=KT)
        yk = ring[:, 0:3, :].rearrange("p a n -> p (a n)").rearrange("p (k n) -> p k n", k=12)
        acc = ring[:, 3, 0:3072].rearrange("p (b n) -> p b n", b=3)
        wpg = [ring[:, s, :].rearrange("p (k n) -> p k n", k=4) for s in (4, 5)]
        wpl = Zb[:, 0:2048].rearrange("p (k n) -> p k n", k=2)
        pT = Zb[:, 2048:2048 + 2 * T].rearrange("p (k t) -> p k t", k=2)
        sgp = Zb[:, 4096:4096 + KT * T].rearrange("p (k t) -> p k t", k=KT)

        NOVER = (NCHUNK - 1) * E

        def overflow(eng):
            return eng.If(eng.value_load(most, min_val=0, max_val=T) > CAP)

        ident = cst[:, C_ID:C_ID + P]
        ones = cst[:, C_ONE:C_ONE + P]
        tri = cst[:, C_TRI:C_TRI + P]
        eps = cst[:, C_EPS:C_EPS + 1]

        def fv(c):
            return feat[:, :, c:c + 1].to_broadcast([P, KT, T])

        def over_tiles(v, n=KT):
            return v.unsqueeze(1).to_broadcast([v.shape[0], n, v.shape[-1]])

        hrow = nc.dram_tensor("hrow", (T, D), F32).ap()
        tabd = nc.dram_tensor("tabd", (P, NCHUNK * E), I32).ap()
        yrow2 = nc.dram_tensor("yrow2", ((NCHUNK - 1) * E * CAP, D), F32).ap()
        yrow = nc.dram_tensor("yrow", (E * CAP, D), F32).ap()
        block = ctx.enter_context(nc.Block())

        @block.sync
        def _(sp):
            xT0 = Z[:, ZGL:ZGL + KT, :]
            sp.dma_start(cst[:, :], a["cst"]).then_inc(S.cst_in, 16)
            sp.dma_start(xT0, a["xT"]).then_inc(S.x_in, 16)
            sp.dma_start(feat[:, :, :], a["feat"]).then_inc(S.x_in, 16)

            def win(piece, slot):
                return sp.dma_start(ring[:, slot, :], a["win"][piece].rearrange("p k n -> p (k n)"))

            wins = (S.win0, S.win1, S.win2, S.win3)
            for s in range(4):
                win(s, s).then_inc(wins[s], 16)
            sp.dma_start(rope, a["rope"]).then_inc(S.rope_in, 16)
            sp.dma_start(gqk[:, :], a["gqk"]).then_inc(S.rope_in, 16)
            with sp.Fori(1, 4) as i:
                for s in range(4):
                    sp.wait_ge(S.z_done, 16 * i + 4 * s - 12)
                    win(4 * i + s, s).then_inc(wins[s], 16)
            sp.wait_ge(S.z_done, 4 * 13)
            win(16, 0).then_inc(S.win0, 16)
            sp.wait_ge(S.z_done, 4 * 14)
            sp.dma_start(ring[:, 1, :], a["wrg"]).then_inc(S.wrg_in, 16)
            sp.wait_ge(S.z_done, 4 * 15)
            sp.dma_start(kts[0], a["kt0"]).then_inc(S.kt0_in, 16)
            sp.wait_ge(S.z_done, 4 * 16)
            sp.dma_start(kts[1], a["kt1"]).then_inc(S.kt1_in, 16)
            sp.wait_ge(S.z_done, NZ)
            sp.dma_start(kts[2], a["kt2"]).then_inc(S.kt2_in, 16)
            sp.wait_ge(S.gate_mm, 16)
            sp.dma_start(brt[:, :], a["b_router"]).then_inc(S.wr_in, 16)

            def cached_v(g, sem):
                n = SKEYS[g]
                src = a[f"cache{g}"].rearrange("b (k r) n -> k b r n", r=DIL[g])[:, :, 0, CH:2 * CH]
                sp.dma_start(vts[g][0:n, :, :], src).then_inc(sem, 16)

            cached_v(0, S.v_in)
            sp.wait_ge(S.ss_mm, 1)
            cached_v(1, S.v_in)
            cached_v(2, S.v_in)

            def half(w, k0, view, sem):
                sp.dma_start(view, w[k0 * P:(k0 + 4) * P, :].rearrange("(k p) n -> p k n", p=P)).then_inc(sem, 16)

            half(a["w_br_att"], 0, wba, S.wba_in)
            sp.wait_ge(S.spv_mm, 1)
            half(a["w_br_lru"], 0, wbl[0], S.wbl_in)
            half(a["w_br_lru"], 4, wbl[1], S.wbl_in)
            half(a["w_out"], 0, wout[0], S.wout_in)
            sp.wait_ge(S.ba_mm, KT)
            half(a["w_out"], 4, wout[1], S.wout_in)

            def gu(e, c, h):
                return a["w_gu"][e].rearrange("(k p) n -> p k n", p=P)[:, :, c * D + h * CH:c * D + h * CH + CH]

            def dn(e, h):
                return a["w_down"][e][h * CH:(h + 1) * CH, :].rearrange("(k p) n -> p k n", p=P)

            def r8(s):
                return ring[:, s, :].rearrange("p (k n) -> p k n", k=8)

            def r4(s):
                return ring[:, s, :].rearrange("p (k n) -> p k n", k=4)

            full = (S.w0, S.w1, S.w2, S.w3, S.w4, S.w5)
            used = (S.g0_mm, S.u0_mm, S.g1_mm, S.u1_mm, S.d0_mm, S.d1_mm)
            sp.wait_ge(S.at_pv, 8)
            sp.wait_ge(S.tk_out, TK_OUT[4])
            sp.wait_ge(S.vt_out, VT_OUT)
            sp.dma_start(wr[:, :, :], a["w_router"].rearrange("(k p) n -> p k n", p=P)).then_inc(S.wr_in, 16)
            sp.dma_start(r4(4), dn(0, 0)).then_inc(S.w4, 16)
            sp.dma_start(r4(5), dn(0, 1)).then_inc(S.w5, 16)
            sp.wait_ge(S.bl_mm, KT)
            sp.dma_start(r8(1), gu(0, 1, 0)).then_inc(S.w1, 16)
            sp.dma_start(r8(2), gu(0, 0, 1)).then_inc(S.w2, 16)
            sp.wait_ge(S.wo_mm, KT)
            sp.dma_start(r8(0), gu(0, 0, 0)).then_inc(S.w0, 16)
            sp.dma_start(r8(3), gu(0, 1, 1)).then_inc(S.w3, 16)
            with sp.Fori(1, E) as e:
                for s in range(6):
                    sp.wait_ge(used[s], e)
                    if s < 4:
                        sp.dma_start(r8(s), gu(e, s % 2, s // 2)).then_inc(full[s], 16)
                    else:
                        sp.dma_start(r4(s), dn(e, s - 4)).then_inc(full[s], 16)
            sp.wait_ge(S.cnt_ready, 1)
            with overflow(sp):
                for s in range(6):
                    sp.wait_ge(used[s], E)
                for c in range(NCHUNK - 1):
                    with sp.Fori(0, E) as e:
                        sp.wait_ge(S.o_y, e + c * E + 1)
                        for s in range(4):
                            sp.dma_start(r8(s), gu(e, s % 2, s // 2)).then_inc(S.o_w, 16)
                        for s in range(2):
                            sp.dma_start(r4(4 + s), dn(e, s)).then_inc(S.o_w, 16)
                sp.wait_ge(S.o_y, NOVER + 1)
            sp.wait_ge(S.d0_mm, E)
            half(a["w_ple_gate"], 0, wpg[0], S.wpg_in)
            sp.wait_ge(S.d1_mm, E)
            half(a["w_ple_gate"], 4, wpg[1], S.wpg_in)
            sp.wait_ge(S.t_mm, 5 + 4 * (E - 2) + 3)
            sp.dma_start(wpl, a["w_ple"].rearrange("(k p) n -> p k n", p=P)).then_inc(S.wpl_in, 16)
            sp.dma_start(pT, a["pT"]).then_inc(S.wpl_in, 16)
            sp.wait_ge(S.y_ok, 1)
            sp.dma_start(a["yT"], sgp).then_inc(S.out_done, 16)
            sp.wait_ge(S.out_done, 16)
            sp.wait_ge(S.kv_copy, 16 * (NS + 1) * NG)
            sp.wait_ge(S.conv_out, 48)
            sp.wait_ge(S.h_out, 32)

        @block.tensor
        def _(pe):
            mm = nc.tensor.matmul

            def sum_sq(src, nth):
                pe.wait_ge(S.sq_ok, nth)
                for k in range(KT):
                    last = mm(PS[:, 4, 0:T], ones, src[:, k, :], start=(k == 0), stop=(k == KT - 1))
                last.then_inc(S.ss_sum, 1)

            pe.wait_ge(S.cst_in, 16)
            sum_sq(hT, 1)
            pe.wait_ge(S.h_ok, 1)
            wins = (S.win0, S.win1, S.win2, S.win3)

            def z_piece(piece, slot, fill, first=False):
                w = ring[:, slot, :].rearrange("p (k n) -> p k n", k=KT)
                pe.wait_ge(wins[slot], fill)
                for t in range(4):
                    if not first:
                        pe.wait_ge(S.z_evac, 4 * piece + t - 3)
                    for k in range(KT):
                        last = mm(PS[:, t, 0:T], w[:, k, t * P:(t + 1) * P], hT[:, k, :],
                                  start=(k == 0), stop=(k == KT - 1))
                    last.then_inc(S.z_done, 1)

            for s in range(4):
                z_piece(s, s, 16, first=(s == 0))
            for s in range(4):
                z_piece(4 + s, s, 32)
            pe.wait_ge(S.sq_qk, 1)
            for c in range(13):
                n = min(CH, 24 * T - c * CH)
                if c >= 4:
                    pe.wait_ge(S.qkn_ev, c - 3)
                mm(PS[:, 4 + c % 4, 0:n], ones, sq_qk[:, c * CH:c * CH + n], start=True, stop=True).then_inc(S.qkn_mm, 1)
            with pe.Fori(2, 4) as i:
                for s in range(4):
                    z_piece(4 * i + s, s, 16 * i + 16)
            z_piece(16, 0, 16 * 5)

            pe.wait_ge(S.wrg_in, 16)
            pe.wait_ge(S.conv_done, 1)
            for j in range(KT):
                for m in range(2):
                    n = 2 * j + m
                    pe.wait_ge(S.z_evac, NZ)
                    if n >= 8:
                        pe.wait_ge(S.gate_ev, n - 7)
                    for c in range(2):
                        last = mm(PS[:, n % 8, 0:T], wrg[:, m, j // 2, c, (j % 2) * P:(j % 2 + 1) * P],
                                  xc[:, 2 * (j // 2) + c, :], start=(c == 0), stop=(c == 1))
                    last.then_inc(S.gate_mm, 1)

            pe.wait_ge(S.roped, 1)
            pe.wait_ge(S.gate_ev, 16)
            for g, sem in enumerate((S.kt0_in, S.kt1_in, S.kt2_in)):
                pe.wait_ge(sem, 16)
                for b in range(NS):
                    for h in range(HPG):
                        c = b * HPG + h
                        last = mm(PS[0:SKEYS[g], 4, g * 32 + c:g * 32 + c + 1], kts[g][:, c, :],
                                  Z[:, ZQ + g * HPG + h, NP + b:NP + b + 1], start=True, stop=True)
            last.then_inc(S.ss_mm, 1)

            n = 0
            for z0 in (ZK, ZV):
                for b, (t0, nt) in enumerate(BLK):
                    for g in range(NG):
                        if n >= 4:
                            pe.wait_ge(S.tk_ev, n - 3)
                        for h in range(HPG):
                            last = nc.tensor.transpose(PS[0:nt, n % 4, h * P:(h + 1) * P],
                                                       Z[:, z0 + g * HPG + h, t0:t0 + nt], ident)
                        last.then_inc(S.tk_mm, 1)
                        n += 1

            pe.wait_ge(S.ss_ev, 1)
            off = 0
            for g in range(NG):
                n = SKEYS[g]
                nc.tensor.transpose(PS[0:32, 5, off:off + n], sct[0:n, g * 32:(g + 1) * 32], ident[0:n, 0:n])
                off += n
            pe.wait_ge(S.ss_prod, 1)
            for g in range(NG):
                last = mm(PS[0:32, 5, off + g:off + g + 1], prod[:, g * 32:(g + 1) * 32], ones[:, 0:1],
                          start=True, stop=True)
            last.then_inc(S.ss_rows, 1)

            def scores(it):
                h, qb = it // 2, it % 2
                n = P * (qb + 1)
                if it == 0:
                    pe.wait_ge(S.tk_ev, 18)
                if it >= 2:
                    pe.wait_ge(S.at_s, it - 1)
                ps = PS[:, 2 * (it % 2):2 * (it % 2) + 2, :].rearrange("p a n -> p (a n)")
                for g in range(NG):
                    last = mm(ps[:, g * n:(g + 1) * n], Z[:, ZQ + g * HPG + h, qb * P:(qb + 1) * P],
                              Z[:, ZK + g * HPG + h, 0:n], start=True, stop=True)
                last.then_inc(S.at_sc, 1)

            def weigh(it):
                h, qb = it // 2, it % 2
                blocks = [(g, kb) for g in range(NG) for kb in range(qb + 1)]
                pe.wait_ge(S.at_p, it + 1)
                if it >= 1:
                    pe.wait_ge(S.at_pt, it)
                else:
                    pe.wait_ge(S.sb_ev, 1)
                ps = PS[:, 4:6, :].rearrange("p a n -> p (a n)")
                for j in range(len(blocks)):
                    last = nc.tensor.transpose(ps[:, j * P:(j + 1) * P], sS[:, it % 2, j * P:(j + 1) * P], ident)
                last.then_inc(S.at_t, 1)
                pe.wait_ge(S.at_pt, it + 1)
                if it >= 2:
                    pe.wait_ge(S.at_ev, it - 1)
                for j, (g, kb) in enumerate(blocks):
                    last = mm(PS[:, 6 + it % 2, 0:P], vtok[:, kb, (g * HPG + h) * P:(g * HPG + h + 1) * P],
                              sPT[:, it % 2, j * P:(j + 1) * P], start=(j == 0), stop=(j == len(blocks) - 1))
                last.then_inc(S.at_pv, 1)

            scores(0)
            scores(1)
            pe.wait_ge(S.sp_ready, 1)
            off = 0
            for g in range(NG):
                n = SKEYS[g]
                last = nc.tensor.transpose(PS[0:n, 6, g * 32:(g + 1) * 32], srow[:, off:off + n], ident[0:32, 0:32])
                off += n
            last.then_inc(S.st_mm, 1)
            pe.wait_ge(S.sd_ready, 1)
            for g in range(NG):
                last = mm(PS[:, 7, g * 32:(g + 1) * 32], ones[0:32, :], sdiag[:, g, :], start=True, stop=True)
            last.then_inc(S.sb_mm, 1)
            for it in range(8):
                weigh(it)
                if it + 2 < 8:
                    scores(it + 2)
            pe.wait_ge(S.st_ev, 1)
            pe.wait_ge(S.at_s, 8)
            pe.wait_ge(S.v_in, 48)
            for b in range(NS):
                for h in range(HPG):
                    c = b * HPG + h
                    for g in range(NG):
                        n = SKEYS[g]
                        last = mm(PS[:, 0, c:c + 1], vts[g][0:n, b, h * P:(h + 1) * P],
                                  sptt[0:n, g * 32 + c:g * 32 + c + 1], start=(g == 0), stop=(g == NG - 1))
            last.then_inc(S.spv_mm, 1)

            def dense(weights, arrived, src, nk, done, evac, base=1):
                for m in range(KT):
                    if m >= 4:
                        pe.wait_ge(evac, m - 3)
                    for k in range(nk):
                        if m == 0 and k in arrived:
                            pe.wait_ge(*arrived[k])
                        last = mm(PS[:, 4 * base + m % 4, 0:T], weights(k)[:, m * P:(m + 1) * P], src[:, k, :],
                                  start=(k == 0), stop=(k == nk - 1))
                    last.then_inc(done, 1)

            pe.wait_ge(S.satt, 1)
            pe.wait_ge(S.at_ev, 8)
            dense(lambda k: wba[:, k, :], {0: (S.wba_in, 16)}, attT, 4, S.ba_mm, S.ba_ev)
            pe.wait_ge(S.lru_yg, 1)
            dense(lambda k: wbl[k // 4][:, k % 4, :], {0: (S.wbl_in, 32)}, Z[:, ZGR:ZGR + KT, :], 8, S.bl_mm, S.bl_ev, 0)
            pe.wait_ge(S.ba_ev, KT)
            pe.wait_ge(S.merged, 1)
            dense(lambda k: wout[k // 4][:, k % 4, :], {0: (S.wout_in, 32)}, hT, 8, S.wo_mm, S.wo_ev)
            pe.wait_ge(S.wo_ev, KT)

            sum_sq(lt, 2)
            pe.wait_ge(S.h_ok, 2)
            pe.wait_ge(S.wr_in, 32)
            for b, (t0, nt) in enumerate(BLK):
                o = PS[0:nt, 0, b * E:(b + 1) * E]
                mm(o, ones[0:1, 0:nt], brt[:, :], start=True, stop=False)
                for k in range(KT):
                    last = mm(o, hT[:, k, t0:t0 + nt], wr[:, k, :], start=False, stop=(k == KT - 1))
            last.then_inc(S.lg_mm, 1)
            for b, (t0, nt) in enumerate(BLK):
                if b:
                    pe.wait_ge(S.ht_ev, b)
                ps = PS[:, 6:8, :].rearrange("p a n -> p (a n)")
                for k in range(KT):
                    last = nc.tensor.transpose(ps[0:nt, k * P:(k + 1) * P], hT[:, k, t0:t0 + nt], ident)
                last.then_inc(S.ht_mm, 1)
            pe.wait_ge(S.oh_ready, 1)
            for b in range(3):
                o = PS[:, 1, b * E:(b + 1) * E]
                for c in range(b):
                    mm(o, ones, route[:, c, :], start=(c == 0), stop=False)
                mm(o, tri, route[:, b, :], start=(b == 0), stop=True)
            for c in range(3):
                last = mm(PS[:, 1, 3 * E:4 * E], ones, route[:, c, :], start=(c == 0), stop=(c == 2))
            last.then_inc(S.rk_mm, 1)

            turns = [0]

            def tr(n, src, dst_tiles):
                if n is not None:
                    pe.wait_ge(S.t_cp, n)
                bank = 6 + turns[0] % 2
                turns[0] += 1
                for j in range(4):
                    last = nc.tensor.transpose(PS[:, bank, j * P:(j + 1) * P], src[:, (dst_tiles + j) * P:(dst_tiles + j + 1) * P], ident)
                last.then_inc(S.t_mm, 1)
                return last

            def gu_part(e, par, slot, bank, arrive, done):
                w = ring[:, slot, :].rearrange("p (k n) -> p k n", k=KT)
                pe.wait_ge(arrive, 16 * (e + 1))
                for k in range(KT):
                    last = mm(PS[:, bank, :], xgT[par][:, k, :], w[:, k, :], start=(k == 0), stop=(k == KT - 1))
                last.then_inc(done, 1)

            def down(e):
                for half_, (arrive, done) in enumerate(((S.w4, S.d0_mm), (S.w5, S.d1_mm))):
                    w = ring[:, 4 + half_, :].rearrange("p (k n) -> p k n", k=4)
                    pe.wait_ge(arrive, 16 * (e + 1))
                    for k in range(4):
                        kk = 4 * half_ + k
                        for c in range(2):
                            last = mm(PS[:, 4 + c, :], hmT[:, kk, :], w[:, k, c * CH:(c + 1) * CH],
                                      start=(kk == 0), stop=(kk == KT - 1))
                    last.then_inc(done, 1)
                    if half_ == 0:
                        yield

            def finish(e, n, first):
                pe.wait_ge(S.h1_ok, e + 1)
                tr(n, hm, 4)
                if not first:
                    pe.wait_ge(S.y_ev, e)
                d = down(e)
                next(d)
                pe.wait_ge(S.t_cp, n + 2)
                for _ in d:
                    pass

            def body(e, par, base, first=False, last=False, second=False):
                if not first:
                    pe.wait_ge(S.ps0_rd, e)
                pe.wait_ge(S.t_cp, base - 1 if not first else 2)
                gu_part(e, par, 0, 0, S.w0, S.g0_mm)
                gu_part(e, par, 1, 1, S.w1, S.u0_mm)
                n = base
                if not first:
                    finish(e - 1, n - 1, second)
                    n = n + 1
                if not last:
                    pe.wait_ge(S.xg_in, 16 * (e + 2))
                    tr(n - 1, xg, 0)
                    tr(n, xg, 4)
                    n = n + 2
                if not first:
                    pe.wait_ge(S.ps1_rd, e)
                gu_part(e, par, 2, 2, S.w2, S.g1_mm)
                gu_part(e, par, 3, 3, S.w3, S.u1_mm)
                pe.wait_ge(S.h0_ok, e + 1)
                tr(n - 1, hm, 0)

            pe.wait_ge(S.ht_ev, 3)
            pe.wait_ge(S.cnt_ready, 1)
            pe.wait_ge(S.xg_in, 16)
            tr(None, xg, 0)
            tr(None, xg, 4)
            body(0, 0, 2, first=True)
            body(1, 1, 5, second=True)
            with pe.Fori(0, (E - 4) // 2) as i:
                for u in range(2):
                    body(2 * i + 2 + u, u, 8 * i + 9 + 4 * u)
            body(E - 2, 0, 5 + 4 * (E - 3))
            body(E - 1, 1, 5 + 4 * (E - 2), last=True)
            finish(E - 1, 5 + 4 * (E - 2) + 2 - 1, False)

            with overflow(pe):
                with pe.Fori(0, NOVER) as n:
                    pe.wait_ge(S.o_x, 16 * (n + 1))
                    for k in range(KT):
                        last = nc.tensor.transpose(PS[:, 6 + k // 4, (k % 4) * P:(k % 4 + 1) * P],
                                                   xg[:, k * P:(k + 1) * P], ident)
                    last.then_inc(S.o_t, 1)
                    pe.wait_ge(S.o_tc, 2 * n + 1)
                    pe.wait_ge(S.o_w, 96 * (n + 1))
                    for q in range(4):
                        w = ring[:, q, :].rearrange("p (k n) -> p k n", k=KT)
                        for k in range(KT):
                            last = mm(PS[:, q, :], xgT[0][:, k, :], w[:, k, :], start=(k == 0), stop=(k == KT - 1))
                    last.then_inc(S.o_gu, 1)
                    pe.wait_ge(S.o_h, 2 * n + 2)
                    for k in range(KT):
                        last = nc.tensor.transpose(PS[:, 6 + k // 4, (k % 4) * P:(k % 4 + 1) * P],
                                                   hm[:, k * P:(k + 1) * P], ident)
                    last.then_inc(S.o_t, 1)
                    pe.wait_ge(S.o_tc, 2 * n + 2)
                    for k in range(KT):
                        w = ring[:, 4 + k // 4, :].rearrange("p (k n) -> p k n", k=4)
                        for c in range(2):
                            last = mm(PS[:, 4 + c, :], hmT[:, k, :], w[:, k % 4, c * CH:(c + 1) * CH],
                                      start=(k == 0), stop=(k == KT - 1))
                    last.then_inc(S.o_d, 1)

            pe.wait_ge(S.moe_ok, 3)
            with overflow(pe):
                pe.wait_ge(S.o_add, 1)
            for b, (t0, nt) in enumerate(BLK):
                if b == 0:
                    pe.wait_ge(S.y_ev, E)
                    pe.wait_ge(S.t_cp, 5 + 4 * (E - 2) + 3)
                if b >= 2:
                    pe.wait_ge(S.mt_ev, b - 1)
                q = 4 * (b % 2)
                ps = PS[:, q:q + 2, :].rearrange("p a n -> p (a n)")
                for k in range(KT):
                    last = nc.tensor.transpose(ps[:, k * P:k * P + nt], acc[0:nt, b, k * P:(k + 1) * P], ident[0:nt, 0:nt])
                last.then_inc(S.mt_mm, 1)
            pe.wait_ge(S.mt_ev, 3)

            sum_sq(lt, 3)
            pe.wait_ge(S.h_ok, 3)
            dense(lambda k: wpg[k // 4][:, k % 4, :], {0: (S.wpg_in, 32)}, hT, 8, S.pg_mm, S.pg_ev, 0)
            dense(lambda k: wpl[:, k, :], {0: (S.wpl_in, 32)}, pT, 2, S.pl_mm, S.pl_ev)

        @block.scalar
        def _(act):
            A = nc.scalar.activation

            def root(nth, out, ps, scale):
                act.wait_ge(S.ss_sum, nth)
                return A(out, ps, ACT.Sqrt, bias=eps, scale=scale)

            act.wait_ge(S.cst_in, 16)
            root(1, rstd[:, :], PS[:, 4, 0:T], 1.0 / D).then_inc(S.rms_ok, 1)

            act.wait_ge(S.x_in, 32)
            A(nsp[:, 0, :], feat[:, :, FLAM], ACT.Abs).then_inc(S.act, 1)
            act.wait_ge(S.act, 1)
            A(nsp[:, 0, :], nsp[:, 0, :], ACT.Exp, scale=-1.0).then_inc(S.nsp, 1)
            act.wait_ge(S.nsp, 1)
            A(nsp[:, 1, :], nsp[:, 0, :], ACT.Ln, bias=ones[:, 0:1]).then_inc(S.nsp, 1)

            def evac(n, bank):
                act.wait_ge(S.z_done, n + 1)
                A(Z[:, n, :], PS[:, bank, 0:T], ACT.Copy).then_inc(S.z_evac, 1)

            with act.Fori(0, LOOP_A) as i:
                for t in range(4):
                    evac(4 * i + t, t)
            for c in range(13):
                n = min(CH, 24 * T - c * CH)
                act.wait_ge(S.qkn_mm, c + 1)
                A(sq_qk[:, c * CH:c * CH + n], PS[:, 4 + c % 4, 0:n], ACT.Sqrt, bias=eps, scale=1.0 / HD)\
                    .then_inc(S.qkn_ev, 1)
            act.wait_ge(S.h_ok, 1)
            with act.Fori(LOOP_A, NPIECE) as i:
                for t in range(4):
                    evac(4 * i + t, t)

            act.wait_ge(S.conv_out, 48)
            for n in range(16):
                j, m = n // 2, n % 2
                act.wait_ge(S.gate_mm, n + 1)
                dst = hT[:, j, :] if m == 0 else Z[:, ZX + j, :]
                c = FBA if m == 0 else FBX
                A(dst, PS[:, n % 8, 0:T], ACT.Sigmoid, bias=feat[:, j, c:c + 1]).then_inc(S.gate_ev, 1)
            act.wait_ge(S.ss_mm, 1)
            A(sct[:, 0:64], PS[:, 4, 0:64], ACT.Copy)
            A(sct[0:64, 64:96], PS[0:64, 4, 64:96], ACT.Copy).then_inc(S.ss_ev, 1)
            n = 0
            for kv in range(2):
                for b, (t0, nt) in enumerate(BLK):
                    direct = kv == 1 and b < 2
                    if not direct and (kv, b) != (0, 0):
                        act.wait_ge(S.tk_out, TK_OUT[b] if kv == 0 else TK_OUT[3])
                    for g in range(NG):
                        act.wait_ge(S.tk_mm, n + 1)
                        dst = vtok[:, b, g * CH:(g + 1) * CH] if direct else stage[0:nt, g * CH:(g + 1) * CH]
                        if n == 0:
                            act.wait_ge(S.roped, 1)
                        A(dst, PS[0:nt, n % 4, :], ACT.Copy).then_inc(S.tk_ev, 1)
                        n += 1
            act.wait_ge(S.z_evac, NZ)
            A(Z[:, ZGR:ZGR + KT, :], Z[:, ZGR:ZGR + KT, :], ACT.Gelu_apprx_tanh).then_inc(S.gelu_z, 1)
            A(Z[:, ZGL:ZGL + 16, :], Z[:, ZGL:ZGL + 16, :], ACT.Sigmoid).then_inc(S.sig_z, 1)
            act.wait_ge(S.sp_exp, 1)
            A(srow[:, 0:323], srow[:, 0:323], ACT.Exp, bias=sm[0:32, 1:2], scale=SCALE, accum_out=sm[0:32, 2:3])\
                .then_inc(S.sp_exp, 1)
            act.wait_ge(S.lru_l, 1)
            A(lt[:, :, :], hT[:, :, :], ACT.Exp, scale=2.0).then_inc(S.lru_e, 1)
            A(xc[:, :, :], hT[:, :, :], ACT.Tanh, scale=-1.0).then_inc(S.lru_th, 1)
            act.wait_ge(S.lru_th, 1)
            A(hT[:, :, :], hT[:, :, :], ACT.Exp).then_inc(S.lru_a, 1)
            act.wait_ge(S.lru_c, 1)
            A(xc[:, :, :], xc[:, :, :], ACT.Sqrt).then_inc(S.lru_s, 1)

            def prompt_exp(it):
                n = 3 * P * (it % 2 + 1)
                act.wait_ge(S.at_nm, it + 1)
                A(sS[:, it % 2, 0:n], sS[:, it % 2, 0:n], ACT.Exp, bias=sm[:, 8 + it:9 + it], scale=SCALE,
                  accum_out=sm[:, 16 + it:17 + it]).then_inc(S.at_e, 1)

            def prompt_out(it):
                n = 3 * P * (it % 2 + 1)
                act.wait_ge(S.at_t, it + 1)
                if it >= 2:
                    act.wait_ge(S.at_pv, it - 1)
                A(sPT[:, it % 2, 0:n], PS[:, 4:6, :].rearrange("p a n -> p (a n)")[:, 0:n], ACT.Copy).then_inc(S.at_pt, 1)

            def prompt_att(it):
                act.wait_ge(S.at_pv, it + 1)
                A(attT[:, it // 2, (it % 2) * P:(it % 2 + 1) * P], PS[:, 6 + it % 2, 0:P], ACT.Copy).then_inc(S.at_ev, 1)

            prompt_exp(0)
            act.wait_ge(S.st_mm, 1)
            A(sptt[:, 0:64], PS[:, 6, 0:64], ACT.Copy)
            A(sptt[0:64, 64:96], PS[0:64, 6, 64:96], ACT.Copy).then_inc(S.st_ev, 1)
            act.wait_ge(S.sb_mm, 1)
            A(prod[:, :], PS[:, 7, 0:96], ACT.Copy).then_inc(S.sb_ev, 1)
            for it in range(8):
                prompt_out(it)
                if it + 1 < 8:
                    prompt_exp(it + 1)
                prompt_att(it)

            root(2, rstd[:, :], PS[:, 4, 0:T], 1.0 / D).then_inc(S.rms_ok, 1)
            for b, (t0, nt) in enumerate(BLK):
                act.wait_ge(S.ht_mm, b + 1)
                if b:
                    act.wait_ge(S.ht_out, 16 * b)
                act.wait_ge(S.bl_ev, KT)
                A(hstage[0:nt, :], PS[:, 6:8, :].rearrange("p a n -> p (a n)")[0:nt, :], ACT.Copy).then_inc(S.ht_ev, 1)
            act.wait_ge(S.rt_exp, 1)
            A(ge[:, :, :], ge[:, :, :], ACT.Exp).then_inc(S.rt_exp, 1)

            bank = [0]

            def cp(n, dst):
                act.wait_ge(S.t_mm, n + 1)
                bb = 6 + bank[0] % 2
                bank[0] += 1
                A(dst, PS[:, bb, :].rearrange("p (k n) -> p k n", k=4), ACT.Copy).then_inc(S.t_cp, 1)

            def sigm(n):
                act.wait_ge(S.gmin, n + 1)
                A(ss_, sg, ACT.Sigmoid, scale=ALPHA).then_inc(S.sig, 1)

            def body(e, par, base, first=False, last=False):
                n = base
                if not first:
                    sigm(2 * e - 1)
                    cp(n, hmT[:, 4:8, :])
                    n = n + 1
                sigm(2 * e)
                if not last:
                    if not first:
                        act.wait_ge(S.u1_mm, e)
                    cp(n, xgT[1 - par][:, 0:4, :])
                    cp(n + 1, xgT[1 - par][:, 4:8, :])
                    n = n + 2
                if not first:
                    act.wait_ge(S.d0_mm, e)
                cp(n, hmT[:, 0:4, :])

            cp(0, xgT[0][:, 0:4, :])
            cp(1, xgT[0][:, 4:8, :])
            body(0, 0, 2, first=True)
            body(1, 1, 5)
            with act.Fori(0, (E - 4) // 2) as i:
                for u in range(2):
                    body(2 * i + 2 + u, u, 8 * i + 9 + 4 * u)
            body(E - 2, 0, 5 + 4 * (E - 3))
            body(E - 1, 1, 5 + 4 * (E - 2), last=True)
            sigm(2 * E - 1)
            cp(5 + 4 * (E - 2) + 2, hmT[:, 4:8, :])

            with overflow(act):
                with act.Fori(0, NOVER) as n:
                    def two_banks(dst, count):
                        act.wait_ge(S.o_t, count)
                        A(dst.rearrange("p k n -> p (k n)"), PS[:, 6:8, :].rearrange("p a n -> p (a n)"), ACT.Copy)\
                            .then_inc(S.o_tc, 1)

                    two_banks(xgT[0], 2 * n + 1)
                    for h in range(2):
                        act.wait_ge(S.o_g, 2 * n + h + 1)
                        A(ss_, sg, ACT.Sigmoid, scale=ALPHA).then_inc(S.o_sig, 1)
                    two_banks(hmT, 2 * n + 2)

            root(3, rstd[:, :], PS[:, 4, 0:T], 1.0 / D).then_inc(S.rms_ok, 1)
            for m in range(KT):
                act.wait_ge(S.pg_mm, m + 1)
                A(sgp[:, m, :], PS[:, m % 4, 0:T], ACT.Sigmoid).then_inc(S.pg_ev, 1)

        @block.vector
        def _(v):
            TT, TS, STT = nc.vector.tensor_tensor, nc.vector.tensor_scalar, nc.vector.scalar_tensor_tensor
            done = [0]

            def link(ins):
                ins.then_inc(S.dve, 1)
                done[0] = done[0] + 1
                v.wait_ge(S.dve, done[0])

            def normed(nth, x, gcol):
                v.wait_ge(S.rms_ok, nth)
                link(nc.vector.reciprocal(rstd[:, :], rstd[:, :]))
                link(TT(hT[:, :, :], x, fv(gcol), ALU.mult))
                TT(hT[:, :, :], hT[:, :, :], over_tiles(rstd[:, :]), ALU.mult).then_inc(S.h_ok, 1)

            x0 = Z[:, ZGL:ZGL + KT, :]
            v.wait_ge(S.x_in, 32)
            TT(hT[:, :, :], x0, x0, ALU.mult).then_inc(S.sq_ok, 1)
            v.wait_ge(S.ss_sum, 1)
            normed(1, x0, FGM)

            v.wait_ge(S.z_evac, 24)
            TT(sq_qk, Zb[:, 0:24 * T], Zb[:, 0:24 * T], ALU.mult).then_inc(S.sq_qk, 1)
            v.wait_ge(S.z_evac, ZX + KT)
            X = Z[:, ZX:ZX + KT, :]
            link(TT(xc[:, :, :], X, fv(FW + 3), ALU.mult))
            link(TT(xc[:, :, :], xc[:, :, :], fv(FCB), ALU.add))
            for back in (1, 2, 3):
                w = feat[:, :, FW + 3 - back:FW + 4 - back]
                n = NP - back
                link(TT(lt[:, :, 0:n], X[:, :, 0:n], w.to_broadcast([P, KT, n]), ALU.mult))
                link(TT(lt[:, :, NP:T], feat[:, :, FSC + (3 - back) * NS:FSC + (4 - back) * NS],
                        w.to_broadcast([P, KT, NS]), ALU.mult))
                link(TT(xc[:, :, back:NP], xc[:, :, back:NP], lt[:, :, 0:n], ALU.add))
                ins = TT(xc[:, :, NP:T], xc[:, :, NP:T], lt[:, :, NP:T], ALU.add)
                if back < 3:
                    link(ins)
            ins.then_inc(S.conv_done, 1)
            v.wait_ge(S.conv_done, 1)

            v.wait_ge(S.qkn_ev, 13)
            v.wait_ge(S.rope_in, 32)
            link(nc.vector.reciprocal(sq_qk, sq_qk))
            for m in range(2):
                zz = Zb[:, m * 12 * T:(m + 1) * 12 * T]
                ins = STT(zz, zz, gqk[:, m:m + 1], sq_qk[:, m * 12 * T:(m + 1) * 12 * T], ALU.mult, ALU.mult)
                if m == 0:
                    link(ins)
            ins.then_inc(S.qk_normed, 1)
            v.wait_ge(S.qk_normed, 1)
            v.wait_ge(S.rot_in, 32)
            zr = Z[0:32, 0:24, :]
            link(TT(rot, rot, over_tiles(rope[:, 1, :], 24), ALU.mult))
            link(TT(zr, zr, over_tiles(rope[:, 0, :], 24), ALU.mult))
            TT(zr, zr, rot, ALU.add).then_inc(S.roped, 1)
            v.wait_ge(S.roped, 1)
            TT(prod[:, :].rearrange("p (g b h) -> p g b h", g=NG, b=NS),
               Z[:, ZQ:ZQ + NHEAD, NP:T].rearrange("p (g h) b -> p g b h", g=NG),
               Z[:, ZK:ZK + NHEAD, NP:T].rearrange("p (g h) b -> p g b h", g=NG), ALU.mult).then_inc(S.ss_prod, 1)

            lam = feat[:, :, FLAM]
            v.wait_ge(S.nsp, 2)
            link(TS(nsp[:, 2, :], nsp[:, 0, :], 1.0, -1.0, ALU.add, ALU.add))
            link(TS(nsp[:, 3, :], nsp[:, 2, :], 1e-30, None, ALU.max))
            link(nc.vector.reciprocal(nsp[:, 3, :], nsp[:, 3, :]))
            link(TT(nsp[:, 1, :], nsp[:, 1, :], nsp[:, 3, :], ALU.mult))
            link(TS(nsp[:, 4, :], nsp[:, 2, :], 0.0, None, ALU.is_equal))
            link(TT(nsp[:, 1, :], nsp[:, 1, :], nsp[:, 4, :], ALU.add))
            link(TT(nsp[:, 1, :], nsp[:, 1, :], nsp[:, 0, :], ALU.mult))
            link(TS(nsp[:, 5, :], lam, -1.0, 0.0, ALU.mult, ALU.max))
            link(TT(nsp[:, 1, :], nsp[:, 1, :], nsp[:, 5, :], ALU.add))
            link(TS(nsp[:, 1, :], nsp[:, 1, :], -LRU_C, None, ALU.mult))
            v.wait_ge(S.gate_ev, 16)
            TT(hT[:, :, :], hT[:, :, :], nsp[:, 1, :].unsqueeze(2).to_broadcast([P, KT, T]), ALU.mult)\
                .then_inc(S.lru_l, 1)
            link(TT(X, X, xc[:, :, :], ALU.mult))

            v.wait_ge(S.ss_rows, 1)
            link(nc.vector.tensor_copy(srow[:, 0:323], PS[0:32, 5, 0:323]))
            link(nc.vector.tensor_reduce(sm[0:32, 0:1], srow[:, 0:323], AX, ALU.max))
            TS(sm[0:32, 1:2], sm[0:32, 0:1], -SCALE, None, ALU.mult).then_inc(S.sp_exp, 1)
            v.wait_ge(S.sp_exp, 2)
            link(nc.vector.reciprocal(sm[0:32, 3:4], sm[0:32, 2:3]))
            TS(srow[:, 0:323], srow[:, 0:323], sm[0:32, 3:4], None, ALU.mult).then_inc(S.sp_ready, 1)
            v.wait_ge(S.sp_ready, 1)
            for g in range(NG):
                ins = TS(sdiag[:, g, :], ident[0:32, 0:32], srow[:, 320 + g:321 + g], None, ALU.mult)
            ins.then_inc(S.sd_ready, 1)

            def mask_max(it):
                h, qb = it // 2, it % 2
                n = 3 * P * (qb + 1)
                m = cst[:, C_MASK1:C_MASK1 + n] if qb else cst[:, C_MASK0:C_MASK0 + n]
                v.wait_ge(S.at_sc, it + 1)
                if it >= 2:
                    v.wait_ge(S.at_t, it - 1)
                ps = PS[:, 2 * (it % 2):2 * (it % 2) + 2, :].rearrange("p a n -> p (a n)")[:, 0:n]
                TT(sS[:, it % 2, 0:n], ps, m, ALU.add).then_inc(S.at_s, 1)
                v.wait_ge(S.at_s, it + 1)
                link(nc.vector.tensor_reduce(sm[:, 24:25], sS[:, it % 2, 0:n], AX, ALU.max))
                TS(sm[:, 8 + it:9 + it], sm[:, 24:25], -SCALE, None, ALU.mult).then_inc(S.at_nm, 1)

            def divide(it):
                n = 3 * P * (it % 2 + 1)
                v.wait_ge(S.at_e, it + 1)
                link(nc.vector.reciprocal(sm[:, 25:26], sm[:, 16 + it:17 + it]))
                TS(sS[:, it % 2, 0:n], sS[:, it % 2, 0:n], sm[:, 25:26], None, ALU.mult).then_inc(S.at_p, 1)

            mask_max(0)
            v.wait_ge(S.lru_th, 1)
            v.wait_ge(S.lru_e, 1)
            STT(xc[:, :, :], lt[:, :, :], 1.0, xc[:, :, :], ALU.add, ALU.mult).then_inc(S.lru_c, 1)
            divide(0)
            mask_max(1)
            v.wait_ge(S.lru_s, 1)
            link(TT(X, X, xc[:, :, :], ALU.mult))
            v.wait_ge(S.lru_a, 1)
            for j in range(KT):
                nc.vector.tensor_tensor_scan(lt[:, j, 0:NP], hT[:, j, 0:NP], X[:, j, 0:NP], 0.0, ALU.mult, ALU.add)
            link(TT(lt[:, :, NP:T], hT[:, :, NP:T], feat[:, :, FSH:FSH + NS], ALU.mult))
            TT(lt[:, :, NP:T], lt[:, :, NP:T], X[:, :, NP:T], ALU.add).then_inc(S.lru_y, 1)
            v.wait_ge(S.gelu_z, 1)
            v.wait_ge(S.lru_y, 1)
            TT(Z[:, ZGR:ZGR + KT, :], Z[:, ZGR:ZGR + KT, :], lt[:, :, :], ALU.mult).then_inc(S.lru_yg, 1)
            for it in range(1, 8):
                divide(it)
                if it + 1 < 8:
                    mask_max(it + 1)
            v.wait_ge(S.sb_ev, 1)
            link(TT(prod[:, :].rearrange("p (g b h) -> p g b h", g=NG, b=NS),
                    prod[:, :].rearrange("p (g b h) -> p g b h", g=NG, b=NS),
                    Z[:, ZV:ZV + NHEAD, NP:T].rearrange("p (g h) b -> p g b h", g=NG), ALU.mult))
            link(TT(prod[:, 0:32], prod[:, 0:32], prod[:, 32:64], ALU.add))
            link(TT(prod[:, 0:32], prod[:, 0:32], prod[:, 64:96], ALU.add))
            v.wait_ge(S.spv_mm, 1)
            TT(attT[:, :, NP:T], PS[:, 0, 0:32].rearrange("p (b h) -> p h b", b=NS),
               prod[:, 0:32].rearrange("p (b h) -> p h b", b=NS), ALU.add).then_inc(S.satt, 1)

            v.wait_ge(S.sig_z, 1)
            for m in range(KT):
                v.wait_ge(S.ba_mm, m + 1)
                TT(Z[:, ZGA + m, :], Z[:, ZGA + m, :], PS[:, 4 + m % 4, 0:T], ALU.mult).then_inc(S.ba_ev, 1)
            for m in range(KT):
                v.wait_ge(S.bl_mm, m + 1)
                TT(Z[:, ZGL + m, :], Z[:, ZGL + m, :], PS[:, m % 4, 0:T], ALU.mult).then_inc(S.bl_ev, 1)
            v.wait_ge(S.bl_ev, KT)
            v.wait_ge(S.ba_ev, KT)
            TT(hT[:, :, :], Z[:, ZGL:ZGL + KT, :], Z[:, ZGA:ZGA + KT, :], ALU.add).then_inc(S.merged, 1)
            v.wait_ge(S.res_in, 16)
            for m in range(KT):
                v.wait_ge(S.wo_mm, m + 1)
                TT(xc[:, m, :], xc[:, m, :], PS[:, 4 + m % 4, 0:T], ALU.add).then_inc(S.wo_ev, 1)
            v.wait_ge(S.wo_ev, KT)
            v.wait_ge(S.h_out, 32)
            TT(lt[:, :, :], xc[:, :, :], xc[:, :, :], ALU.mult).then_inc(S.sq_ok, 1)
            v.wait_ge(S.wo_mm, KT)
            normed(2, xc[:, :, :], FGF)

            link(nc.vector.memset(logit[:, 2, :], 0.0))
            v.wait_ge(S.lg_mm, 1)
            link(nc.vector.tensor_copy(logit[:, 0:2, :].rearrange("p a n -> p (a n)"), PS[:, 0, 0:2 * E]))
            link(nc.vector.tensor_copy(logit[0:NS, 2, :], PS[0:NS, 0, 2 * E:3 * E]))
            for b in range(3):
                link(nc.vector.max(mx[:, b, :], logit[:, b, :]))
                link(nc.vector.max_index(mxi[:, b, :], mx[:, b, :], logit[:, b, :]))
            link(nc.vector.tensor_copy(mif[:, :, :], mxi[:, :, :]))
            TT(ge[:, :, :], mx[:, :, 0:TOPK], mx[:, :, 0:1].to_broadcast([P, 3, TOPK]), ALU.subtract).then_inc(S.rt_exp, 1)
            iota = cst[:, C_IOTA:C_IOTA + E].unsqueeze(1).to_broadcast([P, 3, E])
            valid = cst[:, C_VALID:C_VALID + 3].unsqueeze(2).to_broadcast([P, 3, E])
            for k in range(TOPK):
                link(TT(oh[k], iota, mif[:, :, k:k + 1].to_broadcast([P, 3, E]), ALU.is_equal))
                link(TT(oh[k], oh[k], valid, ALU.mult))
            link(TT(route, oh[0], oh[1], ALU.add))
            link(TT(rtmp, oh[2], oh[3], ALU.add))
            TT(route, route, rtmp, ALU.add).then_inc(S.oh_ready, 1)
            v.wait_ge(S.rk_mm, 1)
            link(nc.vector.tensor_reduce(cmax, PS[0:1, 1, 3 * E:4 * E], AX, ALU.max))
            link(nc.vector.tensor_copy(most, cmax))
            rank = PS[:, 1, 0:3 * E].rearrange("p (b e) -> p b e", b=3)
            link(TS(rtmp, rank, float(CAP), None, ALU.is_ge))
            link(TS(rtab, rank, float(2 * CAP), None, ALU.is_ge))
            link(TT(rtmp, rtmp, rtab, ALU.add))
            link(STT(rrow, rtmp, float(E * CAP - CAP), rank, ALU.mult, ALU.add))
            link(STT(rtab, rtmp, -float(CAP), rank, ALU.mult, ALU.add))
            link(TS(rtab, rtab, float(NCHUNK * E), None, ALU.mult))
            link(STT(rtab, rtmp, float(E), rtab, ALU.mult, ALU.add))
            link(TT(rrow, rrow, cst[:, C_EOFF:C_EOFF + E].unsqueeze(1).to_broadcast([P, 3, E]), ALU.add))
            link(TT(rtab, rtab, iota, ALU.add))
            for src, dst in ((rrow, drow), (rtab, dtab)):
                for k in range(TOPK):
                    link(TT(rtmp, src, oh[k], ALU.mult))
                    link(nc.vector.tensor_reduce(dst[:, :, k], rtmp, AX, ALU.add))
            link(TS(over, drow, float(E * CAP), None, ALU.is_ge))
            link(STT(drow, over, -float(E * CAP), drow, ALU.mult, ALU.add))
            link(TT(drow2, drow, over, ALU.mult))
            link(TT(drow, drow, drow2, ALU.subtract))
            link(nc.vector.tensor_copy(irow, drow.rearrange("p a n -> p (a n)")))
            link(nc.vector.tensor_copy(irow2, drow2.rearrange("p a n -> p (a n)")))
            link(nc.vector.tensor_copy(itab, dtab.rearrange("p a n -> p (a n)")))
            nc.vector.tensor_copy(tokid, cst[:, C_TOK:C_TOK + 3]).then_inc(S.rt_ready, 1)
            v.wait_ge(S.rt_exp, 2)
            link(nc.vector.tensor_reduce(gs, ge, AX, ALU.add))
            link(nc.vector.reciprocal(gs, gs))
            link(TT(ge, ge, gs.unsqueeze(2).to_broadcast([P, 3, TOPK]), ALU.mult))
            link(TT(ge2, ge, over, ALU.mult))
            TT(ge, ge, ge2, ALU.subtract).then_inc(S.cnt_ready, 1)

            def half_act(e, n, gb, ub, bias, bias_at, bias_n, bank, hcol, rd, hok, hfree, before):
                if before is not None:
                    v.wait_ge(*before)
                v.wait_ge(bias_at, bias_n)
                v.wait_ge(gb, e + 1)
                link(TT(sg, PS[:, bank, :], bias[:, 0, :], ALU.add))
                TS(sg, sg, LIMIT, None, ALU.min).then_inc(S.gmin, 1)
                v.wait_ge(ub, e + 1)
                TT(su, PS[:, bank + 1, :], bias[:, 1, :], ALU.add).then_inc(rd, 1)
                v.wait_ge(rd, e + 1)
                link(TS(su, su, LIMIT, -LIMIT, ALU.min, ALU.max))
                v.wait_ge(S.sig, n + 1)
                link(TT(sg, sg, ss_, ALU.mult))
                if hfree is not None:
                    v.wait_ge(*hfree)
                STT(hm[:, hcol:hcol + CH], su, 1.0, sg, ALU.add, ALU.mult).then_inc(hok, 1)

            def act0(e, base, first=False):
                half_act(e, 2 * e, S.g0_mm, S.u0_mm, bg0, S.bc0, e + 1, 0, 0, S.ps0_rd, S.h0_ok,
                         None if first else (S.t_mm, base), None if first else (S.h1_ok, e))

            def act1(e, base, first=False):
                half_act(e, 2 * e + 1, S.g1_mm, S.u1_mm, bg1, S.bc1, e + 1, 2, CH, S.ps1_rd, S.h1_ok,
                         None if first else (S.t_mm, base + 1), (S.h0_ok, e + 1))

            def y_out(e, first=False):
                v.wait_ge(S.d1_mm, e + 1)
                v.wait_ge(S.bcd, e + 1)
                if not first:
                    v.wait_ge(S.y_out, 16 * e)
                TT(yb, PS[:, 4:6, :].rearrange("p a n -> p (a n)"), bd, ALU.add).then_inc(S.y_ev, 1)

            per = 2 * 3

            act0(0, 2, first=True)
            act1(0, 2, first=True)
            act0(1, 5)
            y_out(0, first=True)
            act1(1, 5)
            act0(2, 9)
            y_out(1)
            start = done[0]
            with v.Fori(0, E - 4) as i:
                done[0] = start + i * per
                act1(i + 2, 4 * i + 9)
                act0(i + 3, 4 * i + 13)
                y_out(i + 2)
            done[0] = start + (E - 4) * per
            act1(E - 2, 5 + 4 * (E - 3))
            act0(E - 1, 5 + 4 * (E - 2))
            y_out(E - 2)
            act1(E - 1, 5 + 4 * (E - 2))
            y_out(E - 1)

            with overflow(v):
                v.wait_ge(S.y_ev, E)
                v.wait_ge(S.h1_ok, E)
                TS(sm[:, 26:27], ones[:, 0:1], 0.0, None, ALU.mult).then_inc(S.o_y, 1)
                with v.Fori(0, NOVER) as n:
                    olinks = [0]

                    def olink(ins):
                        ins.then_inc(S.o_dve, 1)
                        olinks[0] += 1
                        v.wait_ge(S.o_dve, 8 * n + olinks[0])

                    v.wait_ge(S.o_bc, 3 * (n + 1))
                    v.wait_ge(S.o_gu, n + 1)
                    for h, bias in enumerate((bg0, bg1)):
                        olink(TT(sg, PS[:, 2 * h, :], bias[:, 0, :], ALU.add))
                        TS(sg, sg, LIMIT, None, ALU.min).then_inc(S.o_g, 1)
                        olink(TT(su, PS[:, 2 * h + 1, :], bias[:, 1, :], ALU.add))
                        olink(TS(su, su, LIMIT, -LIMIT, ALU.min, ALU.max))
                        v.wait_ge(S.o_sig, 2 * n + h + 1)
                        olink(TT(sg, sg, ss_, ALU.mult))
                        ins = STT(hm[:, h * CH:(h + 1) * CH], su, 1.0, sg, ALU.add, ALU.mult)
                        ins.then_inc(S.o_h, 1)
                        v.wait_ge(S.o_h, 2 * n + h + 1)
                    v.wait_ge(S.o_d, n + 1)
                    TT(yb, PS[:, 4:6, :].rearrange("p a n -> p (a n)"), bd, ALU.add).then_inc(S.o_y, 1)

            for b in range(3):
                nt = BLK[b][1]
                v.wait_ge((S.yk0_in, S.yk1_in, S.yk2_in)[b], 16 * TOPK)
                for k in range(TOPK):
                    src = yk[0:nt, b * TOPK + k, :]
                    if k == 0:
                        link(TS(acc[0:nt, b, :], src, ge[0:nt, b, 0:1], None, ALU.mult))
                    else:
                        ins = STT(acc[0:nt, b, :], src, ge[0:nt, b, k:k + 1], acc[0:nt, b, :], ALU.mult, ALU.add)
                        if k < TOPK - 1:
                            link(ins)
                ins.then_inc(S.moe_ok, 1)
            with overflow(v):
                v.wait_ge(S.moe_ok, 3)
                v.wait_ge(S.o_yk, 16 * 3 * TOPK)
                start = 8 * NOVER
                for b in range(3):
                    nt = BLK[b][1]
                    for k in range(TOPK):
                        ins = STT(acc[0:nt, b, :], yk[0:nt, b * TOPK + k, :], ge2[0:nt, b, k:k + 1], acc[0:nt, b, :],
                                  ALU.mult, ALU.add)
                        if b < 2 or k < TOPK - 1:
                            start += 1
                            ins.then_inc(S.o_dve, 1)
                            v.wait_ge(S.o_dve, start)
                ins.then_inc(S.o_add, 1)
            for b, (t0, nt) in enumerate(BLK):
                v.wait_ge(S.mt_mm, b + 1)
                q = 4 * (b % 2)
                ps = PS[:, q:q + 2, :].rearrange("p a n -> p (a n)").rearrange("p (k n) -> p k n", k=KT)[:, :, 0:nt]
                TT(xc[:, :, t0:t0 + nt], xc[:, :, t0:t0 + nt], ps, ALU.add).then_inc(S.mt_ev, 1)
            v.wait_ge(S.mt_ev, 3)
            TT(lt[:, :, :], xc[:, :, :], xc[:, :, :], ALU.mult).then_inc(S.sq_ok, 1)
            normed(3, xc[:, :, :], FGP)
            for m in range(KT):
                v.wait_ge(S.pg_ev, m + 1)
                v.wait_ge(S.pl_mm, m + 1)
                TT(sgp[:, m, :], sgp[:, m, :], PS[:, 4 + m % 4, 0:T], ALU.mult).then_inc(S.pl_ev, 1)
            v.wait_ge(S.pl_ev, KT)
            TT(sgp, sgp, xc[:, :, :], ALU.add).then_inc(S.y_ok, 1)

        @block.gpsimd
        def _(po):
            po.wait_ge(S.h_ok, 1)
            for g in range(NG):
                n = (WB[g] - 1) // 16 * 16
                src, dst = a[f"cache{g}"], a[f"kvs{g}"]
                with po.Fori(0, NS) as b:
                    po.dma_start(dst[b, 0:n, :].rearrange("(q r) n -> q (r n)", q=16),
                                 src[b, 1:n + 1, :].rearrange("(q r) n -> q (r n)", q=16)).then_inc(S.kv_copy, 16)
                po.dma_start(dst[:, n:WB[g] - 1, :].rearrange("b r n -> r b n"),
                             src[:, n + 1:WB[g], :].rearrange("b r n -> r b n")).then_inc(S.kv_copy, 16)
            po.dma_start(tabd, a["zeros"]).then_inc(S.tab_z, 16)
            po.wait_ge(S.z_evac, ZX + KT)
            po.wait_ge(S.x_in, 32)
            po.dma_start(a["convp"], Z[:, ZX:ZX + KT, NP - 3:NP]).then_inc(S.conv_out, 16)
            po.dma_start(a["convs"][:, :, 0:2 * NS], feat[:, :, FSC + NS:FSC + 3 * NS]).then_inc(S.conv_out, 16)
            po.dma_start(a["convs"][:, :, 2 * NS:3 * NS], Z[:, ZX:ZX + KT, NP:T]).then_inc(S.conv_out, 16)
            po.wait_ge(S.qk_normed, 1)
            po.dma_start(rot[0:16, :, :], Z[16:32, 0:24, :]).then_inc(S.rot_in, 16)
            po.dma_start(rot[16:32, :, :], Z[0:16, 0:24, :]).then_inc(S.rot_in, 16)
            for kv in range(2):
                for b, (t0, nt) in enumerate(BLK):
                    direct = kv == 1 and b < 2
                    po.wait_ge(S.tk_ev, 9 * kv + 3 * b + 3)
                    for g in range(NG):
                        src = vtok[:, b % 2, g * CH:(g + 1) * CH] if direct else stage[0:nt, g * CH:(g + 1) * CH]
                        if b == 2:
                            dst = a[f"kvs{g}"][:, WB[g] - 1, kv * CH:(kv + 1) * CH]
                        elif g == 0:
                            if b == 0:
                                continue
                            dst = a["kvp0"][:, kv * CH:(kv + 1) * CH]
                        else:
                            dst = a[f"kvp{g}"][t0:t0 + nt, kv * CH:(kv + 1) * CH]
                        po.dma_start(dst, src).then_inc(S.vt_out if direct else S.tk_out, 16)
            po.wait_ge(S.lru_y, 1)
            po.dma_start(a["hp"], lt[:, :, NP - 1:NP], allow_slow_non_contiguous=True).then_inc(S.h_out, 16)
            po.dma_start(a["hs"], lt[:, :, NP:T]).then_inc(S.h_out, 16)
            po.wait_ge(S.lru_yg, 1)
            po.dma_start(xc[:, :, :], a["xT"]).then_inc(S.res_in, 16)
            for b, (t0, nt) in enumerate(BLK):
                po.wait_ge(S.ht_ev, b + 1)
                po.dma_start(hrow[t0:t0 + nt, :], hstage[0:nt, :]).then_inc(S.ht_out, 16)
            po.wait_ge(S.rt_ready, 1)
            po.wait_ge(S.tab_z, 16)
            for b, (t0, nt) in enumerate(BLK):
                for k in range(TOPK):
                    c = b * TOPK + k
                    po.indirect_dma_start(tabd.rearrange("p (n o) -> (p n) o", o=1),
                                          bass.IndirectOffsetOnAxis(ap=itab[0:nt, c:c + 1], axis=0),
                                          tokid[0:nt, b:b + 1], None).then_inc(S.tab_put, 16)
            po.wait_ge(S.tab_put, 16 * 3 * TOPK)
            po.dma_start(tab, tabd).then_inc(S.tab_in, 16)
            po.wait_ge(S.tab_in, 16)
            po.wait_ge(S.ht_out, 48)
            po.wait_ge(S.cnt_ready, 1)

            carriers = iter(range(64))

            def held(sem, n):
                po.wait_ge(sem, n)
                if not isinstance(n, int):
                    c = next(carriers)
                    one = cst[0:1, C_ONE:C_ONE + 1]
                    nc.gpsimd.tensor_tensor(carried[:, c:c + 1], one, one, op=ALU.add)

            def gather(e, done):
                if done is not None:
                    held(S.xg_in, 16 * done)
                nc.gpsimd.tensor_copy(idxc, tab[:, e:e + 1] if isinstance(e, int) else tab[:, bass.ds(e, 1)])\
                    .then_inc(S.idx_ok, 1)
                held(S.idx_ok, e + 1)
                po.indirect_dma_start(xg, None, hrow, bass.IndirectOffsetOnAxis(ap=idxc, axis=0)).then_inc(S.xg_in, 16)

            def biases(e):
                po.dma_start(brow, a["bcat"][e]).then_inc(S.brow_in, 16)
                held(S.brow_in, 16 * (e + 1))

            def spread(dst, at, n, sem):
                nc.gpsimd.partition_broadcast(dst, brow[:, at:at + n]).then_inc(sem, 1)

            def flat(v):
                return v.rearrange("p a n -> p (a n)")

            def step(e, last=False):
                held(S.bcd, e)
                biases(e)
                held(S.ps0_rd, e)
                spread(flat(bg0), 0, D, S.bc0)
                if not last:
                    held(S.t_mm, 4 * e)
                    gather(e + 1, e + 1)
                held(S.ps1_rd, e)
                spread(flat(bg1), D, D, S.bc1)
                held(S.y_ev, e)
                po.dma_start(yrow[bass.ds((e - 1) * CAP, CAP), :], yb).then_inc(S.y_out, 16)
                spread(bd, 2 * D, D, S.bcd)

            gather(0, None)
            biases(0)
            spread(flat(bg0), 0, D, S.bc0)
            spread(flat(bg1), D, D, S.bc1)
            spread(bd, 2 * D, D, S.bcd)
            held(S.t_mm, 2)
            gather(1, 1)
            with po.Fori(1, E - 1) as e:
                step(e)
            step(E - 1, last=True)
            held(S.y_ev, E)
            po.dma_start(yrow[(E - 1) * CAP:E * CAP, :], yb).then_inc(S.y_out, 16)
            held(S.y_out, 16 * E)
            held(S.d1_mm, E)
            with overflow(po):
                for c in range(NCHUNK - 1):
                    with po.Fori(0, E) as e:
                        n = e + c * E
                        held(S.o_y, n + 1)
                        nc.gpsimd.tensor_copy(idxc, tab[:, bass.ds(n + E, 1)]).then_inc(S.o_idx, 1)
                        held(S.o_idx, n + 1)
                        po.indirect_dma_start(xg, None, hrow, bass.IndirectOffsetOnAxis(ap=idxc, axis=0)).then_inc(S.o_x, 16)
                        po.dma_start(brow, a["bcat"][e]).then_inc(S.o_b, 16)
                        held(S.o_b, 16 * (n + 1))
                        spread(flat(bg0), 0, D, S.o_bc)
                        spread(flat(bg1), D, D, S.o_bc)
                        spread(bd, 2 * D, D, S.o_bc)
                        held(S.o_x, 16 * (n + 1))
                        held(S.o_y, n + 2)
                        po.dma_start(yrow2[bass.ds(n * CAP, CAP), :], yb).then_inc(S.o_st, 16)
                        held(S.o_st, 16 * (n + 1))
            for b, (t0, nt) in enumerate(BLK):
                for k in range(TOPK):
                    c = b * TOPK + k
                    po.indirect_dma_start(yk[0:nt, c, :], None, yrow,
                                          bass.IndirectOffsetOnAxis(ap=irow[0:nt, c:c + 1], axis=0)).then_inc((S.yk0_in, S.yk1_in, S.yk2_in)[b], 16)
            with overflow(po):
                held(S.moe_ok, 3)
                for b, (t0, nt) in enumerate(BLK):
                    for k in range(TOPK):
                        c = b * TOPK + k
                        po.indirect_dma_start(yk[0:nt, c, :], None, yrow2,
                                              bass.IndirectOffsetOnAxis(ap=irow2[0:nt, c:c + 1], axis=0)).then_inc(S.o_yk, 16)


_OUTS = [("yT", (P, KT, T)), ("kvp0", (1, 1, 128, 2, HPG, HD)), ("kvp1", (1, 1, NP, 2, HPG, HD)),
         ("kvp2", (1, 1, NP, 2, HPG, HD)), ("convp", (P, KT, 3)), ("hp", (P, KT, 1)),
         ("kvs0", (1, NS, WB[0], 2, HPG, HD)), ("kvs1", (1, NS, WB[1], 2, HPG, HD)),
         ("kvs2", (1, NS, WB[2], 2, HPG, HD)), ("convs", (P, KT, 3 * NS)), ("hs", (P, KT, NS))]


def constants():
    import numpy as np
    c = np.zeros((P, NCST), np.float32)
    p = np.arange(P)
    c[:, C_ID:C_ID + P] = np.eye(P)
    c[:, C_ONE:C_ONE + P] = 1
    c[:, C_TRI:C_TRI + P] = p[:, None] < p[None, :]
    for qb, at in ((0, C_MASK0), (1, C_MASK1)):
        n = P * (qb + 1)
        rel = (qb * P + p)[:, None] - np.arange(n)[None, :]
        for g in range(NG):
            ok = (rel >= 0) & (rel % DIL[g] == 0) & (rel <= (128, 512, 2048)[g])
            c[:, at + g * n:at + (g + 1) * n] = np.where(ok, 0, -1e30)
    c[:, C_IOTA:C_IOTA + E] = np.arange(E)
    c[:, C_EOFF:C_EOFF + E] = np.arange(E) * CAP
    for b, (t0, nt) in enumerate(BLK):
        c[:, C_TOK + b] = t0 + p
        c[:, C_VALID + b] = p < nt
    c[:, C_EPS] = 1e-6
    half = HD // 8
    freqs = np.float32(500000.0) ** (-np.arange(half, dtype=np.float32) * np.float32(2.0 / (2 * half)))
    where = np.concatenate([np.arange(NP), np.full(NS, 1024)]).astype(np.float32)
    ang = (where[None, :] * freqs.astype(np.float32)[:, None]).astype(np.float32).astype(np.float64)
    cos, sin = np.cos(ang), np.sin(ang)
    rope = np.stack([np.concatenate([cos, cos]), np.concatenate([-sin, sin])], 1).astype(np.float32)
    return c, np.ascontiguousarray(rope)


def layout(i):
    import numpy as np
    i = {k: np.asarray(v) for k, v in i.items()}
    cst, rope = constants()

    def cols(v):
        v = np.moveaxis(v.reshape(-1, KT, P), 0, -1)
        return np.ascontiguousarray(v.transpose(1, 0, 2))

    order = [4, 5, 6, 7, 8, 9, 0, 1, 2, 3, 10, 11, 12, 13, 14, 15, 16]
    win = i["w_in"][0].reshape(KT, P, NPIECE, CH).transpose(2, 1, 0, 3)[order]
    sc = i["state_conv"][0].transpose(1, 0, 2).reshape(3 * NS, D)
    feat = np.concatenate([i["conv_w"][0], i["conv_b"], i["b_rg_a"], i["b_rg_x"], i["lru_lambda"], i["g_mix"],
                           i["g_ffn"], i["g_ple"], sc, i["state_h"][0]], 0)
    wrg = np.stack([i["w_rg_a"][0], i["w_rg_x"][0]]).reshape(2, 4, 2, P, 256).transpose(3, 0, 1, 2, 4)
    out = dict(
        cst=cst, rope=rope, zeros=np.zeros((P, NCHUNK * E), np.int32), feat=cols(feat),
        xT=cols(np.concatenate([i["x_prompt"][0], i["x_sample"][:, 0]], 0)),
        win=np.ascontiguousarray(win), gqk=np.ascontiguousarray(np.concatenate([i["g_q"], i["g_k"]], 0).T),
        wrg=np.ascontiguousarray(wrg.reshape(P, 4096)),
        w_router=i["w_router"][0], b_router=i["b_router"], w_br_lru=i["w_br_lru"][0], w_br_att=i["w_br_att"][0],
        w_out=i["w_out"][0], w_gu=i["w_gu"][0], w_down=i["w_down"][0], w_ple_gate=i["w_ple_gate"][0],
        w_ple=i["w_ple"][0])
    for g in range(NG):
        c = i[f"cache_kv_g{g}"][0]
        out[f"cache{g}"] = c.reshape(NS, WB[g], 2 * CH)
        out[f"kt{g}"] = np.ascontiguousarray(c[:, ::DIL[g], 0].transpose(3, 0, 2, 1)).reshape(P, -1)
    pp = np.concatenate([i["p_prompt"][0, 0], i["p_sample"][0, :, 0]], 0)
    out["pT"] = np.ascontiguousarray(pp.reshape(T, 2, P).transpose(2, 1, 0))
    b = i["b_gu"][0].reshape(E, 2, 2, CH).transpose(0, 2, 1, 3).reshape(E, 2 * D)
    out["bcat"] = np.concatenate([b, i["b_down"][0]], 1).reshape(E, 1, 3 * D)
    return out


def program(nc, arrays):
    a = {}
    for n, v in arrays.items():
        a[n] = nc.dram_tensor("in_" + n, v.shape, mybir.dt.from_np(v.dtype), kind="ExternalInput").ap()
    for n, s in _OUTS:
        ap = nc.dram_tensor("out_" + n, s, F32, kind="ExternalOutput").ap()
        if n.startswith("kvp"):
            ap = ap.rearrange("l o s c h d -> (l o s) (c h d)")
        elif n.startswith("kvs"):
            ap = ap.rearrange("l b s c h d -> (l b) s (c h d)")
        a[n] = ap
    for g in range(NG):
        n = SKEYS[g]
        a[f"kt{g}"] = a[f"kt{g}"].rearrange("p (s k) -> p s k", k=n)
    build(nc, a)


def kernel(**inputs):
    import numpy as np
    import concourse.bacc as bacc
    from concourse.bass_utils import run_bass_kernel_spmd

    arrays = layout(inputs)
    nc = bacc.Bacc("TRN2", target_bir_lowering=False, num_devices=1)
    program(nc, arrays)
    r = run_bass_kernel_spmd(nc, [{"in_" + n: v for n, v in arrays.items()}], core_ids=[0])
    return assemble({n: r.results[0]["out_" + n] for n, _ in _OUTS})


def assemble(o):
    import numpy as np

    def rows(v):
        return np.ascontiguousarray(v.transpose(2, 1, 0)).reshape(v.shape[2], D)

    y = rows(o["yT"])
    convs = rows(o["convs"]).reshape(3, NS, D).transpose(1, 0, 2)
    return (y[None, 0:NP], y[NP:T, None], o["kvp0"], o["kvp1"], o["kvp2"], rows(o["convp"])[None, None],
            rows(o["hp"])[None], o["kvs0"], o["kvs1"], o["kvs2"], np.ascontiguousarray(convs)[None],
            rows(o["hs"])[None])
```

```python
from contextlib import ExitStack

import concourse.bass as bass
from concourse import mybir

P = 128
D = 1024
KT = D // P
NP, NS = 256, 8
T = NP + NS
HD = 128
HPG = 4
NG = 3
NHEAD = NG * HPG
E = 32
TOPK = 4
NFEAT = 43
BLK = [(0, 128), (128, 128), (256, NS)]
WB = (128, 512, 1024)
DIL = (1, 4, 16)
SKEYS = (128, 128, 64)
CH = 512
NPIECE = 17
LOOP_A = 8
ZQ, ZK, ZX, ZGR, ZV, ZGL, ZGA = 0, 12, 24, 32, 40, 52, 60
NZ = 68
SCALE = HD ** -0.5
LIMIT, ALPHA, LRU_C = 7.0, 1.702, 8.0
FW, FCB, FBA, FBX, FLAM, FGM, FGF, FGP, FSC, FSH = 0, 4, 5, 6, 7, 8, 9, 10, 11, 35
C_ID, C_ONE, C_TRI, C_MASK0, C_MASK1 = 0, 128, 256, 384, 768
C_IOTA, C_EOFF, C_ETAB, C_TOK, C_VALID, C_EPS, NCST = 1536, 1568, 1600, 1632, 1635, 1638, 1640
CAP = 64
TK_OUT = (0, 32, 80, 128, 176)
VT_OUT = 80
NCHUNK = 3

ALU = mybir.AluOpType
ACT = mybir.ActivationFunctionType
AX = mybir.AxisListType.X
F32 = mybir.dt.float32
I32 = mybir.dt.int32
U32 = mybir.dt.uint32


class Signals:

    def __init__(self, sem):
        self.sq_ok = sem("sq_ok")
        self.ss_sum = sem("ss_sum")
        self.rms_ok = sem("rms_ok")
        self.h_ok = sem("h_ok")
        self.v_in = sem("v_in")
        self.cst_in = sem("cst_in")
        self.x_in = sem("x_in")
        self.rope_in = sem("rope_in")
        self.win0 = sem("win0")
        self.win1 = sem("win1")
        self.win2 = sem("win2")
        self.win3 = sem("win3")
        self.z_done = sem("z_done")
        self.z_evac = sem("z_evac")
        self.sq_qk = sem("sq_qk")
        self.qkn_mm = sem("qkn_mm")
        self.qkn_ev = sem("qkn_ev")
        self.qk_normed = sem("qk_normed")
        self.rot_in = sem("rot_in")
        self.roped = sem("roped")
        self.conv_done = sem("conv_done")
        self.conv_out = sem("conv_out")
        self.wrg_in = sem("wrg_in")
        self.gate_mm = sem("gate_mm")
        self.gate_ev = sem("gate_ev")
        self.kt0_in = sem("kt0_in")
        self.kt1_in = sem("kt1_in")
        self.kt2_in = sem("kt2_in")
        self.ss_mm = sem("ss_mm")
        self.ss_ev = sem("ss_ev")
        self.ss_prod = sem("ss_prod")
        self.ss_rows = sem("ss_rows")
        self.sp_exp = sem("sp_exp")
        self.sp_ready = sem("sp_ready")
        self.st_mm = sem("st_mm")
        self.st_ev = sem("st_ev")
        self.sd_ready = sem("sd_ready")
        self.sb_mm = sem("sb_mm")
        self.sb_ev = sem("sb_ev")
        self.spv_mm = sem("spv_mm")
        self.satt = sem("satt")
        self.tk_mm = sem("tk_mm")
        self.tk_ev = sem("tk_ev")
        self.tk_out = sem("tk_out")
        self.vt_out = sem("vt_out")
        self.h_out = sem("h_out")
        self.at_sc = sem("at_sc")
        self.at_s = sem("at_s")
        self.at_nm = sem("at_nm")
        self.at_e = sem("at_e")
        self.at_p = sem("at_p")
        self.at_t = sem("at_t")
        self.at_pt = sem("at_pt")
        self.at_pv = sem("at_pv")
        self.at_ev = sem("at_ev")
        self.nsp = sem("nsp")
        self.lru_l = sem("lru_l")
        self.lru_th = sem("lru_th")
        self.lru_e = sem("lru_e")
        self.lru_c = sem("lru_c")
        self.lru_s = sem("lru_s")
        self.lru_a = sem("lru_a")
        self.lru_y = sem("lru_y")
        self.lru_yg = sem("lru_yg")
        self.gelu_z = sem("gelu_z")
        self.sig_z = sem("sig_z")
        self.wba_in = sem("wba_in")
        self.wbl_in = sem("wbl_in")
        self.wout_in = sem("wout_in")
        self.ba_mm = sem("ba_mm")
        self.ba_ev = sem("ba_ev")
        self.bl_mm = sem("bl_mm")
        self.bl_ev = sem("bl_ev")
        self.merged = sem("merged")
        self.wo_mm = sem("wo_mm")
        self.wo_ev = sem("wo_ev")
        self.res_in = sem("res_in")
        self.wr_in = sem("wr_in")
        self.lg_mm = sem("lg_mm")
        self.ht_mm = sem("ht_mm")
        self.ht_ev = sem("ht_ev")
        self.ht_out = sem("ht_out")
        self.rk_mm = sem("rk_mm")
        self.rt_exp = sem("rt_exp")
        self.oh_ready = sem("oh_ready")
        self.rt_ready = sem("rt_ready")
        self.tab_z = sem("tab_z")
        self.tab_put = sem("tab_put")
        self.tab_in = sem("tab_in")
        self.cnt_ready = sem("cnt_ready")
        self.xg_in = sem("xg_in")
        self.idx_ok = sem("idx_ok")
        self.brow_in = sem("brow_in")
        self.g_mm = sem("g_mm")
        self.u_mm = sem("u_mm")
        self.d0_mm = sem("d0_mm")
        self.d1_mm = sem("d1_mm")
        self.w0 = sem("w0")
        self.w1 = sem("w1")
        self.w2 = sem("w2")
        self.w3 = sem("w3")
        self.w4 = sem("w4")
        self.w5 = sem("w5")
        self.x_tr = sem("x_tr")
        self.xT_ok = sem("xT_ok")
        self.h_tr = sem("h_tr")
        self.hT_ok = sem("hT_ok")
        self.bias_used = sem("bias_used")
        self.gmin = sem("gmin")
        self.sig = sem("sig")
        self.gated = sem("gated")
        self.u_rd = sem("u_rd")
        self.hid_ok = sem("hid_ok")
        self.y_ev = sem("y_ev")
        self.y_out = sem("y_out")
        self.yk0_in = sem("yk0_in")
        self.yk1_in = sem("yk1_in")
        self.yk2_in = sem("yk2_in")
        self.moe_ok = sem("moe_ok")
        self.mt_mm = sem("mt_mm")
        self.mt_ev = sem("mt_ev")
        self.wpg_in = sem("wpg_in")
        self.wpl_in = sem("wpl_in")
        self.pg_mm = sem("pg_mm")
        self.pg_ev = sem("pg_ev")
        self.pl_mm = sem("pl_mm")
        self.pl_ev = sem("pl_ev")
        self.y_ok = sem("y_ok")
        self.out_done = sem("out_done")
        self.kv_copy = sem("kv_copy")
        self.dve = sem("dve")
        self.act = sem("act")
        self.o_w = sem("o_w")
        self.o_idx = sem("o_idx")
        self.o_x = sem("o_x")
        self.o_b = sem("o_b")
        self.o_bc = sem("o_bc")
        self.o_st = sem("o_st")
        self.o_t = sem("o_t")
        self.o_tc = sem("o_tc")
        self.o_gu = sem("o_gu")
        self.o_g = sem("o_g")
        self.o_sig = sem("o_sig")
        self.o_h = sem("o_h")
        self.o_d = sem("o_d")
        self.o_y = sem("o_y")
        self.o_yk = sem("o_yk")
        self.o_add = sem("o_add")
        self.o_dve = sem("o_dve")



def build(nc, a):
    with ExitStack() as ctx:
        def sb(name, shape, dt=F32):
            return ctx.enter_context(nc.sbuf_tensor(name, shape, dt))

        S = Signals(lambda name: ctx.enter_context(nc.semaphore(name)))
        PS = ctx.enter_context(nc.psum_tensor("PS", [P, 8, CH], F32))

        ring = sb("ring", [P, 6, 4096])
        Zb = sb("Zb", [P, NZ * T])
        Z = Zb[:, :].rearrange("p (n t) -> p n t", t=T)
        cst = sb("cst", [P, NCST])
        feat = sb("feat", [P, KT, NFEAT])
        gqk = sb("gqk", [P, 2])
        hT = sb("hT", [P, KT, T])
        xc = sb("xc", [P, KT, T])
        lt = sb("lt", [P, KT, T])
        attT = sb("attT", [P, HPG, T])
        rope = attT[0:32, 0:2, :]
        rstd = sb("rstd", [P, T])
        sm = sb("sm", [P, 64])
        nsp = sb("nsp", [P, 6, KT])
        sct = sb("sct", [P, 96])
        prod = sb("prod", [P, 96])
        srow = sb("srow", [32, 324])
        sdiag = sb("sdiag", [32, 3, 32])
        sptt = sb("sptt", [P, 96])
        brt = sb("brt", [1, E])
        W2 = ring[:, 4:6, :].rearrange("p a n -> p (a n)")
        sq_qk = W2[:, 0:24 * T]
        rot = W2[0:32, 0:24 * T].rearrange("p (n t) -> p n t", t=T)
        vtok = W2[:, 0:3072].rearrange("p (b n) -> p b n", b=2)
        sS = W2[:, 3072:4608].rearrange("p (b n) -> p b n", b=2)
        sPT = W2[:, 4608:6144].rearrange("p (b n) -> p b n", b=2)
        stage = W2[:, 6144:7680]
        wrg = ring[:, 1, :].rearrange("p (a n c d) -> p a n c d", a=2, n=4, c=2)
        kts = [ring[:, 2, :].rearrange("p (s k) -> p s k", s=32), ring[:, 3, :].rearrange("p (s k) -> p s k", s=32),
               ring[:, 0, 0:2048].rearrange("p (s k) -> p s k", s=32)]
        vts = [ring[:, s, :].rearrange("p (b n) -> p b n", b=NS) for s in (1, 2, 3)]
        wba = ring[:, 0, :].rearrange("p (k n) -> p k n", k=4)
        wbl = [ring[:, s, :].rearrange("p (k n) -> p k n", k=4) for s in (1, 2)]
        wout = [ring[:, s, :].rearrange("p (k n) -> p k n", k=4) for s in (3, 0)]
        pos = [0]

        def zb(shape, dt=None):
            n = 1
            for s in shape[1:]:
                n *= s
            v = Zb[0:shape[0], pos[0]:pos[0] + n]
            pos[0] += n
            if dt is not None:
                v = v.bitcast(dt)
            return v if len(shape) == 2 else v.rearrange("p (a n) -> p a n", a=shape[1])

        xg = zb([P, D])
        xgT = zb([P, KT, P])
        hm = zb([P, D])
        hmT = zb([P, KT, P])
        sg, ss_, su = zb([P, CH]), zb([P, CH]), zb([P, CH])
        yb = zb([P, D])
        brow = zb([1, 3 * D])
        bg0, bg1, bd = zb([P, 2, CH]), zb([P, 2, CH]), zb([P, D])
        logit = zb([P, 3, E])
        oh = [zb([P, 3, E]) for _ in range(TOPK)]
        route = zb([P, 3, E])
        rtmp, rtab, rrow, rslot = zb([P, 3, E]), zb([P, 3, E]), zb([P, 3, E]), zb([P, 3, E])
        rsel = zb([P, 3, E])
        mx, mxi, mif = zb([P, 3, 8]), zb([P, 3, 8], U32), zb([P, 3, 8])
        ge, gs = zb([P, 3, TOPK]), zb([P, 3])
        drow, dtab = zb([P, 3, TOPK]), zb([P, 3, TOPK])
        irow, itab = zb([P, 3 * TOPK], I32), zb([P, 3 * TOPK], I32)
        over, drow2, ge2 = zb([P, 3, TOPK]), zb([P, 3, TOPK]), zb([P, 3, TOPK])
        irow2 = zb([P, 3 * TOPK], I32)
        cmax, most = zb([1, 1]), zb([1, 1], I32)
        tokid = zb([P, 3], I32)
        tab = zb([P, NCHUNK * E], I32)
        idxc = zb([P, 1], I32)
        carried = zb([1, 64])

        assert pos[0] <= NZ * T, pos[0]
        hstage = xg
        wr = hm[:, 0:KT * E].rearrange("p (k n) -> p k n", k=KT)
        yk = ring[:, 0:3, :].rearrange("p a n -> p (a n)").rearrange("p (k n) -> p k n", k=12)
        acc = ring[:, 3, 0:3072].rearrange("p (b n) -> p b n", b=3)
        wpg = [ring[:, s, :].rearrange("p (k n) -> p k n", k=4) for s in (4, 5)]
        wpl = Zb[:, 0:2048].rearrange("p (k n) -> p k n", k=2)
        pT = Zb[:, 2048:2048 + 2 * T].rearrange("p (k t) -> p k t", k=2)
        sgp = Zb[:, 4096:4096 + KT * T].rearrange("p (k t) -> p k t", k=KT)

        NOVER = (NCHUNK - 1) * E

        def overflow(eng):
            return eng.If(eng.value_load(most, min_val=0, max_val=T) > CAP)

        ident = cst[:, C_ID:C_ID + P]
        ones = cst[:, C_ONE:C_ONE + P]
        tri = cst[:, C_TRI:C_TRI + P]
        eps = cst[:, C_EPS:C_EPS + 1]

        def fv(c):
            return feat[:, :, c:c + 1].to_broadcast([P, KT, T])

        def over_tiles(v, n=KT):
            return v.unsqueeze(1).to_broadcast([v.shape[0], n, v.shape[-1]])

        hrow = nc.dram_tensor("hrow", (T, D), F32).ap()
        tabd = nc.dram_tensor("tabd", (P, NCHUNK * E), I32).ap()
        yrow2 = nc.dram_tensor("yrow2", (NOVER * P, D), F32).ap()
        yrow = nc.dram_tensor("yrow", (E * CAP, D), F32).ap()
        block = ctx.enter_context(nc.Block())

        @block.sync
        def _(sp):
            xT0 = Z[:, ZGL:ZGL + KT, :]
            sp.dma_start(cst[:, :], a["cst"]).then_inc(S.cst_in, 16)
            sp.dma_start(xT0, a["xT"]).then_inc(S.x_in, 16)
            sp.dma_start(feat[:, :, :], a["feat"]).then_inc(S.x_in, 16)

            def win(piece, slot):
                return sp.dma_start(ring[:, slot, :], a["win"][piece].rearrange("p k n -> p (k n)"))

            wins = (S.win0, S.win1, S.win2, S.win3)
            for s in range(4):
                win(s, s).then_inc(wins[s], 16)
            sp.dma_start(rope, a["rope"]).then_inc(S.rope_in, 16)
            sp.dma_start(gqk[:, :], a["gqk"]).then_inc(S.rope_in, 16)
            with sp.Fori(1, 4) as i:
                for s in range(4):
                    sp.wait_ge(S.z_done, 16 * i + 4 * s - 12)
                    win(4 * i + s, s).then_inc(wins[s], 16)
            sp.wait_ge(S.z_done, 4 * 13)
            win(16, 0).then_inc(S.win0, 16)
            sp.wait_ge(S.z_done, 4 * 14)
            sp.dma_start(ring[:, 1, :], a["wrg"]).then_inc(S.wrg_in, 16)
            sp.wait_ge(S.z_done, 4 * 15)
            sp.dma_start(kts[0], a["kt0"]).then_inc(S.kt0_in, 16)
            sp.wait_ge(S.z_done, 4 * 16)
            sp.dma_start(kts[1], a["kt1"]).then_inc(S.kt1_in, 16)
            sp.wait_ge(S.z_done, NZ)
            sp.dma_start(kts[2], a["kt2"]).then_inc(S.kt2_in, 16)
            sp.wait_ge(S.gate_mm, 16)
            sp.dma_start(brt[:, :], a["b_router"]).then_inc(S.wr_in, 16)

            def cached_v(g, sem):
                n = SKEYS[g]
                src = a[f"cache{g}"].rearrange("b (k r) n -> k b r n", r=DIL[g])[:, :, 0, CH:2 * CH]
                sp.dma_start(vts[g][0:n, :, :], src).then_inc(sem, 16)

            cached_v(0, S.v_in)
            sp.wait_ge(S.ss_mm, 1)
            cached_v(1, S.v_in)
            cached_v(2, S.v_in)

            def half(w, k0, view, sem):
                sp.dma_start(view, w[k0 * P:(k0 + 4) * P, :].rearrange("(k p) n -> p k n", p=P)).then_inc(sem, 16)

            half(a["w_br_att"], 0, wba, S.wba_in)
            sp.wait_ge(S.spv_mm, 1)
            half(a["w_br_lru"], 0, wbl[0], S.wbl_in)
            half(a["w_br_lru"], 4, wbl[1], S.wbl_in)
            half(a["w_out"], 0, wout[0], S.wout_in)
            sp.wait_ge(S.ba_mm, KT)
            half(a["w_out"], 4, wout[1], S.wout_in)

            def gu(e, c, h):
                return a["w_gu"][e].rearrange("(k p) n -> p k n", p=P)[:, :, c * D + h * CH:c * D + h * CH + CH]

            def dn(e, h):
                return a["w_down"][e][h * CH:(h + 1) * CH, :].rearrange("(k p) n -> p k n", p=P)

            def r8(s):
                return ring[:, s, :].rearrange("p (k n) -> p k n", k=8)

            def r4(s):
                return ring[:, s, :].rearrange("p (k n) -> p k n", k=4)

            full = (S.w0, S.w1, S.w2, S.w3, S.w4, S.w5)
            used = (S.g_mm, S.g_mm, S.u_mm, S.u_mm, S.d0_mm, S.d1_mm)
            sp.wait_ge(S.at_pv, 8)
            sp.wait_ge(S.tk_out, TK_OUT[4])
            sp.wait_ge(S.vt_out, VT_OUT)
            sp.dma_start(wr[:, :, :], a["w_router"].rearrange("(k p) n -> p k n", p=P)).then_inc(S.wr_in, 16)
            sp.dma_start(r4(4), dn(0, 0)).then_inc(S.w4, 16)
            sp.dma_start(r4(5), dn(0, 1)).then_inc(S.w5, 16)
            sp.wait_ge(S.bl_mm, KT)
            sp.dma_start(r8(1), gu(0, 0, 1)).then_inc(S.w1, 16)
            sp.dma_start(r8(2), gu(0, 1, 0)).then_inc(S.w2, 16)
            sp.wait_ge(S.wo_mm, KT)
            sp.dma_start(r8(0), gu(0, 0, 0)).then_inc(S.w0, 16)
            sp.dma_start(r8(3), gu(0, 1, 1)).then_inc(S.w3, 16)
            with sp.Fori(1, E) as e:
                for s in range(6):
                    sp.wait_ge(used[s], e)
                    if s < 4:
                        sp.dma_start(r8(s), gu(e, s // 2, s % 2)).then_inc(full[s], 16)
                    else:
                        sp.dma_start(r4(s), dn(e, s - 4)).then_inc(full[s], 16)
            sp.wait_ge(S.cnt_ready, 1)
            with overflow(sp):
                for s in range(6):
                    sp.wait_ge(used[s], E)
                for c in range(NCHUNK - 1):
                    with sp.Fori(0, E) as e:
                        sp.wait_ge(S.o_y, e + c * E + 1)
                        for s in range(4):
                            sp.dma_start(r8(s), gu(e, s % 2, s // 2)).then_inc(S.o_w, 16)
                        for s in range(2):
                            sp.dma_start(r4(4 + s), dn(e, s)).then_inc(S.o_w, 16)
                sp.wait_ge(S.o_y, NOVER + 1)
            sp.wait_ge(S.d0_mm, E)
            half(a["w_ple_gate"], 0, wpg[0], S.wpg_in)
            sp.wait_ge(S.d1_mm, E)
            half(a["w_ple_gate"], 4, wpg[1], S.wpg_in)
            sp.wait_ge(S.h_tr, E)
            sp.dma_start(wpl, a["w_ple"].rearrange("(k p) n -> p k n", p=P)).then_inc(S.wpl_in, 16)
            sp.dma_start(pT, a["pT"]).then_inc(S.wpl_in, 16)
            sp.wait_ge(S.y_ok, 1)
            sp.dma_start(a["yT"], sgp).then_inc(S.out_done, 16)
            sp.wait_ge(S.out_done, 16)
            sp.wait_ge(S.kv_copy, 16 * (NS + 1) * NG)
            sp.wait_ge(S.conv_out, 48)
            sp.wait_ge(S.h_out, 32)

        @block.tensor
        def _(pe):
            mm = nc.tensor.matmul

            def sum_sq(src, nth):
                pe.wait_ge(S.sq_ok, nth)
                for k in range(KT):
                    last = mm(PS[:, 4, 0:T], ones, src[:, k, :], start=(k == 0), stop=(k == KT - 1))
                last.then_inc(S.ss_sum, 1)

            pe.wait_ge(S.cst_in, 16)
            sum_sq(hT, 1)
            pe.wait_ge(S.h_ok, 1)
            wins = (S.win0, S.win1, S.win2, S.win3)

            def z_piece(piece, slot, fill, first=False):
                w = ring[:, slot, :].rearrange("p (k n) -> p k n", k=KT)
                pe.wait_ge(wins[slot], fill)
                for t in range(4):
                    if not first:
                        pe.wait_ge(S.z_evac, 4 * piece + t - 3)
                    for k in range(KT):
                        last = mm(PS[:, t, 0:T], w[:, k, t * P:(t + 1) * P], hT[:, k, :],
                                  start=(k == 0), stop=(k == KT - 1))
                    last.then_inc(S.z_done, 1)

            for s in range(4):
                z_piece(s, s, 16, first=(s == 0))
            for s in range(4):
                z_piece(4 + s, s, 32)
            pe.wait_ge(S.sq_qk, 1)
            for c in range(13):
                n = min(CH, 24 * T - c * CH)
                if c >= 4:
                    pe.wait_ge(S.qkn_ev, c - 3)
                mm(PS[:, 4 + c % 4, 0:n], ones, sq_qk[:, c * CH:c * CH + n], start=True, stop=True).then_inc(S.qkn_mm, 1)
            with pe.Fori(2, 4) as i:
                for s in range(4):
                    z_piece(4 * i + s, s, 16 * i + 16)
            z_piece(16, 0, 16 * 5)

            pe.wait_ge(S.wrg_in, 16)
            pe.wait_ge(S.conv_done, 1)
            for j in range(KT):
                for m in range(2):
                    n = 2 * j + m
                    pe.wait_ge(S.z_evac, NZ)
                    if n >= 8:
                        pe.wait_ge(S.gate_ev, n - 7)
                    for c in range(2):
                        last = mm(PS[:, n % 8, 0:T], wrg[:, m, j // 2, c, (j % 2) * P:(j % 2 + 1) * P],
                                  xc[:, 2 * (j // 2) + c, :], start=(c == 0), stop=(c == 1))
                    last.then_inc(S.gate_mm, 1)

            pe.wait_ge(S.roped, 1)
            pe.wait_ge(S.gate_ev, 16)
            for g, sem in enumerate((S.kt0_in, S.kt1_in, S.kt2_in)):
                pe.wait_ge(sem, 16)
                for b in range(NS):
                    for h in range(HPG):
                        c = b * HPG + h
                        last = mm(PS[0:SKEYS[g], 4, g * 32 + c:g * 32 + c + 1], kts[g][:, c, :],
                                  Z[:, ZQ + g * HPG + h, NP + b:NP + b + 1], start=True, stop=True)
            last.then_inc(S.ss_mm, 1)

            n = 0
            for z0 in (ZK, ZV):
                for b, (t0, nt) in enumerate(BLK):
                    for g in range(NG):
                        if n >= 4:
                            pe.wait_ge(S.tk_ev, n - 3)
                        for h in range(HPG):
                            last = nc.tensor.transpose(PS[0:nt, n % 4, h * P:(h + 1) * P],
                                                       Z[:, z0 + g * HPG + h, t0:t0 + nt], ident)
                        last.then_inc(S.tk_mm, 1)
                        n += 1

            pe.wait_ge(S.ss_ev, 1)
            off = 0
            for g in range(NG):
                n = SKEYS[g]
                nc.tensor.transpose(PS[0:32, 5, off:off + n], sct[0:n, g * 32:(g + 1) * 32], ident[0:n, 0:n])
                off += n
            pe.wait_ge(S.ss_prod, 1)
            for g in range(NG):
                last = mm(PS[0:32, 5, off + g:off + g + 1], prod[:, g * 32:(g + 1) * 32], ones[:, 0:1],
                          start=True, stop=True)
            last.then_inc(S.ss_rows, 1)

            def scores(it):
                h, qb = it // 2, it % 2
                n = P * (qb + 1)
                if it == 0:
                    pe.wait_ge(S.tk_ev, 18)
                if it >= 2:
                    pe.wait_ge(S.at_s, it - 1)
                ps = PS[:, 2 * (it % 2):2 * (it % 2) + 2, :].rearrange("p a n -> p (a n)")
                for g in range(NG):
                    last = mm(ps[:, g * n:(g + 1) * n], Z[:, ZQ + g * HPG + h, qb * P:(qb + 1) * P],
                              Z[:, ZK + g * HPG + h, 0:n], start=True, stop=True)
                last.then_inc(S.at_sc, 1)

            def weigh(it):
                h, qb = it // 2, it % 2
                blocks = [(g, kb) for g in range(NG) for kb in range(qb + 1)]
                pe.wait_ge(S.at_p, it + 1)
                if it >= 1:
                    pe.wait_ge(S.at_pt, it)
                else:
                    pe.wait_ge(S.sb_ev, 1)
                ps = PS[:, 4:6, :].rearrange("p a n -> p (a n)")
                for j in range(len(blocks)):
                    last = nc.tensor.transpose(ps[:, j * P:(j + 1) * P], sS[:, it % 2, j * P:(j + 1) * P], ident)
                last.then_inc(S.at_t, 1)
                pe.wait_ge(S.at_pt, it + 1)
                if it >= 2:
                    pe.wait_ge(S.at_ev, it - 1)
                for j, (g, kb) in enumerate(blocks):
                    last = mm(PS[:, 6 + it % 2, 0:P], vtok[:, kb, (g * HPG + h) * P:(g * HPG + h + 1) * P],
                              sPT[:, it % 2, j * P:(j + 1) * P], start=(j == 0), stop=(j == len(blocks) - 1))
                last.then_inc(S.at_pv, 1)

            scores(0)
            scores(1)
            pe.wait_ge(S.sp_ready, 1)
            off = 0
            for g in range(NG):
                n = SKEYS[g]
                last = nc.tensor.transpose(PS[0:n, 6, g * 32:(g + 1) * 32], srow[:, off:off + n], ident[0:32, 0:32])
                off += n
            last.then_inc(S.st_mm, 1)
            pe.wait_ge(S.sd_ready, 1)
            for g in range(NG):
                last = mm(PS[:, 7, g * 32:(g + 1) * 32], ones[0:32, :], sdiag[:, g, :], start=True, stop=True)
            last.then_inc(S.sb_mm, 1)
            for it in range(8):
                weigh(it)
                if it + 2 < 8:
                    scores(it + 2)
            pe.wait_ge(S.st_ev, 1)
            pe.wait_ge(S.at_s, 8)
            pe.wait_ge(S.v_in, 48)
            for b in range(NS):
                for h in range(HPG):
                    c = b * HPG + h
                    for g in range(NG):
                        n = SKEYS[g]
                        last = mm(PS[:, 0, c:c + 1], vts[g][0:n, b, h * P:(h + 1) * P],
                                  sptt[0:n, g * 32 + c:g * 32 + c + 1], start=(g == 0), stop=(g == NG - 1))
            last.then_inc(S.spv_mm, 1)

            def dense(weights, arrived, src, nk, done, evac, base=1):
                for m in range(KT):
                    if m >= 4:
                        pe.wait_ge(evac, m - 3)
                    for k in range(nk):
                        if m == 0 and k in arrived:
                            pe.wait_ge(*arrived[k])
                        last = mm(PS[:, 4 * base + m % 4, 0:T], weights(k)[:, m * P:(m + 1) * P], src[:, k, :],
                                  start=(k == 0), stop=(k == nk - 1))
                    last.then_inc(done, 1)

            pe.wait_ge(S.satt, 1)
            pe.wait_ge(S.at_ev, 8)
            dense(lambda k: wba[:, k, :], {0: (S.wba_in, 16)}, attT, 4, S.ba_mm, S.ba_ev)
            pe.wait_ge(S.lru_yg, 1)
            dense(lambda k: wbl[k // 4][:, k % 4, :], {0: (S.wbl_in, 32)}, Z[:, ZGR:ZGR + KT, :], 8, S.bl_mm, S.bl_ev, 0)
            pe.wait_ge(S.ba_ev, KT)
            pe.wait_ge(S.merged, 1)
            dense(lambda k: wout[k // 4][:, k % 4, :], {0: (S.wout_in, 32)}, hT, 8, S.wo_mm, S.wo_ev)
            pe.wait_ge(S.wo_ev, KT)

            sum_sq(lt, 2)
            pe.wait_ge(S.h_ok, 2)
            pe.wait_ge(S.wr_in, 32)
            for b, (t0, nt) in enumerate(BLK):
                o = PS[0:nt, 0, b * E:(b + 1) * E]
                mm(o, ones[0:1, 0:nt], brt[:, :], start=True, stop=False)
                for k in range(KT):
                    last = mm(o, hT[:, k, t0:t0 + nt], wr[:, k, :], start=False, stop=(k == KT - 1))
            last.then_inc(S.lg_mm, 1)
            for b, (t0, nt) in enumerate(BLK):
                if b:
                    pe.wait_ge(S.ht_ev, b)
                ps = PS[:, 6:8, :].rearrange("p a n -> p (a n)")
                for k in range(KT):
                    last = nc.tensor.transpose(ps[0:nt, k * P:(k + 1) * P], hT[:, k, t0:t0 + nt], ident)
                last.then_inc(S.ht_mm, 1)
            pe.wait_ge(S.oh_ready, 1)
            for b in range(3):
                o = PS[:, 1, b * E:(b + 1) * E]
                for c in range(b):
                    mm(o, ones, route[:, c, :], start=(c == 0), stop=False)
                mm(o, tri, route[:, b, :], start=(b == 0), stop=True)
            for c in range(3):
                last = mm(PS[:, 1, 3 * E:4 * E], ones, route[:, c, :], start=(c == 0), stop=(c == 2))
            last.then_inc(S.rk_mm, 1)

            def seed(bank, at, stride):
                for h in range(2):
                    c = at + h * stride
                    last = mm(PS[CAP * h:CAP * (h + 1), bank, :], ones[0:1, 0:CAP], brow[:, c:c + CH],
                              start=True, stop=False)
                return last

            def gate_up(bank, slot):
                w = [ring[:, slot + h, :].rearrange("p (k n) -> p k n", k=KT) for h in range(2)]
                for k in range(KT):
                    for h in range(2):
                        last = mm(PS[CAP * h:CAP * (h + 1), bank, :], xgT[:, k, 0:CAP], w[h][:, k, :],
                                  start=False, stop=(k == KT - 1))
                return last

            def down(half_):
                w = ring[:, 4 + half_, :].rearrange("p (k n) -> p k n", k=4)
                for k in range(4):
                    for h in range(2):
                        last = mm(PS[CAP * h:CAP * (h + 1), 4, :], hmT[:, k, half_ * CAP:(half_ + 1) * CAP],
                                  w[:, k, h * CH:(h + 1) * CH], start=False, stop=(half_ == 1 and k == 3))
                return last

            def rows_to_features():
                for k in range(KT):
                    last = nc.tensor.transpose(PS[:, 6, k * CAP:(k + 1) * CAP], xg[0:CAP, k * P:(k + 1) * P],
                                               ident[0:CAP, 0:CAP])
                last.then_inc(S.x_tr, 1)

            def body(e, first=False, last=False):
                pe.wait_ge(S.brow_in, 16 * (e + 1))
                if not first:
                    pe.wait_ge(S.gmin, e)
                seed(0, 0, 2 * CH)
                pe.wait_ge(S.w0, 16 * (e + 1))
                pe.wait_ge(S.w1, 16 * (e + 1))
                pe.wait_ge(S.xT_ok, e + 1)
                gate_up(0, 0).then_inc(S.g_mm, 1)
                if not first:
                    pe.wait_ge(S.u_rd, e)
                seed(1, CH, 2 * CH)
                pe.wait_ge(S.w2, 16 * (e + 1))
                pe.wait_ge(S.w3, 16 * (e + 1))
                gate_up(1, 2).then_inc(S.u_mm, 1)
                if not last:
                    pe.wait_ge(S.xg_in, 16 * (e + 2))
                if not first:
                    pe.wait_ge(S.y_ev, e)
                seed(4, 2 * D, CH).then_inc(S.bias_used, 1)
                if not last:
                    rows_to_features()
                pe.wait_ge(S.hid_ok, e + 1)
                for j in range(4):
                    tr = nc.tensor.transpose(PS[:, 7, j * P:(j + 1) * P], hm[:, j * P:(j + 1) * P], ident)
                tr.then_inc(S.h_tr, 1)
                pe.wait_ge(S.w4, 16 * (e + 1))
                pe.wait_ge(S.hT_ok, e + 1)
                down(0).then_inc(S.d0_mm, 1)
                pe.wait_ge(S.w5, 16 * (e + 1))
                down(1).then_inc(S.d1_mm, 1)

            pe.wait_ge(S.ht_ev, 3)
            pe.wait_ge(S.rt_ready, 1)
            pe.wait_ge(S.xg_in, 16)
            rows_to_features()
            body(0, first=True)
            with pe.Fori(1, E - 1) as e:
                body(e)
            body(E - 1, last=True)
            pe.wait_ge(S.cnt_ready, 1)

            with overflow(pe):
                with pe.Fori(0, NOVER) as n:
                    pe.wait_ge(S.o_x, 16 * (n + 1))
                    for k in range(KT):
                        last = nc.tensor.transpose(PS[:, 6 + k // 4, (k % 4) * P:(k % 4 + 1) * P],
                                                   xg[:, k * P:(k + 1) * P], ident)
                    last.then_inc(S.o_t, 1)
                    pe.wait_ge(S.o_tc, 2 * n + 1)
                    pe.wait_ge(S.o_w, 96 * (n + 1))
                    for q in range(4):
                        w = ring[:, q, :].rearrange("p (k n) -> p k n", k=KT)
                        for k in range(KT):
                            last = mm(PS[:, q, :], xgT[:, k, :], w[:, k, :], start=(k == 0), stop=(k == KT - 1))
                    last.then_inc(S.o_gu, 1)
                    pe.wait_ge(S.o_h, 2 * n + 2)
                    for k in range(KT):
                        last = nc.tensor.transpose(PS[:, 6 + k // 4, (k % 4) * P:(k % 4 + 1) * P],
                                                   hm[:, k * P:(k + 1) * P], ident)
                    last.then_inc(S.o_t, 1)
                    pe.wait_ge(S.o_tc, 2 * n + 2)
                    for k in range(KT):
                        w = ring[:, 4 + k // 4, :].rearrange("p (k n) -> p k n", k=4)
                        for c in range(2):
                            last = mm(PS[:, 4 + c, :], hmT[:, k, :], w[:, k % 4, c * CH:(c + 1) * CH],
                                      start=(k == 0), stop=(k == KT - 1))
                    last.then_inc(S.o_d, 1)

            pe.wait_ge(S.moe_ok, 3)
            with overflow(pe):
                pe.wait_ge(S.o_add, 1)
            for b, (t0, nt) in enumerate(BLK):
                if b == 0:
                    pe.wait_ge(S.y_ev, E)
                if b >= 2:
                    pe.wait_ge(S.mt_ev, b - 1)
                q = 4 * (b % 2)
                ps = PS[:, q:q + 2, :].rearrange("p a n -> p (a n)")
                for k in range(KT):
                    last = nc.tensor.transpose(ps[:, k * P:k * P + nt], acc[0:nt, b, k * P:(k + 1) * P], ident[0:nt, 0:nt])
                last.then_inc(S.mt_mm, 1)
            pe.wait_ge(S.mt_ev, 3)

            sum_sq(lt, 3)
            pe.wait_ge(S.h_ok, 3)
            dense(lambda k: wpg[k // 4][:, k % 4, :], {0: (S.wpg_in, 32)}, hT, 8, S.pg_mm, S.pg_ev, 0)
            dense(lambda k: wpl[:, k, :], {0: (S.wpl_in, 32)}, pT, 2, S.pl_mm, S.pl_ev)

        @block.scalar
        def _(act):
            A = nc.scalar.activation

            def root(nth, out, ps, scale):
                act.wait_ge(S.ss_sum, nth)
                return A(out, ps, ACT.Sqrt, bias=eps, scale=scale)

            act.wait_ge(S.cst_in, 16)
            root(1, rstd[:, :], PS[:, 4, 0:T], 1.0 / D).then_inc(S.rms_ok, 1)

            act.wait_ge(S.x_in, 32)
            A(nsp[:, 0, :], feat[:, :, FLAM], ACT.Abs).then_inc(S.act, 1)
            act.wait_ge(S.act, 1)
            A(nsp[:, 0, :], nsp[:, 0, :], ACT.Exp, scale=-1.0).then_inc(S.nsp, 1)
            act.wait_ge(S.nsp, 1)
            A(nsp[:, 1, :], nsp[:, 0, :], ACT.Ln, bias=ones[:, 0:1]).then_inc(S.nsp, 1)

            def evac(n, bank):
                act.wait_ge(S.z_done, n + 1)
                A(Z[:, n, :], PS[:, bank, 0:T], ACT.Copy).then_inc(S.z_evac, 1)

            def shift(g, b):
                n = (WB[g] - 1) // 16 * 16
                act.dma_start(a[f"kvs{g}"][b, 0:n, :].rearrange("(q r) n -> q (r n)", q=16),
                              a[f"cache{g}"][b, 1:n + 1, :].rearrange("(q r) n -> q (r n)", q=16)).then_inc(S.kv_copy, 16)

            def shift_rest(g):
                n = (WB[g] - 1) // 16 * 16
                act.dma_start(a[f"kvs{g}"][:, n:WB[g] - 1, :].rearrange("b r n -> r b n"),
                              a[f"cache{g}"][:, n + 1:WB[g], :].rearrange("b r n -> r b n")).then_inc(S.kv_copy, 16)

            with act.Fori(0, LOOP_A) as i:
                for t in range(4):
                    evac(4 * i + t, t)
                shift(0, i)
                shift(1, i)
            for c in range(13):
                n = min(CH, 24 * T - c * CH)
                act.wait_ge(S.qkn_mm, c + 1)
                A(sq_qk[:, c * CH:c * CH + n], PS[:, 4 + c % 4, 0:n], ACT.Sqrt, bias=eps, scale=1.0 / HD)\
                    .then_inc(S.qkn_ev, 1)
            act.wait_ge(S.h_ok, 1)
            with act.Fori(LOOP_A, NPIECE - 1) as i:
                for t in range(4):
                    evac(4 * i + t, t)
                shift(2, i - LOOP_A)
            for t in range(4):
                evac(4 * (NPIECE - 1) + t, t)
            for g in range(NG):
                shift_rest(g)

            act.wait_ge(S.conv_out, 48)
            for n in range(16):
                j, m = n // 2, n % 2
                act.wait_ge(S.gate_mm, n + 1)
                dst = hT[:, j, :] if m == 0 else Z[:, ZX + j, :]
                c = FBA if m == 0 else FBX
                A(dst, PS[:, n % 8, 0:T], ACT.Sigmoid, bias=feat[:, j, c:c + 1]).then_inc(S.gate_ev, 1)
            act.wait_ge(S.ss_mm, 1)
            A(sct[:, 0:64], PS[:, 4, 0:64], ACT.Copy)
            A(sct[0:64, 64:96], PS[0:64, 4, 64:96], ACT.Copy).then_inc(S.ss_ev, 1)
            n = 0
            for kv in range(2):
                for b, (t0, nt) in enumerate(BLK):
                    direct = kv == 1 and b < 2
                    if not direct and (kv, b) != (0, 0):
                        act.wait_ge(S.tk_out, TK_OUT[b] if kv == 0 else TK_OUT[3])
                    for g in range(NG):
                        act.wait_ge(S.tk_mm, n + 1)
                        dst = vtok[:, b, g * CH:(g + 1) * CH] if direct else stage[0:nt, g * CH:(g + 1) * CH]
                        if n == 0:
                            act.wait_ge(S.roped, 1)
                        A(dst, PS[0:nt, n % 4, :], ACT.Copy).then_inc(S.tk_ev, 1)
                        n += 1
            act.wait_ge(S.z_evac, NZ)
            A(Z[:, ZGR:ZGR + KT, :], Z[:, ZGR:ZGR + KT, :], ACT.Gelu_apprx_tanh).then_inc(S.gelu_z, 1)
            A(Z[:, ZGL:ZGL + 16, :], Z[:, ZGL:ZGL + 16, :], ACT.Sigmoid).then_inc(S.sig_z, 1)
            act.wait_ge(S.sp_exp, 1)
            A(srow[:, 0:323], srow[:, 0:323], ACT.Exp, bias=sm[0:32, 1:2], scale=SCALE, accum_out=sm[0:32, 2:3])\
                .then_inc(S.sp_exp, 1)
            act.wait_ge(S.lru_l, 1)
            A(lt[:, :, :], hT[:, :, :], ACT.Exp, scale=2.0).then_inc(S.lru_e, 1)
            A(xc[:, :, :], hT[:, :, :], ACT.Tanh, scale=-1.0).then_inc(S.lru_th, 1)
            act.wait_ge(S.lru_th, 1)
            A(hT[:, :, :], hT[:, :, :], ACT.Exp).then_inc(S.lru_a, 1)
            act.wait_ge(S.lru_c, 1)
            A(xc[:, :, :], xc[:, :, :], ACT.Sqrt).then_inc(S.lru_s, 1)

            def prompt_exp(it):
                n = 3 * P * (it % 2 + 1)
                act.wait_ge(S.at_nm, it + 1)
                A(sS[:, it % 2, 0:n], sS[:, it % 2, 0:n], ACT.Exp, bias=sm[:, 8 + it:9 + it], scale=SCALE,
                  accum_out=sm[:, 16 + it:17 + it]).then_inc(S.at_e, 1)

            def prompt_out(it):
                n = 3 * P * (it % 2 + 1)
                act.wait_ge(S.at_t, it + 1)
                if it >= 2:
                    act.wait_ge(S.at_pv, it - 1)
                A(sPT[:, it % 2, 0:n], PS[:, 4:6, :].rearrange("p a n -> p (a n)")[:, 0:n], ACT.Copy).then_inc(S.at_pt, 1)

            def prompt_att(it):
                act.wait_ge(S.at_pv, it + 1)
                A(attT[:, it // 2, (it % 2) * P:(it % 2 + 1) * P], PS[:, 6 + it % 2, 0:P], ACT.Copy).then_inc(S.at_ev, 1)

            prompt_exp(0)
            act.wait_ge(S.st_mm, 1)
            A(sptt[:, 0:64], PS[:, 6, 0:64], ACT.Copy)
            A(sptt[0:64, 64:96], PS[0:64, 6, 64:96], ACT.Copy).then_inc(S.st_ev, 1)
            act.wait_ge(S.sb_mm, 1)
            A(prod[:, :], PS[:, 7, 0:96], ACT.Copy).then_inc(S.sb_ev, 1)
            for it in range(8):
                prompt_out(it)
                if it + 1 < 8:
                    prompt_exp(it + 1)
                prompt_att(it)

            root(2, rstd[:, :], PS[:, 4, 0:T], 1.0 / D).then_inc(S.rms_ok, 1)
            for b, (t0, nt) in enumerate(BLK):
                act.wait_ge(S.ht_mm, b + 1)
                if b:
                    act.wait_ge(S.ht_out, 16 * b)
                act.wait_ge(S.bl_ev, KT)
                A(hstage[0:nt, :], PS[:, 6:8, :].rearrange("p a n -> p (a n)")[0:nt, :], ACT.Copy).then_inc(S.ht_ev, 1)
            act.wait_ge(S.rt_exp, 1)
            A(ge[:, :, :], ge[:, :, :], ACT.Exp).then_inc(S.rt_exp, 1)

            def rows_copy(n):
                act.wait_ge(S.x_tr, n)
                A(xgT[:, :, 0:CAP], PS[:, 6, :].rearrange("p (k n) -> p k n", k=KT), ACT.Copy).then_inc(S.xT_ok, 1)

            def body(e, last=False):
                act.wait_ge(S.gmin, e + 1)
                A(ss_, sg, ACT.Sigmoid, scale=ALPHA).then_inc(S.sig, 1)
                if not last:
                    rows_copy(e + 2)
                act.wait_ge(S.h_tr, e + 1)
                A(hmT[:, 0:4, :], PS[:, 7, :].rearrange("p (k n) -> p k n", k=4), ACT.Copy).then_inc(S.hT_ok, 1)

            rows_copy(1)
            with act.Fori(0, E - 1) as e:
                body(e)
            body(E - 1, last=True)

            with overflow(act):
                with act.Fori(0, NOVER) as n:
                    def two_banks(dst, count):
                        act.wait_ge(S.o_t, count)
                        A(dst.rearrange("p k n -> p (k n)"), PS[:, 6:8, :].rearrange("p a n -> p (a n)"), ACT.Copy)\
                            .then_inc(S.o_tc, 1)

                    two_banks(xgT, 2 * n + 1)
                    for h in range(2):
                        act.wait_ge(S.o_g, 2 * n + h + 1)
                        A(ss_, sg, ACT.Sigmoid, scale=ALPHA).then_inc(S.o_sig, 1)
                    two_banks(hmT, 2 * n + 2)

            root(3, rstd[:, :], PS[:, 4, 0:T], 1.0 / D).then_inc(S.rms_ok, 1)
            for m in range(KT):
                act.wait_ge(S.pg_mm, m + 1)
                A(sgp[:, m, :], PS[:, m % 4, 0:T], ACT.Sigmoid).then_inc(S.pg_ev, 1)

        @block.vector
        def _(v):
            TT, TS, STT = nc.vector.tensor_tensor, nc.vector.tensor_scalar, nc.vector.scalar_tensor_tensor
            done = [0]

            def link(ins):
                ins.then_inc(S.dve, 1)
                done[0] = done[0] + 1
                v.wait_ge(S.dve, done[0])

            def normed(nth, x, gcol):
                v.wait_ge(S.rms_ok, nth)
                link(nc.vector.reciprocal(rstd[:, :], rstd[:, :]))
                link(TT(hT[:, :, :], x, fv(gcol), ALU.mult))
                TT(hT[:, :, :], hT[:, :, :], over_tiles(rstd[:, :]), ALU.mult).then_inc(S.h_ok, 1)

            x0 = Z[:, ZGL:ZGL + KT, :]
            v.wait_ge(S.x_in, 32)
            TT(hT[:, :, :], x0, x0, ALU.mult).then_inc(S.sq_ok, 1)
            v.wait_ge(S.ss_sum, 1)
            normed(1, x0, FGM)

            v.wait_ge(S.z_evac, 24)
            TT(sq_qk, Zb[:, 0:24 * T], Zb[:, 0:24 * T], ALU.mult).then_inc(S.sq_qk, 1)
            v.wait_ge(S.z_evac, ZX + KT)
            X = Z[:, ZX:ZX + KT, :]
            link(TT(xc[:, :, :], X, fv(FW + 3), ALU.mult))
            link(TT(xc[:, :, :], xc[:, :, :], fv(FCB), ALU.add))
            for back in (1, 2, 3):
                w = feat[:, :, FW + 3 - back:FW + 4 - back]
                n = NP - back
                link(TT(lt[:, :, 0:n], X[:, :, 0:n], w.to_broadcast([P, KT, n]), ALU.mult))
                link(TT(lt[:, :, NP:T], feat[:, :, FSC + (3 - back) * NS:FSC + (4 - back) * NS],
                        w.to_broadcast([P, KT, NS]), ALU.mult))
                link(TT(xc[:, :, back:NP], xc[:, :, back:NP], lt[:, :, 0:n], ALU.add))
                ins = TT(xc[:, :, NP:T], xc[:, :, NP:T], lt[:, :, NP:T], ALU.add)
                if back < 3:
                    link(ins)
            ins.then_inc(S.conv_done, 1)
            v.wait_ge(S.conv_done, 1)

            v.wait_ge(S.qkn_ev, 13)
            v.wait_ge(S.rope_in, 32)
            link(nc.vector.reciprocal(sq_qk, sq_qk))
            for m in range(2):
                zz = Zb[:, m * 12 * T:(m + 1) * 12 * T]
                ins = STT(zz, zz, gqk[:, m:m + 1], sq_qk[:, m * 12 * T:(m + 1) * 12 * T], ALU.mult, ALU.mult)
                if m == 0:
                    link(ins)
            ins.then_inc(S.qk_normed, 1)
            v.wait_ge(S.qk_normed, 1)
            v.wait_ge(S.rot_in, 32)
            zr = Z[0:32, 0:24, :]
            link(TT(rot, rot, over_tiles(rope[:, 1, :], 24), ALU.mult))
            link(TT(zr, zr, over_tiles(rope[:, 0, :], 24), ALU.mult))
            TT(zr, zr, rot, ALU.add).then_inc(S.roped, 1)
            v.wait_ge(S.roped, 1)
            TT(prod[:, :].rearrange("p (g b h) -> p g b h", g=NG, b=NS),
               Z[:, ZQ:ZQ + NHEAD, NP:T].rearrange("p (g h) b -> p g b h", g=NG),
               Z[:, ZK:ZK + NHEAD, NP:T].rearrange("p (g h) b -> p g b h", g=NG), ALU.mult).then_inc(S.ss_prod, 1)

            lam = feat[:, :, FLAM]
            v.wait_ge(S.nsp, 2)
            link(TS(nsp[:, 2, :], nsp[:, 0, :], 1.0, -1.0, ALU.add, ALU.add))
            link(TS(nsp[:, 3, :], nsp[:, 2, :], 1e-30, None, ALU.max))
            link(nc.vector.reciprocal(nsp[:, 3, :], nsp[:, 3, :]))
            link(TT(nsp[:, 1, :], nsp[:, 1, :], nsp[:, 3, :], ALU.mult))
            link(TS(nsp[:, 4, :], nsp[:, 2, :], 0.0, None, ALU.is_equal))
            link(TT(nsp[:, 1, :], nsp[:, 1, :], nsp[:, 4, :], ALU.add))
            link(TT(nsp[:, 1, :], nsp[:, 1, :], nsp[:, 0, :], ALU.mult))
            link(TS(nsp[:, 5, :], lam, -1.0, 0.0, ALU.mult, ALU.max))
            link(TT(nsp[:, 1, :], nsp[:, 1, :], nsp[:, 5, :], ALU.add))
            link(TS(nsp[:, 1, :], nsp[:, 1, :], -LRU_C, None, ALU.mult))
            v.wait_ge(S.gate_ev, 16)
            TT(hT[:, :, :], hT[:, :, :], nsp[:, 1, :].unsqueeze(2).to_broadcast([P, KT, T]), ALU.mult)\
                .then_inc(S.lru_l, 1)
            link(TT(X, X, xc[:, :, :], ALU.mult))

            v.wait_ge(S.ss_rows, 1)
            link(nc.vector.tensor_copy(srow[:, 0:323], PS[0:32, 5, 0:323]))
            link(nc.vector.tensor_reduce(sm[0:32, 0:1], srow[:, 0:323], AX, ALU.max))
            TS(sm[0:32, 1:2], sm[0:32, 0:1], -SCALE, None, ALU.mult).then_inc(S.sp_exp, 1)
            v.wait_ge(S.sp_exp, 2)
            link(nc.vector.reciprocal(sm[0:32, 3:4], sm[0:32, 2:3]))
            TS(srow[:, 0:323], srow[:, 0:323], sm[0:32, 3:4], None, ALU.mult).then_inc(S.sp_ready, 1)
            v.wait_ge(S.sp_ready, 1)
            for g in range(NG):
                ins = TS(sdiag[:, g, :], ident[0:32, 0:32], srow[:, 320 + g:321 + g], None, ALU.mult)
            ins.then_inc(S.sd_ready, 1)

            def mask_max(it):
                h, qb = it // 2, it % 2
                n = 3 * P * (qb + 1)
                m = cst[:, C_MASK1:C_MASK1 + n] if qb else cst[:, C_MASK0:C_MASK0 + n]
                v.wait_ge(S.at_sc, it + 1)
                if it >= 2:
                    v.wait_ge(S.at_t, it - 1)
                ps = PS[:, 2 * (it % 2):2 * (it % 2) + 2, :].rearrange("p a n -> p (a n)")[:, 0:n]
                TT(sS[:, it % 2, 0:n], ps, m, ALU.add).then_inc(S.at_s, 1)
                v.wait_ge(S.at_s, it + 1)
                link(nc.vector.tensor_reduce(sm[:, 24:25], sS[:, it % 2, 0:n], AX, ALU.max))
                TS(sm[:, 8 + it:9 + it], sm[:, 24:25], -SCALE, None, ALU.mult).then_inc(S.at_nm, 1)

            def divide(it):
                n = 3 * P * (it % 2 + 1)
                v.wait_ge(S.at_e, it + 1)
                link(nc.vector.reciprocal(sm[:, 25:26], sm[:, 16 + it:17 + it]))
                TS(sS[:, it % 2, 0:n], sS[:, it % 2, 0:n], sm[:, 25:26], None, ALU.mult).then_inc(S.at_p, 1)

            mask_max(0)
            v.wait_ge(S.lru_th, 1)
            v.wait_ge(S.lru_e, 1)
            STT(xc[:, :, :], lt[:, :, :], 1.0, xc[:, :, :], ALU.add, ALU.mult).then_inc(S.lru_c, 1)
            divide(0)
            mask_max(1)
            v.wait_ge(S.lru_s, 1)
            link(TT(X, X, xc[:, :, :], ALU.mult))
            v.wait_ge(S.lru_a, 1)
            for j in range(KT):
                nc.vector.tensor_tensor_scan(lt[:, j, 0:NP], hT[:, j, 0:NP], X[:, j, 0:NP], 0.0, ALU.mult, ALU.add)
            link(TT(lt[:, :, NP:T], hT[:, :, NP:T], feat[:, :, FSH:FSH + NS], ALU.mult))
            TT(lt[:, :, NP:T], lt[:, :, NP:T], X[:, :, NP:T], ALU.add).then_inc(S.lru_y, 1)
            v.wait_ge(S.gelu_z, 1)
            v.wait_ge(S.lru_y, 1)
            TT(Z[:, ZGR:ZGR + KT, :], Z[:, ZGR:ZGR + KT, :], lt[:, :, :], ALU.mult).then_inc(S.lru_yg, 1)
            for it in range(1, 8):
                divide(it)
                if it + 1 < 8:
                    mask_max(it + 1)
            v.wait_ge(S.sb_ev, 1)
            link(TT(prod[:, :].rearrange("p (g b h) -> p g b h", g=NG, b=NS),
                    prod[:, :].rearrange("p (g b h) -> p g b h", g=NG, b=NS),
                    Z[:, ZV:ZV + NHEAD, NP:T].rearrange("p (g h) b -> p g b h", g=NG), ALU.mult))
            link(TT(prod[:, 0:32], prod[:, 0:32], prod[:, 32:64], ALU.add))
            link(TT(prod[:, 0:32], prod[:, 0:32], prod[:, 64:96], ALU.add))
            v.wait_ge(S.spv_mm, 1)
            TT(attT[:, :, NP:T], PS[:, 0, 0:32].rearrange("p (b h) -> p h b", b=NS),
               prod[:, 0:32].rearrange("p (b h) -> p h b", b=NS), ALU.add).then_inc(S.satt, 1)

            v.wait_ge(S.sig_z, 1)
            for m in range(KT):
                v.wait_ge(S.ba_mm, m + 1)
                TT(Z[:, ZGA + m, :], Z[:, ZGA + m, :], PS[:, 4 + m % 4, 0:T], ALU.mult).then_inc(S.ba_ev, 1)
            for m in range(KT):
                v.wait_ge(S.bl_mm, m + 1)
                TT(Z[:, ZGL + m, :], Z[:, ZGL + m, :], PS[:, m % 4, 0:T], ALU.mult).then_inc(S.bl_ev, 1)
            v.wait_ge(S.bl_ev, KT)
            v.wait_ge(S.ba_ev, KT)
            TT(hT[:, :, :], Z[:, ZGL:ZGL + KT, :], Z[:, ZGA:ZGA + KT, :], ALU.add).then_inc(S.merged, 1)
            v.wait_ge(S.res_in, 16)
            for m in range(KT):
                v.wait_ge(S.wo_mm, m + 1)
                TT(xc[:, m, :], xc[:, m, :], PS[:, 4 + m % 4, 0:T], ALU.add).then_inc(S.wo_ev, 1)
            v.wait_ge(S.wo_ev, KT)
            v.wait_ge(S.h_out, 32)
            TT(lt[:, :, :], xc[:, :, :], xc[:, :, :], ALU.mult).then_inc(S.sq_ok, 1)
            v.wait_ge(S.wo_mm, KT)
            normed(2, xc[:, :, :], FGF)

            link(nc.vector.memset(logit[:, 2, :], 0.0))
            v.wait_ge(S.lg_mm, 1)
            link(nc.vector.tensor_copy(logit[:, 0:2, :].rearrange("p a n -> p (a n)"), PS[:, 0, 0:2 * E]))
            link(nc.vector.tensor_copy(logit[0:NS, 2, :], PS[0:NS, 0, 2 * E:3 * E]))
            for b in range(3):
                link(nc.vector.max(mx[:, b, :], logit[:, b, :]))
                link(nc.vector.max_index(mxi[:, b, :], mx[:, b, :], logit[:, b, :]))
            link(nc.vector.tensor_copy(mif[:, :, :], mxi[:, :, :]))
            TT(ge[:, :, :], mx[:, :, 0:TOPK], mx[:, :, 0:1].to_broadcast([P, 3, TOPK]), ALU.subtract).then_inc(S.rt_exp, 1)
            iota = cst[:, C_IOTA:C_IOTA + E].unsqueeze(1).to_broadcast([P, 3, E])
            valid = cst[:, C_VALID:C_VALID + 3].unsqueeze(2).to_broadcast([P, 3, E])
            for k in range(TOPK):
                link(TT(oh[k], iota, mif[:, :, k:k + 1].to_broadcast([P, 3, E]), ALU.is_equal))
                link(TT(oh[k], oh[k], valid, ALU.mult))
            link(TT(route, oh[0], oh[1], ALU.add))
            link(TT(rtmp, oh[2], oh[3], ALU.add))
            TT(route, route, rtmp, ALU.add).then_inc(S.oh_ready, 1)
            v.wait_ge(S.rk_mm, 1)
            iota3 = cst[:, C_IOTA:C_IOTA + E].unsqueeze(1).to_broadcast([P, 3, E])
            eoff3 = cst[:, C_EOFF:C_EOFF + E].unsqueeze(1).to_broadcast([P, 3, E])
            rank = PS[:, 1, 0:3 * E].rearrange("p (b e) -> p b e", b=3)
            link(TS(rtmp, rank, float(CAP), None, ALU.is_ge))
            link(TS(rrow, rank, float(CAP + P), None, ALU.is_ge))
            link(STT(rslot, rtmp, -float(CAP), rank, ALU.mult, ALU.add))
            link(STT(rslot, rrow, -float(P), rslot, ALU.mult, ALU.add))
            link(STT(rtab, rrow, 1.0, rtmp, ALU.mult, ALU.add))
            link(STT(rtab, rslot, float(NCHUNK), rtab, ALU.mult, ALU.add))
            link(TS(rtab, rtab, float(E), None, ALU.mult))
            link(TT(rtab, rtab, iota3, ALU.add))

            def chosen(src, dst):
                for k in range(TOPK):
                    link(TT(rsel, src, oh[k], ALU.mult))
                    link(nc.vector.tensor_reduce(dst[:, :, k], rsel, AX, ALU.add))

            chosen(rtab, dtab)
            link(nc.vector.tensor_reduce(cmax, PS[0:1, 1, 3 * E:4 * E], AX, ALU.max))
            link(nc.vector.tensor_copy(tokid, cst[:, C_TOK:C_TOK + 3]))
            link(nc.vector.tensor_copy(itab, dtab.rearrange("p a n -> p (a n)")))
            nc.vector.tensor_copy(most, cmax).then_inc(S.rt_ready, 1)
            link(STT(rrow, rrow, float(E * P), rslot, ALU.mult, ALU.add))
            link(STT(rrow, rtmp, float(E * CAP), rrow, ALU.mult, ALU.add))
            link(TT(rtmp, rtmp, eoff3, ALU.mult))
            link(TT(rrow, rrow, rtmp, ALU.add))
            link(TT(rrow, rrow, eoff3, ALU.add))
            chosen(rrow, drow)
            link(TS(over, drow, float(E * CAP), None, ALU.is_ge))
            link(STT(drow, over, -float(E * CAP), drow, ALU.mult, ALU.add))
            link(TT(drow2, drow, over, ALU.mult))
            link(TT(drow, drow, drow2, ALU.subtract))
            link(nc.vector.tensor_copy(irow, drow.rearrange("p a n -> p (a n)")))
            link(nc.vector.tensor_copy(irow2, drow2.rearrange("p a n -> p (a n)")))
            v.wait_ge(S.rt_exp, 2)
            link(nc.vector.tensor_reduce(gs, ge, AX, ALU.add))
            link(nc.vector.reciprocal(gs, gs))
            link(TT(ge, ge, gs.unsqueeze(2).to_broadcast([P, 3, TOPK]), ALU.mult))
            link(TT(ge2, ge, over, ALU.mult))
            TT(ge, ge, ge2, ALU.subtract).then_inc(S.cnt_ready, 1)

            def swiglu(e, first=False):
                if not first:
                    v.wait_ge(S.hid_ok, e)
                v.wait_ge(S.g_mm, e + 1)
                TS(sg, PS[:, 0, :], LIMIT, None, ALU.min).then_inc(S.gmin, 1)
                v.wait_ge(S.sig, e + 1)
                TT(sg, sg, ss_, ALU.mult).then_inc(S.gated, 1)
                v.wait_ge(S.u_mm, e + 1)
                TS(su, PS[:, 1, :], LIMIT, -LIMIT, ALU.min, ALU.max).then_inc(S.u_rd, 1)
                v.wait_ge(S.gated, e + 1)
                v.wait_ge(S.u_rd, e + 1)
                if not first:
                    v.wait_ge(S.h_tr, e)
                STT(hm[:, 0:CH], su, 1.0, sg, ALU.add, ALU.mult).then_inc(S.hid_ok, 1)

            def result(e, first=False):
                v.wait_ge(S.d1_mm, e + 1)
                if not first:
                    v.wait_ge(S.y_out, 32 * e)
                nc.vector.tensor_copy(yb[:, 0:CH], PS[:, 4, :]).then_inc(S.y_ev, 1)

            swiglu(0, first=True)
            result(0, first=True)
            with v.Fori(1, E) as e:
                swiglu(e)
                result(e)

            with overflow(v):
                v.wait_ge(S.y_ev, E)
                v.wait_ge(S.hid_ok, E)
                TS(sm[:, 26:27], ones[:, 0:1], 0.0, None, ALU.mult).then_inc(S.o_y, 1)
                with v.Fori(0, NOVER) as n:
                    olinks = [0]

                    def olink(ins):
                        ins.then_inc(S.o_dve, 1)
                        olinks[0] += 1
                        v.wait_ge(S.o_dve, 8 * n + olinks[0])

                    v.wait_ge(S.o_bc, 3 * (n + 1))
                    v.wait_ge(S.o_gu, n + 1)
                    for h, bias in enumerate((bg0, bg1)):
                        olink(TT(sg, PS[:, 2 * h, :], bias[:, 0, :], ALU.add))
                        TS(sg, sg, LIMIT, None, ALU.min).then_inc(S.o_g, 1)
                        olink(TT(su, PS[:, 2 * h + 1, :], bias[:, 1, :], ALU.add))
                        olink(TS(su, su, LIMIT, -LIMIT, ALU.min, ALU.max))
                        v.wait_ge(S.o_sig, 2 * n + h + 1)
                        olink(TT(sg, sg, ss_, ALU.mult))
                        ins = STT(hm[:, h * CH:(h + 1) * CH], su, 1.0, sg, ALU.add, ALU.mult)
                        ins.then_inc(S.o_h, 1)
                        v.wait_ge(S.o_h, 2 * n + h + 1)
                    v.wait_ge(S.o_d, n + 1)
                    TT(yb, PS[:, 4:6, :].rearrange("p a n -> p (a n)"), bd, ALU.add).then_inc(S.o_y, 1)

            for b in range(3):
                nt = BLK[b][1]
                v.wait_ge((S.yk0_in, S.yk1_in, S.yk2_in)[b], 16 * TOPK)
                for k in range(TOPK):
                    src = yk[0:nt, b * TOPK + k, :]
                    if k == 0:
                        link(TS(acc[0:nt, b, :], src, ge[0:nt, b, 0:1], None, ALU.mult))
                    else:
                        ins = STT(acc[0:nt, b, :], src, ge[0:nt, b, k:k + 1], acc[0:nt, b, :], ALU.mult, ALU.add)
                        if k < TOPK - 1:
                            link(ins)
                ins.then_inc(S.moe_ok, 1)
            with overflow(v):
                v.wait_ge(S.moe_ok, 3)
                v.wait_ge(S.o_yk, 16 * 3 * TOPK)
                start = 8 * NOVER
                for b in range(3):
                    nt = BLK[b][1]
                    for k in range(TOPK):
                        ins = STT(acc[0:nt, b, :], yk[0:nt, b * TOPK + k, :], ge2[0:nt, b, k:k + 1], acc[0:nt, b, :],
                                  ALU.mult, ALU.add)
                        if b < 2 or k < TOPK - 1:
                            start += 1
                            ins.then_inc(S.o_dve, 1)
                            v.wait_ge(S.o_dve, start)
                ins.then_inc(S.o_add, 1)
            for b, (t0, nt) in enumerate(BLK):
                v.wait_ge(S.mt_mm, b + 1)
                q = 4 * (b % 2)
                ps = PS[:, q:q + 2, :].rearrange("p a n -> p (a n)").rearrange("p (k n) -> p k n", k=KT)[:, :, 0:nt]
                TT(xc[:, :, t0:t0 + nt], xc[:, :, t0:t0 + nt], ps, ALU.add).then_inc(S.mt_ev, 1)
            v.wait_ge(S.mt_ev, 3)
            TT(lt[:, :, :], xc[:, :, :], xc[:, :, :], ALU.mult).then_inc(S.sq_ok, 1)
            normed(3, xc[:, :, :], FGP)
            for m in range(KT):
                v.wait_ge(S.pg_ev, m + 1)
                v.wait_ge(S.pl_mm, m + 1)
                TT(sgp[:, m, :], sgp[:, m, :], PS[:, 4 + m % 4, 0:T], ALU.mult).then_inc(S.pl_ev, 1)
            v.wait_ge(S.pl_ev, KT)
            TT(sgp, sgp, xc[:, :, :], ALU.add).then_inc(S.y_ok, 1)

        @block.gpsimd
        def _(po):
            po.dma_start(tabd, a["zeros"]).then_inc(S.tab_z, 16)
            po.wait_ge(S.z_evac, ZX + KT)
            po.wait_ge(S.x_in, 32)
            po.dma_start(a["convp"], Z[:, ZX:ZX + KT, NP - 3:NP]).then_inc(S.conv_out, 16)
            po.dma_start(a["convs"][:, :, 0:2 * NS], feat[:, :, FSC + NS:FSC + 3 * NS]).then_inc(S.conv_out, 16)
            po.dma_start(a["convs"][:, :, 2 * NS:3 * NS], Z[:, ZX:ZX + KT, NP:T]).then_inc(S.conv_out, 16)
            po.wait_ge(S.qk_normed, 1)
            po.dma_start(rot[0:16, :, :], Z[16:32, 0:24, :]).then_inc(S.rot_in, 16)
            po.dma_start(rot[16:32, :, :], Z[0:16, 0:24, :]).then_inc(S.rot_in, 16)
            for kv in range(2):
                for b, (t0, nt) in enumerate(BLK):
                    direct = kv == 1 and b < 2
                    po.wait_ge(S.tk_ev, 9 * kv + 3 * b + 3)
                    for g in range(NG):
                        src = vtok[:, b % 2, g * CH:(g + 1) * CH] if direct else stage[0:nt, g * CH:(g + 1) * CH]
                        if b == 2:
                            dst = a[f"kvs{g}"][:, WB[g] - 1, kv * CH:(kv + 1) * CH]
                        elif g == 0:
                            if b == 0:
                                continue
                            dst = a["kvp0"][:, kv * CH:(kv + 1) * CH]
                        else:
                            dst = a[f"kvp{g}"][t0:t0 + nt, kv * CH:(kv + 1) * CH]
                        po.dma_start(dst, src).then_inc(S.vt_out if direct else S.tk_out, 16)
            po.wait_ge(S.lru_y, 1)
            po.dma_start(a["hp"], lt[:, :, NP - 1:NP], allow_slow_non_contiguous=True).then_inc(S.h_out, 16)
            po.dma_start(a["hs"], lt[:, :, NP:T]).then_inc(S.h_out, 16)
            po.wait_ge(S.lru_yg, 1)
            po.dma_start(xc[:, :, :], a["xT"]).then_inc(S.res_in, 16)
            for b, (t0, nt) in enumerate(BLK):
                po.wait_ge(S.ht_ev, b + 1)
                po.dma_start(hrow[t0:t0 + nt, :], hstage[0:nt, :]).then_inc(S.ht_out, 16)
            po.wait_ge(S.rt_ready, 1)
            po.wait_ge(S.tab_z, 16)
            for b, (t0, nt) in enumerate(BLK):
                for k in range(TOPK):
                    c = b * TOPK + k
                    po.indirect_dma_start(tabd.rearrange("p (n o) -> (p n) o", o=1),
                                          bass.IndirectOffsetOnAxis(ap=itab[0:nt, c:c + 1], axis=0),
                                          tokid[0:nt, b:b + 1], None).then_inc(S.tab_put, 16)
            po.wait_ge(S.tab_put, 16 * 3 * TOPK)
            po.dma_start(tab, tabd).then_inc(S.tab_in, 16)
            po.wait_ge(S.tab_in, 16)
            po.wait_ge(S.ht_out, 48)

            carriers = iter(range(64))

            def held(sem, n):
                po.wait_ge(sem, n)
                if not isinstance(n, int):
                    c = next(carriers)
                    one = cst[0:1, C_ONE:C_ONE + 1]
                    nc.gpsimd.tensor_tensor(carried[:, c:c + 1], one, one, op=ALU.add)

            def gather(e, done):
                if done is not None:
                    held(S.xg_in, 16 * done)
                nc.gpsimd.tensor_copy(idxc[0:CAP], tab[0:CAP, e:e + 1] if isinstance(e, int) else tab[0:CAP, bass.ds(e, 1)])\
                    .then_inc(S.idx_ok, 1)
                held(S.idx_ok, e + 1)
                po.indirect_dma_start(xg[0:CAP], None, hrow, bass.IndirectOffsetOnAxis(ap=idxc[0:CAP], axis=0)).then_inc(S.xg_in, 16)

            def store(e):
                held(S.y_ev, e + 1)
                for h in range(2):
                    at = slice(e * CAP, (e + 1) * CAP) if isinstance(e, int) else bass.ds(e * CAP, CAP)
                    po.dma_start(yrow[at, h * CH:(h + 1) * CH], yb[CAP * h:CAP * (h + 1), 0:CH]).then_inc(S.y_out, 16)

            def spread(dst, at, n, sem):
                nc.gpsimd.partition_broadcast(dst, brow[:, at:at + n]).then_inc(sem, 1)

            def flat(v):
                return v.rearrange("p a n -> p (a n)")

            def step(e, rows=True):
                held(S.bias_used, e + 1)
                po.dma_start(brow, a["bcat"][e + 1]).then_inc(S.brow_in, 16)
                if rows:
                    held(S.x_tr, e + 2)
                    gather(e + 2, e + 2)
                store(e)

            gather(0, None)
            po.dma_start(brow, a["bcat"][0]).then_inc(S.brow_in, 16)
            held(S.x_tr, 1)
            gather(1, 1)
            with po.Fori(0, E - 2) as e:
                step(e)
            step(E - 2, rows=False)
            store(E - 1)
            held(S.y_out, 32 * E)
            held(S.cnt_ready, 1)
            with overflow(po):
                for c in range(NCHUNK - 1):
                    with po.Fori(0, E) as e:
                        n = e + c * E
                        held(S.o_y, n + 1)
                        nc.gpsimd.tensor_copy(idxc, tab[:, bass.ds(n + E, 1)]).then_inc(S.o_idx, 1)
                        held(S.o_idx, n + 1)
                        po.indirect_dma_start(xg, None, hrow, bass.IndirectOffsetOnAxis(ap=idxc, axis=0)).then_inc(S.o_x, 16)
                        po.dma_start(brow, a["bcat"][e]).then_inc(S.o_b, 16)
                        held(S.o_b, 16 * (n + 1))
                        spread(flat(bg0), 0, D, S.o_bc)
                        spread(flat(bg1), D, D, S.o_bc)
                        spread(bd, 2 * D, D, S.o_bc)
                        held(S.o_x, 16 * (n + 1))
                        held(S.o_y, n + 2)
                        po.dma_start(yrow2[bass.ds(n * P, P), :], yb).then_inc(S.o_st, 16)
                        held(S.o_st, 16 * (n + 1))
            for b, (t0, nt) in enumerate(BLK):
                for k in range(TOPK):
                    c = b * TOPK + k
                    po.indirect_dma_start(yk[0:nt, c, :], None, yrow,
                                          bass.IndirectOffsetOnAxis(ap=irow[0:nt, c:c + 1], axis=0)).then_inc((S.yk0_in, S.yk1_in, S.yk2_in)[b], 16)
            with overflow(po):
                held(S.moe_ok, 3)
                for b, (t0, nt) in enumerate(BLK):
                    for k in range(TOPK):
                        c = b * TOPK + k
                        po.indirect_dma_start(yk[0:nt, c, :], None, yrow2,
                                              bass.IndirectOffsetOnAxis(ap=irow2[0:nt, c:c + 1], axis=0)).then_inc(S.o_yk, 16)


_OUTS = [("yT", (P, KT, T)), ("kvp0", (1, 1, 128, 2, HPG, HD)), ("kvp1", (1, 1, NP, 2, HPG, HD)),
         ("kvp2", (1, 1, NP, 2, HPG, HD)), ("convp", (P, KT, 3)), ("hp", (P, KT, 1)),
         ("kvs0", (1, NS, WB[0], 2, HPG, HD)), ("kvs1", (1, NS, WB[1], 2, HPG, HD)),
         ("kvs2", (1, NS, WB[2], 2, HPG, HD)), ("convs", (P, KT, 3 * NS)), ("hs", (P, KT, NS))]


def constants():
    import numpy as np
    c = np.zeros((P, NCST), np.float32)
    p = np.arange(P)
    c[:, C_ID:C_ID + P] = np.eye(P)
    c[:, C_ONE:C_ONE + P] = 1
    c[:, C_TRI:C_TRI + P] = p[:, None] < p[None, :]
    for qb, at in ((0, C_MASK0), (1, C_MASK1)):
        n = P * (qb + 1)
        rel = (qb * P + p)[:, None] - np.arange(n)[None, :]
        for g in range(NG):
            ok = (rel >= 0) & (rel % DIL[g] == 0) & (rel <= (128, 512, 2048)[g])
            c[:, at + g * n:at + (g + 1) * n] = np.where(ok, 0, -1e30)
    c[:, C_IOTA:C_IOTA + E] = np.arange(E)
    c[:, C_EOFF:C_EOFF + E] = np.arange(E) * CAP
    for b, (t0, nt) in enumerate(BLK):
        c[:, C_TOK + b] = t0 + p
        c[:, C_VALID + b] = p < nt
    c[:, C_EPS] = 1e-6
    half = HD // 8
    freqs = np.float32(500000.0) ** (-np.arange(half, dtype=np.float32) * np.float32(2.0 / (2 * half)))
    where = np.concatenate([np.arange(NP), np.full(NS, 1024)]).astype(np.float32)
    ang = (where[None, :] * freqs.astype(np.float32)[:, None]).astype(np.float32).astype(np.float64)
    cos, sin = np.cos(ang), np.sin(ang)
    rope = np.stack([np.concatenate([cos, cos]), np.concatenate([-sin, sin])], 1).astype(np.float32)
    return c, np.ascontiguousarray(rope)


def layout(i):
    import numpy as np
    i = {k: np.asarray(v) for k, v in i.items()}
    cst, rope = constants()

    def cols(v):
        v = np.moveaxis(v.reshape(-1, KT, P), 0, -1)
        return np.ascontiguousarray(v.transpose(1, 0, 2))

    order = [4, 5, 6, 7, 8, 9, 0, 1, 2, 3, 10, 11, 12, 13, 14, 15, 16]
    win = i["w_in"][0].reshape(KT, P, NPIECE, CH).transpose(2, 1, 0, 3)[order]
    sc = i["state_conv"][0].transpose(1, 0, 2).reshape(3 * NS, D)
    feat = np.concatenate([i["conv_w"][0], i["conv_b"], i["b_rg_a"], i["b_rg_x"], i["lru_lambda"], i["g_mix"],
                           i["g_ffn"], i["g_ple"], sc, i["state_h"][0]], 0)
    wrg = np.stack([i["w_rg_a"][0], i["w_rg_x"][0]]).reshape(2, 4, 2, P, 256).transpose(3, 0, 1, 2, 4)
    out = dict(
        cst=cst, rope=rope, zeros=np.zeros((P, NCHUNK * E), np.int32), feat=cols(feat),
        xT=cols(np.concatenate([i["x_prompt"][0], i["x_sample"][:, 0]], 0)),
        win=np.ascontiguousarray(win), gqk=np.ascontiguousarray(np.concatenate([i["g_q"], i["g_k"]], 0).T),
        wrg=np.ascontiguousarray(wrg.reshape(P, 4096)),
        w_router=i["w_router"][0], b_router=i["b_router"], w_br_lru=i["w_br_lru"][0], w_br_att=i["w_br_att"][0],
        w_out=i["w_out"][0], w_gu=i["w_gu"][0], w_down=i["w_down"][0], w_ple_gate=i["w_ple_gate"][0],
        w_ple=i["w_ple"][0])
    for g in range(NG):
        c = i[f"cache_kv_g{g}"][0]
        out[f"cache{g}"] = c.reshape(NS, WB[g], 2 * CH)
        out[f"kt{g}"] = np.ascontiguousarray(c[:, ::DIL[g], 0].transpose(3, 0, 2, 1)).reshape(P, -1)
    pp = np.concatenate([i["p_prompt"][0, 0], i["p_sample"][0, :, 0]], 0)
    out["pT"] = np.ascontiguousarray(pp.reshape(T, 2, P).transpose(2, 1, 0))
    b = i["b_gu"][0].reshape(E, 2, 2, CH).transpose(0, 2, 1, 3).reshape(E, 2 * D)
    out["bcat"] = np.concatenate([b, i["b_down"][0]], 1).reshape(E, 1, 3 * D)
    return out


def program(nc, arrays):
    a = {}
    for n, v in arrays.items():
        a[n] = nc.dram_tensor("in_" + n, v.shape, mybir.dt.from_np(v.dtype), kind="ExternalInput").ap()
    for n, s in _OUTS:
        ap = nc.dram_tensor("out_" + n, s, F32, kind="ExternalOutput").ap()
        if n.startswith("kvp"):
            ap = ap.rearrange("l o s c h d -> (l o s) (c h d)")
        elif n.startswith("kvs"):
            ap = ap.rearrange("l b s c h d -> (l b) s (c h d)")
        a[n] = ap
    for g in range(NG):
        n = SKEYS[g]
        a[f"kt{g}"] = a[f"kt{g}"].rearrange("p (s k) -> p s k", k=n)
    build(nc, a)


def kernel(**inputs):
    import numpy as np
    import concourse.bacc as bacc
    from concourse.bass_utils import run_bass_kernel_spmd

    arrays = layout(inputs)
    nc = bacc.Bacc("TRN2", target_bir_lowering=False, num_devices=1)
    program(nc, arrays)
    r = run_bass_kernel_spmd(nc, [{"in_" + n: v for n, v in arrays.items()}], core_ids=[0])
    return assemble({n: r.results[0]["out_" + n] for n, _ in _OUTS})


def assemble(o):
    import numpy as np

    def rows(v):
        return np.ascontiguousarray(v.transpose(2, 1, 0)).reshape(v.shape[2], D)

    y = rows(o["yT"])
    convs = rows(o["convs"]).reshape(3, NS, D).transpose(1, 0, 2)
    return (y[None, 0:NP], y[NP:T, None], o["kvp0"], o["kvp1"], o["kvp2"], rows(o["convp"])[None, None],
            rows(o["hp"])[None], o["kvs0"], o["kvs1"], o["kvs2"], np.ascontiguousarray(convs)[None],
            rows(o["hs"])[None])
```

```python
from contextlib import ExitStack

import concourse.bass as bass
from concourse import mybir

P = 128
D = 1024
KT = D // P
NP, NS = 256, 8
T = NP + NS
BLK = [(0, P), (P, P), (NP, NS)]
HD = 128
HPG = 4
NG = 3
NHEAD = NG * HPG
WB = (128, 512, 1024)
DIL = (1, 4, 16)
SKEYS = tuple(w // d for w, d in zip(WB, DIL))
E = 32
TOPK = 4
CAP = 64
NCHUNK = -(-T // CAP)
CH = 512
NPIECE = 17
LOOP_A = 8
EARLY = 6
KV_STORES = 8
SCALE = HD ** -0.5
LIMIT, ALPHA, LRU_C = 7.0, 1.702, 8.0
ZQ, ZK, ZX, ZGR, ZV, ZGL, ZGA, NZ = 0, 12, 24, 32, 40, 52, 60, 68
FW, FCB, FBA, FBX, FLAM, FGM, FGF, FGP, FSC, FSH, NFEAT = 0, 4, 5, 6, 7, 8, 9, 10, 11, 35, 43
C_ID, C_ONE, C_TRI, C_MASK0, C_MASK1 = 0, P, 2 * P, 3 * P, 6 * P
C_IOTA = 12 * P
C_VALID = C_IOTA + CAP
C_EPS = C_VALID + 3
NCST = C_EPS + 1

ALU = mybir.AluOpType
ACT = mybir.ActivationFunctionType
AX = mybir.AxisListType.X
F32 = mybir.dt.float32
I32 = mybir.dt.int32
U32 = mybir.dt.uint32


class Signals:

    def __init__(self, sem):
        self.sq_ok = sem("sq_ok")
        self.sq_tile = sem("sq_tile")
        self.ss_sum = sem("ss_sum")
        self.rms_ok = sem("rms_ok")
        self.h_ok = sem("h_ok")
        self.xgain = sem("xgain")
        self.v_in = sem("v_in")
        self.cst_in = sem("cst_in")
        self.x_in = sem("x_in")
        self.rope_in = sem("rope_in")
        self.win0 = sem("win0")
        self.win1 = sem("win1")
        self.win2 = sem("win2")
        self.win3 = sem("win3")
        self.z_done = sem("z_done")
        self.z_evac = sem("z_evac")
        self.sq_qk = sem("sq_qk")
        self.qkn_mm = sem("qkn_mm")
        self.qkn_ev = sem("qkn_ev")
        self.qk_normed = sem("qk_normed")
        self.rot_in = sem("rot_in")
        self.roped = sem("roped")
        self.conv_done = sem("conv_done")
        self.conv_out = sem("conv_out")
        self.wrg_in = sem("wrg_in")
        self.gate_mm = sem("gate_mm")
        self.gate_ev = sem("gate_ev")
        self.kt0_in = sem("kt0_in")
        self.kt1_in = sem("kt1_in")
        self.kt2_in = sem("kt2_in")
        self.q_zero = sem("q_zero")
        self.q_spread = sem("q_spread")
        self.ss_mm = sem("ss_mm")
        self.p_zero = sem("p_zero")
        self.ss_ev = sem("ss_ev")
        self.ss_prod = sem("ss_prod")
        self.ss_rows = sem("ss_rows")
        self.sp_exp = sem("sp_exp")
        self.sp_ready = sem("sp_ready")
        self.st_mm = sem("st_mm")
        self.st_ev = sem("st_ev")
        self.sd_ready = sem("sd_ready")
        self.sb_mm = sem("sb_mm")
        self.sb_ev = sem("sb_ev")
        self.spv_mm = sem("spv_mm")
        self.spv_ev = sem("spv_ev")
        self.spv_sum = sem("spv_sum")
        self.satt = sem("satt")
        self.tk_mm = sem("tk_mm")
        self.tk_ev = sem("tk_ev")
        self.tk_out = sem("tk_out")
        self.vt_out = sem("vt_out")
        self.h_out = sem("h_out")
        self.at_sc = sem("at_sc")
        self.at_s = sem("at_s")
        self.at_nm = sem("at_nm")
        self.at_e = sem("at_e")
        self.at_p = sem("at_p")
        self.at_t = sem("at_t")
        self.at_pt = sem("at_pt")
        self.at_pv = sem("at_pv")
        self.at_ev = sem("at_ev")
        self.nsp = sem("nsp")
        self.lru_l = sem("lru_l")
        self.lru_th = sem("lru_th")
        self.lru_e = sem("lru_e")
        self.lru_c = sem("lru_c")
        self.lru_s = sem("lru_s")
        self.lru_a = sem("lru_a")
        self.lru_y = sem("lru_y")
        self.lru_yg = sem("lru_yg")
        self.gelu_z = sem("gelu_z")
        self.sig_z = sem("sig_z")
        self.wba_in = sem("wba_in")
        self.wbl_in = sem("wbl_in")
        self.wout_in = sem("wout_in")
        self.ba_mm = sem("ba_mm")
        self.ba_ev = sem("ba_ev")
        self.bl_mm = sem("bl_mm")
        self.bl_ev = sem("bl_ev")
        self.merged = sem("merged")
        self.wo_mm = sem("wo_mm")
        self.wo_ev = sem("wo_ev")
        self.res_in = sem("res_in")
        self.wr_in = sem("wr_in")
        self.lg_mm = sem("lg_mm")
        self.ht_mm = sem("ht_mm")
        self.ht_ev = sem("ht_ev")
        self.rt_exp = sem("rt_exp")
        self.oh_ready = sem("oh_ready")
        self.rk_mm = sem("rk_mm")
        self.rt_ready = sem("rt_ready")
        self.cnt_ready = sem("cnt_ready")
        self.shifted = sem("shifted")
        self.brow_in = sem("brow_in")
        self.bias_used = sem("bias_used")
        self.oh_ok = sem("oh_ok")
        self.go_ok = sem("go_ok")
        self.x_mm = sem("x_mm")
        self.xg_ok = sem("xg_ok")
        self.x_tr = sem("x_tr")
        self.xT_ok = sem("xT_ok")
        self.w0 = sem("w0")
        self.w1 = sem("w1")
        self.w2 = sem("w2")
        self.w3 = sem("w3")
        self.w4 = sem("w4")
        self.w5 = sem("w5")
        self.g0_mm = sem("g0_mm")
        self.g1_mm = sem("g1_mm")
        self.u0_mm = sem("u0_mm")
        self.u1_mm = sem("u1_mm")
        self.d0_mm = sem("d0_mm")
        self.d1_mm = sem("d1_mm")
        self.gmin = sem("gmin")
        self.sig = sem("sig")
        self.gated = sem("gated")
        self.u_rd = sem("u_rd")
        self.hid_ok = sem("hid_ok")
        self.h_tr = sem("h_tr")
        self.hT_ok = sem("hT_ok")
        self.y_ev = sem("y_ev")
        self.go_mm = sem("go_mm")
        self.goT_ok = sem("goT_ok")
        self.c_mm = sem("c_mm")
        self.added = sem("added")
        self.wpg_in = sem("wpg_in")
        self.wpl_in = sem("wpl_in")
        self.pg_mm = sem("pg_mm")
        self.pg_ev = sem("pg_ev")
        self.pl_mm = sem("pl_mm")
        self.pl_ev = sem("pl_ev")
        self.pg_sig = sem("pg_sig")
        self.gated_p = sem("gated_p")
        self.y_ok = sem("y_ok")
        self.out_done = sem("out_done")
        self.kv_copy = sem("kv_copy")
        self.dve = sem("dve")
        self.act = sem("act")


def build(nc, a):
    with ExitStack() as ctx:
        def sb(name, shape, dt=F32):
            return ctx.enter_context(nc.sbuf_tensor(name, shape, dt))

        S = Signals(lambda name: ctx.enter_context(nc.semaphore(name)))
        PS = ctx.enter_context(nc.psum_tensor("PS", [P, 8, CH], F32))

        ring = sb("ring", [P, 6, 4096])
        Zb = sb("Zb", [P, NZ * T])
        Z = Zb[:, :].rearrange("p (n t) -> p n t", t=T)
        cst = sb("cst", [P, NCST])
        feat = sb("feat", [P, KT, NFEAT])
        gqk = sb("gqk", [P, 2])
        hT = sb("hT", [P, KT, T])
        xc = sb("xc", [P, KT, T])
        lt = sb("lt", [P, KT, T])
        attT = sb("attT", [P, HPG, T])
        rope = attT[0:32, 0:2, :]
        rstd = sb("rstd", [P, T])
        sm = sb("sm", [P, 64])
        nsp = sb("nsp", [P, 6, KT])
        pvrows = sb("pvrows", [96, P])
        prod = sb("prod", [P, 96])
        srow = sb("srow", [32, 324])
        sdiag = sb("sdiag", [32, 3, 32])
        brt = sb("brt", [1, E])
        lt_flat = lt[:, :, :].rearrange("p k t -> p (k t)")
        W2 = ring[:, 4:6, :].rearrange("p a n -> p (a n)")
        sq_qk = W2[:, 0:24 * T]
        rot = W2[0:32, 0:24 * T].rearrange("p (n t) -> p n t", t=T)
        vtok = W2[:, 0:3072].rearrange("p (b n) -> p b n", b=2)
        sS = W2[:, 3072:4608].rearrange("p (b n) -> p b n", b=2)
        sPT = W2[:, 4608:6144].rearrange("p (b n) -> p b n", b=2)
        stages = [[[W2[:, at + g * CH:at + (g + 1) * CH] for g in range(NG)] for at in (6144, 3072, 4608)],
                  [None, None, [ring[:, 0, 1024:1536], ring[:, 0, 1536:2048], W2[:, 7680:8192]]]]
        wrg = ring[:, 1, :].rearrange("p (a n c d) -> p a n c d", a=2, n=4, c=2)
        kts = [ring[:, 2, :].rearrange("p (s k) -> p s k", s=32), ring[:, 3, :].rearrange("p (s k) -> p s k", s=32),
               ring[:, 0, 0:2048].rearrange("p (s k) -> p s k", s=32)]
        qdiag = [ring[:, 0, 2048:3072], ring[:, 0, 3072:4096], lt_flat[:, 0:1024]]
        pdiag = [qdiag[0], qdiag[1], ring[:, 0, 0:1024]]
        vts = [ring[:, s, :].rearrange("p (b n) -> p b n", b=NS) for s in (1, 2, 3)]
        wba = ring[:, 0, :].rearrange("p (k n) -> p k n", k=4)
        wbl = [ring[:, s, :].rearrange("p (k n) -> p k n", k=4) for s in (1, 2)]
        wout = [ring[:, s, :].rearrange("p (k n) -> p k n", k=4) for s in (3, 0)]
        pos = [0]

        def zb(shape, dt=None):
            n = 1
            for s in shape[1:]:
                n *= s
            v = Zb[0:shape[0], pos[0]:pos[0] + n]
            pos[0] += n
            if dt is not None:
                v = v.bitcast(dt)
            return v if len(shape) == 2 else v.rearrange("p (a n) -> p a n", a=shape[1])

        hrow = zb([P, 3, D])
        wpl, pT = zb([P, 2, D]), zb([P, 2, T])
        wr = zb([P, KT, E])
        brow = zb([1, 3 * D])
        xg, xgT = zb([P, CH]), zb([P, 4, P])
        sg, ss_, su = zb([P, CH]), zb([P, CH]), zb([P, CH])
        hm, hmT = zb([P, CH]), zb([P, 4, P])
        yb = zb([P, CH])
        pick, gpick, gpickT = zb([P, 3, CAP]), zb([P, 3, 2 * CAP]), zb([P, T])
        logit = zb([P, 3, E])
        oh = [zb([P, 3, E]) for _ in range(TOPK)]
        route, rtmp, rank, gate = zb([P, 3, E]), zb([P, 3, E]), zb([P, 3, E]), zb([P, 3, E])
        mx, mxi, mif = zb([P, 3, 8]), zb([P, 3, 8], U32), zb([P, 3, 8])
        ge, gs = zb([P, 3, TOPK]), zb([P, 3])
        cmax, most = zb([1, 1]), zb([1, 1], I32)
        assert pos[0] <= ZGA * T, pos[0]
        plT = Z[:, ZGA:ZGA + KT, :]
        sgp = Z[:, 0:KT, :]
        wpg = [ring[:, s, :].rearrange("p (k n) -> p k n", k=4) for s in (0, 1)]

        def further(eng, block_of, before=None, after=None):
            for c in range(1, NCHUNK):
                with eng.If(eng.value_load(most, min_val=0, max_val=T) > c * CAP):
                    if before is not None:
                        before(c)
                    with eng.Fori(0, E) as e:
                        block_of(e, e + c * E)
                    if after is not None:
                        after((c + 1) * E)

        ident = cst[:, C_ID:C_ID + P]
        ones = cst[:, C_ONE:C_ONE + P]
        tri = cst[:, C_TRI:C_TRI + P]
        eps = cst[:, C_EPS:C_EPS + 1]

        def fv(c):
            return feat[:, :, c:c + 1].to_broadcast([P, KT, T])

        def over_tiles(v, n=KT):
            return v.unsqueeze(1).to_broadcast([v.shape[0], n, v.shape[-1]])

        block = ctx.enter_context(nc.Block())

        @block.sync
        def _(sp):
            xT0 = Z[:, ZGL:ZGL + KT, :]
            sp.dma_start(xT0, a["xT"]).then_inc(S.x_in, 16)
            sp.dma_start(feat[:, :, :], a["feat"]).then_inc(S.x_in, 16)

            def win(piece, slot):
                return sp.dma_start(ring[:, slot, :], a["win"][piece].rearrange("p k n -> p (k n)"))

            wins = (S.win0, S.win1, S.win2, S.win3)
            for s in range(4):
                win(s, s).then_inc(wins[s], 16)
                if s == 0:
                    sp.dma_start(cst[:, :], a["cst"]).then_inc(S.cst_in, 16)
            sp.dma_start(rope, a["rope"]).then_inc(S.rope_in, 16)
            sp.dma_start(gqk[:, :], a["gqk"]).then_inc(S.rope_in, 16)
            with sp.Fori(1, 4) as i:
                for s in range(4):
                    sp.wait_ge(S.z_done, 16 * i + 4 * s - 12)
                    win(4 * i + s, s).then_inc(wins[s], 16)
            sp.wait_ge(S.z_done, 4 * 13)
            win(16, 0).then_inc(S.win0, 16)
            sp.wait_ge(S.z_done, 4 * 14)
            sp.dma_start(ring[:, 1, :], a["wrg"]).then_inc(S.wrg_in, 16)
            sp.wait_ge(S.z_done, 4 * 15)
            sp.dma_start(kts[0], a["kt0"]).then_inc(S.kt0_in, 16)
            sp.wait_ge(S.z_done, 4 * 16)
            sp.dma_start(kts[1], a["kt1"]).then_inc(S.kt1_in, 16)
            sp.wait_ge(S.z_done, NZ)
            sp.dma_start(kts[2], a["kt2"]).then_inc(S.kt2_in, 16)
            sp.wait_ge(S.gate_mm, 16)
            sp.dma_start(brt[:, :], a["b_router"]).then_inc(S.wr_in, 16)

            def cached_v(g, sem):
                n = SKEYS[g]
                src = a[f"cache{g}"].rearrange("b (k r) n -> k b r n", r=DIL[g])[:, :, 0, CH:2 * CH]
                sp.dma_start(vts[g][0:n, :, :], src).then_inc(sem, 16)

            cached_v(0, S.v_in)
            sp.wait_ge(S.ss_mm, 1)
            cached_v(1, S.v_in)
            cached_v(2, S.v_in)

            def half(w, k0, view, sem):
                sp.dma_start(view, w[k0 * P:(k0 + 4) * P, :].rearrange("(k p) n -> p k n", p=P)).then_inc(sem, 16)

            sp.wait_ge(S.spv_mm, 1)
            sp.wait_ge(S.vt_out, 16 * KV_STORES)
            half(a["w_br_att"], 0, wba, S.wba_in)
            half(a["w_br_lru"], 0, wbl[0], S.wbl_in)
            half(a["w_br_lru"], 4, wbl[1], S.wbl_in)
            half(a["w_out"], 0, wout[0], S.wout_in)
            sp.wait_ge(S.ba_mm, KT)
            half(a["w_out"], 4, wout[1], S.wout_in)

            def weights(e, s):
                rows = slice(s % 2 * CH, (s % 2 + 1) * CH)
                w = a["w_down"][e][rows, :] if s >= 4 else a["w_gu"][e][rows, s // 2 * D:(s // 2 + 1) * D]
                return w.rearrange("(k p) n -> p k n", p=P)

            def slot(s):
                return ring[:, s, :].rearrange("p (k n) -> p k n", k=4)

            full = (S.w0, S.w1, S.w2, S.w3, S.w4, S.w5)
            used = (S.g0_mm, S.g1_mm, S.u0_mm, S.u1_mm, S.d0_mm, S.d1_mm)
            sp.wait_ge(S.at_pv, 8)
            sp.wait_ge(S.tk_out, 16 * KV_STORES)
            sp.dma_start(wr[:, :, :], a["w_router"].rearrange("(k p) n -> p k n", p=P)).then_inc(S.wr_in, 16)
            sp.dma_start(wpl, a["w_ple"].rearrange("(k p) n -> p k n", p=P)).then_inc(S.wpl_in, 16)
            sp.dma_start(pT, a["pT"]).then_inc(S.wpl_in, 16)
            sp.dma_start(slot(4), weights(0, 4)).then_inc(S.w4, 16)
            sp.dma_start(slot(5), weights(0, 5)).then_inc(S.w5, 16)
            sp.wait_ge(S.bl_mm, KT)
            sp.dma_start(slot(1), weights(0, 1)).then_inc(S.w1, 16)
            sp.dma_start(slot(2), weights(0, 2)).then_inc(S.w2, 16)
            sp.dma_start(brow, a["bcat"][0]).then_inc(S.brow_in, 16)
            sp.wait_ge(S.wo_mm, KT)
            sp.dma_start(slot(0), weights(0, 0)).then_inc(S.w0, 16)
            sp.dma_start(slot(3), weights(0, 3)).then_inc(S.w3, 16)

            def load(e, n):
                for s in range(6):
                    sp.wait_ge(used[s], n)
                    sp.dma_start(slot(s), weights(e, s)).then_inc(full[s], 16)
                    if s == 3:
                        sp.wait_ge(S.bias_used, n)
                        sp.dma_start(brow, a["bcat"][e]).then_inc(S.brow_in, 16)

            with sp.Fori(1, E) as e:
                load(e, e)
            sp.wait_ge(S.cnt_ready, 1)
            further(sp, load, after=lambda n: sp.wait_ge(S.d1_mm, n))
            sp.wait_ge(S.g1_mm, E)
            half(a["w_ple_gate"], 0, wpg[0], S.wpg_in)
            half(a["w_ple_gate"], 4, wpg[1], S.wpg_in)
            for half_ in range(2):
                k = slice(4 * half_, 4 * half_ + 4)
                sp.wait_ge(S.y_ok, 4 * half_ + 4)
                sp.dma_start(a["yT"][:, k, :], sgp[:, k, :]).then_inc(S.out_done, 16)
            sp.wait_ge(S.out_done, 32)
            sp.wait_ge(S.kv_copy, 16 * (NS + 1) * NG)
            sp.wait_ge(S.conv_out, 48)
            sp.wait_ge(S.h_out, 32)

        @block.tensor
        def _(pe):
            mm = nc.tensor.matmul

            def sum_sq(src, nth):
                pe.wait_ge(S.sq_ok, nth)
                for k in range(KT):
                    last = mm(PS[:, 4, 0:T], ones, src[:, k, :], start=(k == 0), stop=(k == KT - 1))
                last.then_inc(S.ss_sum, 1)

            wins = (S.win0, S.win1, S.win2, S.win3)

            def z_piece(piece, slot, fill):
                w = ring[:, slot, :].rearrange("p (k n) -> p k n", k=KT)
                pe.wait_ge(wins[slot], fill)
                for t in range(4):
                    pe.wait_ge(S.z_evac, 4 * piece + t - 3)
                    for k in range(KT):
                        last = mm(PS[:, t, 0:T], w[:, k, t * P:(t + 1) * P], hT[:, k, :],
                                  start=(k == 0), stop=(k == KT - 1))
                    last.then_inc(S.z_done, 1)

            pe.wait_ge(S.xgain, 1)
            pe.wait_ge(S.win0, 16)
            w = ring[:, 0, :].rearrange("p (k n) -> p k n", k=KT)
            for t in range(4):
                for k in range(KT):
                    last = mm(PS[:, t, 0:T], w[:, k, t * P:(t + 1) * P], lt[:, k, :], start=(k == 0), stop=(k == KT - 1))
                last.then_inc(S.z_done, 1)
                if t == 0:
                    pe.wait_ge(S.cst_in, 16)
                    sum_sq(hT, 1)
            pe.wait_ge(S.h_ok, 1)
            for s in range(1, 4):
                z_piece(s, s, 16)
            for s in range(4):
                z_piece(4 + s, s, 32)
            pe.wait_ge(S.sq_qk, 1)
            for c in range(13):
                n = min(CH, 24 * T - c * CH)
                if c >= 4:
                    pe.wait_ge(S.qkn_ev, c - 3)
                mm(PS[:, 4 + c % 4, 0:n], ones, sq_qk[:, c * CH:c * CH + n], start=True, stop=True).then_inc(S.qkn_mm, 1)
            with pe.Fori(2, 4) as i:
                for s in range(4):
                    z_piece(4 * i + s, s, 16 * i + 16)
            z_piece(16, 0, 16 * 5)

            pe.wait_ge(S.wrg_in, 16)
            pe.wait_ge(S.conv_done, 1)
            for j in range(KT):
                for m in range(2):
                    n = 2 * j + m
                    pe.wait_ge(S.z_evac, NZ)
                    if n >= 8:
                        pe.wait_ge(S.gate_ev, n - 7)
                    for c in range(2):
                        last = mm(PS[:, n % 8, 0:T], wrg[:, m, j // 2, c, (j % 2) * P:(j % 2 + 1) * P],
                                  xc[:, 2 * (j // 2) + c, :], start=(c == 0), stop=(c == 1))
                    last.then_inc(S.gate_mm, 1)

            pe.wait_ge(S.q_spread, 1)
            pe.wait_ge(S.gate_ev, 16)
            for sem in (S.kt0_in, S.kt1_in, S.kt2_in):
                pe.wait_ge(sem, 16)
            for c in range(NS * HPG):
                for g in range(NG):
                    last = mm(PS[32 * g:32 * g + 32, 4, 0:SKEYS[g]], qdiag[g][:, 32 * c:32 * c + 32], kts[g][:, c, :],
                              start=(c == 0), stop=(c == NS * HPG - 1))
            last.then_inc(S.ss_mm, 1)

            pe.wait_ge(S.ss_prod, 1)
            for g in range(NG):
                last = mm(PS[0:32, 5, g:g + 1], prod[:, g * 32:(g + 1) * 32], ones[:, 0:1], start=True, stop=True)
            last.then_inc(S.ss_rows, 1)

            n = 0
            for z0 in (ZK, ZV):
                for b, (t0, nt) in enumerate(BLK):
                    for g in range(NG):
                        if n >= 4:
                            pe.wait_ge(S.tk_ev, n - 3)
                        for h in range(HPG):
                            last = nc.tensor.transpose(PS[0:nt, n % 4, h * P:(h + 1) * P],
                                                       Z[:, z0 + g * HPG + h, t0:t0 + nt], ident)
                        last.then_inc(S.tk_mm, 1)
                        n += 1

            def scores(it):
                h, qb = it // 2, it % 2
                n = P * (qb + 1)
                if it == 0:
                    pe.wait_ge(S.tk_ev, 18)
                if it >= 2:
                    pe.wait_ge(S.at_s, it - 1)
                ps = PS[:, 2 * (it % 2):2 * (it % 2) + 2, :].rearrange("p a n -> p (a n)")
                for g in range(NG):
                    last = mm(ps[:, g * n:(g + 1) * n], Z[:, ZQ + g * HPG + h, qb * P:(qb + 1) * P],
                              Z[:, ZK + g * HPG + h, 0:n], start=True, stop=True)
                last.then_inc(S.at_sc, 1)

            def weigh(it):
                h, qb = it // 2, it % 2
                blocks = [(g, kb) for g in range(NG) for kb in range(qb + 1)]
                pe.wait_ge(S.at_p, it + 1)
                if it >= 1:
                    pe.wait_ge(S.at_pt, it)
                else:
                    pe.wait_ge(S.sb_ev, 1)
                ps = PS[:, 4:6, :].rearrange("p a n -> p (a n)")
                for j in range(len(blocks)):
                    last = nc.tensor.transpose(ps[:, j * P:(j + 1) * P], sS[:, it % 2, j * P:(j + 1) * P], ident)
                last.then_inc(S.at_t, 1)
                pe.wait_ge(S.at_pt, it + 1)
                if it >= 2:
                    pe.wait_ge(S.at_ev, it - 1)
                for j, (g, kb) in enumerate(blocks):
                    last = mm(PS[:, 6 + it % 2, 0:P], vtok[:, kb, (g * HPG + h) * P:(g * HPG + h + 1) * P],
                              sPT[:, it % 2, j * P:(j + 1) * P], start=(j == 0), stop=(j == len(blocks) - 1))
                last.then_inc(S.at_pv, 1)

            scores(0)
            scores(1)
            pe.wait_ge(S.sp_ready, 1)
            off = 0
            for g in range(NG):
                n = SKEYS[g]
                last = nc.tensor.transpose(PS[0:n, 6, g * 32:(g + 1) * 32], srow[:, off:off + n], ident[0:32, 0:32])
                off += n
            last.then_inc(S.st_mm, 1)
            pe.wait_ge(S.sd_ready, 1)
            for g in range(NG):
                last = mm(PS[:, 7, g * 32:(g + 1) * 32], ones[0:32, :], sdiag[:, g, :], start=True, stop=True)
            last.then_inc(S.sb_mm, 1)
            for it in range(8):
                weigh(it)
                if it + 2 < 8:
                    scores(it + 2)
                if it == 2:
                    pe.wait_ge(S.st_ev, 3)
                    pe.wait_ge(S.sb_ev, 1)
                    pe.wait_ge(S.v_in, 48)
                    for b in range(NS):
                        for h in range(HPG):
                            c = b * HPG + h
                            for g in range(NG):
                                n = SKEYS[g]
                                last = mm(PS[32 * g:32 * g + 32, 7, 256:384], pdiag[g][0:n, 32 * c:32 * c + 32],
                                          vts[g][0:n, b, h * P:(h + 1) * P], start=(c == 0), stop=(c == NS * HPG - 1))
                    last.then_inc(S.spv_mm, 1)
            pe.wait_ge(S.spv_ev, 1)
            pe.wait_ge(S.at_s, 8)
            for g in range(NG):
                last = mm(PS[:, 0, 0:32], pvrows[:, :], ident[0:96, 32 * g:32 * g + 32],
                          start=(g == 0), stop=(g == NG - 1))
            last.then_inc(S.spv_sum, 1)

            def dense(weights, arrived, src, nk, done, evac, base=1):
                for m in range(KT):
                    if m >= 4:
                        pe.wait_ge(evac, m - 3)
                    for k in range(nk):
                        if m == 0 and k in arrived:
                            pe.wait_ge(*arrived[k])
                        last = mm(PS[:, 4 * base + m % 4, 0:T], weights(k)[:, m * P:(m + 1) * P], src[:, k, :],
                                  start=(k == 0), stop=(k == nk - 1))
                    last.then_inc(done, 1)

            pe.wait_ge(S.satt, 1)
            pe.wait_ge(S.at_ev, 8)
            dense(lambda k: wba[:, k, :], {0: (S.wba_in, 16)}, attT, 4, S.ba_mm, S.ba_ev)
            pe.wait_ge(S.lru_yg, 1)
            dense(lambda k: wbl[k // 4][:, k % 4, :], {0: (S.wbl_in, 32)}, Z[:, ZGR:ZGR + KT, :], 8, S.bl_mm, S.bl_ev, 0)
            pe.wait_ge(S.ba_ev, KT)
            pe.wait_ge(S.merged, 1)
            pe.wait_ge(S.wout_in, 32)
            for m in range(KT + 2):
                if m < KT:
                    if m >= 4:
                        pe.wait_ge(S.wo_ev, m - 3)
                    for k in range(KT):
                        last = mm(PS[:, 4 + m % 4, 0:T], wout[k // 4][:, k % 4, m * P:(m + 1) * P], hT[:, k, :],
                                  start=(k == 0), stop=(k == KT - 1))
                    last.then_inc(S.wo_mm, 1)
                if m >= 2:
                    pe.wait_ge(S.sq_tile, m - 1)
                    last = mm(PS[:, 0, 0:T], ones, lt[:, m - 2, :], start=(m == 2), stop=(m == KT + 1))
            last.then_inc(S.ss_sum, 1)

            pe.wait_ge(S.h_ok, 2)
            pe.wait_ge(S.wr_in, 32)
            for b, (t0, nt) in enumerate(BLK):
                o = PS[0:nt, 0, b * E:(b + 1) * E]
                mm(o, ones[0:1, 0:nt], brt[:, :], start=True, stop=False)
                for k in range(KT):
                    last = mm(o, hT[:, k, t0:t0 + nt], wr[:, k, :], start=False, stop=(k == KT - 1))
            last.then_inc(S.lg_mm, 1)
            for b, (t0, nt) in enumerate(BLK):
                if b:
                    pe.wait_ge(S.ht_ev, b)
                ps = PS[:, 6:8, :].rearrange("p a n -> p (a n)")
                for k in range(KT):
                    last = nc.tensor.transpose(ps[0:nt, k * P:(k + 1) * P], hT[:, k, t0:t0 + nt], ident)
                last.then_inc(S.ht_mm, 1)
            pe.wait_ge(S.wpl_in, 32)
            for m in range(KT):
                if m >= 4:
                    pe.wait_ge(S.pl_ev, m - 3)
                for k in range(2):
                    last = mm(PS[:, 2 + m % 4, 0:T], wpl[:, k, m * P:(m + 1) * P], pT[:, k, :],
                              start=(k == 0), stop=(k == 1))
                last.then_inc(S.pl_mm, 1)
            pe.wait_ge(S.oh_ready, 1)
            for b in range(3):
                o = PS[:, 1, b * E:(b + 1) * E]
                for c in range(b):
                    mm(o, ones, route[:, c, :], start=(c == 0), stop=False)
                mm(o, tri, route[:, b, :], start=(b == 0), stop=True)
            for c in range(3):
                last = mm(PS[:, 1, 3 * E:4 * E], ones, route[:, c, :], start=(c == 0), stop=(c == 2))
            last.then_inc(S.rk_mm, 1)

            def seed(bank, at, stride):
                for h in range(2):
                    c = at + h * stride
                    last = mm(PS[CAP * h:CAP * (h + 1), bank, :], ones[0:1, 0:CAP], brow[:, c:c + CH],
                              start=True, stop=False)
                return last

            def half_product(bank, src, slot):
                w = ring[:, slot, :].rearrange("p (k n) -> p k n", k=4)
                f = slot % 2 * CAP
                for k in range(4):
                    for h in range(2):
                        last = mm(PS[CAP * h:CAP * (h + 1), bank, :], src[:, k, f:f + CAP], w[:, k, h * CH:(h + 1) * CH],
                                  start=False, stop=(slot % 2 == 1 and k == 3))
                return last

            def transposes(bank, src):
                for j in range(4):
                    last = nc.tensor.transpose(PS[:, bank, j * P:(j + 1) * P], src[:, j * P:(j + 1) * P], ident)
                return last

            def rows(n):
                pe.wait_ge(S.oh_ok, n + 1)
                for b, (t0, nt) in enumerate(BLK):
                    for h in range(2):
                        last = mm(PS[CAP * h:CAP * (h + 1), 5, :], pick[0:nt, b, :], hrow[0:nt, b, h * CH:(h + 1) * CH],
                                  start=(b == 0), stop=(b == 2))
                last.then_inc(S.x_mm, 1)

            def rows_T(n):
                pe.wait_ge(S.xg_ok, n + 1)
                transposes(6, xg).then_inc(S.x_tr, 1)

            def spread(n, j):
                if not (isinstance(n, int) and n == 0 and j == 0):
                    pe.wait_ge(S.added, 4 * n + j)
                for h in range(2):
                    last = mm(PS[:, 2 + h, 0:T], yb[CAP * h:CAP * (h + 1), j * P:(j + 1) * P],
                              gpickT[CAP * h:CAP * (h + 1), :], start=True, stop=True)
                last.then_inc(S.c_mm, 1)

            def block_(n, prev=True, following=True):
                first = isinstance(n, int) and n == 0
                pe.wait_ge(S.brow_in, 16 * (n + 1))
                if not first:
                    pe.wait_ge(S.gmin, n)
                seed(0, 0, 2 * CH)
                pe.wait_ge(S.w0, 16 * (n + 1))
                pe.wait_ge(S.xT_ok, n + 1)
                half_product(0, xgT, 0).then_inc(S.g0_mm, 1)
                if prev:
                    pe.wait_ge(S.y_ev, n)
                    pe.wait_ge(S.goT_ok, n)
                    spread(n - 1, 0)
                pe.wait_ge(S.w1, 16 * (n + 1))
                half_product(0, xgT, 1).then_inc(S.g1_mm, 1)
                if not first:
                    pe.wait_ge(S.u_rd, n)
                seed(1, CH, 2 * CH)
                if prev:
                    spread(n - 1, 1)
                pe.wait_ge(S.w2, 16 * (n + 1))
                half_product(1, xgT, 2).then_inc(S.u0_mm, 1)
                if prev:
                    spread(n - 1, 2)
                pe.wait_ge(S.w3, 16 * (n + 1))
                half_product(1, xgT, 3).then_inc(S.u1_mm, 1)
                if prev:
                    spread(n - 1, 3)
                seed(4, 2 * D, CH).then_inc(S.bias_used, 1)
                if following:
                    rows(n + 1)
                pe.wait_ge(S.hid_ok, n + 1)
                transposes(7, hm).then_inc(S.h_tr, 1)
                if following:
                    rows_T(n + 1)
                pe.wait_ge(S.go_ok, n + 1)
                for b, (t0, nt) in enumerate(BLK):
                    last = nc.tensor.transpose(PS[:, 5, t0:t0 + nt], gpick[0:nt, b, :], ident[0:nt, 0:nt])
                last.then_inc(S.go_mm, 1)
                pe.wait_ge(S.w4, 16 * (n + 1))
                pe.wait_ge(S.hT_ok, n + 1)
                half_product(4, hmT, 4).then_inc(S.d0_mm, 1)
                pe.wait_ge(S.w5, 16 * (n + 1))
                half_product(4, hmT, 5).then_inc(S.d1_mm, 1)

            def spread_all(n):
                pe.wait_ge(S.y_ev, n + 1)
                pe.wait_ge(S.goT_ok, n + 1)
                for j in range(4):
                    spread(n, j)

            pe.wait_ge(S.pl_ev, KT)
            pe.wait_ge(S.ht_ev, 3)
            rows(0)
            rows_T(0)
            pe.wait_ge(S.rt_ready, 1)
            block_(0, prev=False)
            block_(1)
            with pe.Fori(2, E - 1) as e:
                block_(e)
            block_(E - 1, following=False)
            spread_all(E - 1)
            pe.wait_ge(S.cnt_ready, 1)

            def apart(e, n):
                rows(n)
                rows_T(n)
                block_(n, prev=False, following=False)
                spread_all(n)

            further(pe, apart, after=lambda n: pe.wait_ge(S.added, 4 * n))

            pe.wait_ge(S.h_ok, 3)
            pe.wait_ge(S.wpg_in, 32)
            for m in range(KT):
                if m == 1:
                    sum_sq(lt, 2)
                if m >= 4:
                    pe.wait_ge(S.pg_ev, m - 3)
                for k in range(KT):
                    last = mm(PS[:, m % 4, 0:T], wpg[k // 4][:, k % 4, m * P:(m + 1) * P], hT[:, k, :],
                              start=(k == 0), stop=(k == KT - 1))
                last.then_inc(S.pg_mm, 1)

        @block.scalar
        def _(act):
            A = nc.scalar.activation

            def root(nth, out, ps, scale):
                act.wait_ge(S.ss_sum, nth)
                return A(out, ps, ACT.Sqrt, bias=eps, scale=scale)

            act.wait_ge(S.cst_in, 16)
            root(1, rstd[:, :], PS[:, 4, 0:T], 1.0 / D).then_inc(S.rms_ok, 1)

            act.wait_ge(S.x_in, 32)
            A(nsp[:, 0, :], feat[:, :, FLAM], ACT.Abs).then_inc(S.act, 1)
            act.wait_ge(S.act, 1)
            A(nsp[:, 0, :], nsp[:, 0, :], ACT.Exp, scale=-1.0).then_inc(S.nsp, 1)
            act.wait_ge(S.nsp, 1)
            A(nsp[:, 1, :], nsp[:, 0, :], ACT.Ln, bias=ones[:, 0:1]).then_inc(S.nsp, 1)

            def evac(n, bank):
                act.wait_ge(S.z_done, n + 1)
                A(Z[:, n, :], PS[:, bank, 0:T], ACT.Copy).then_inc(S.z_evac, 1)

            def shift(g, b):
                n = (WB[g] - 1) // 16 * 16
                act.dma_start(a[f"kvs{g}"][b, 0:n, :].rearrange("(q r) n -> q (r n)", q=16),
                              a[f"cache{g}"][b, 1:n + 1, :].rearrange("(q r) n -> q (r n)", q=16)).then_inc(S.kv_copy, 16)

            def shift_rest(g):
                n = (WB[g] - 1) // 16 * 16
                act.dma_start(a[f"kvs{g}"][:, n:WB[g] - 1, :].rearrange("b r n -> r b n"),
                              a[f"cache{g}"][:, n + 1:WB[g], :].rearrange("b r n -> r b n")).then_inc(S.kv_copy, 16)

            shift(0, 0)
            shift(1, 0)
            act.wait_ge(S.z_evac, 4)
            with act.Fori(1, LOOP_A) as i:
                for t in range(4):
                    evac(4 * i + t, t)
                shift(0, i)
                shift(1, i)
            for c in range(13):
                n = min(CH, 24 * T - c * CH)
                act.wait_ge(S.qkn_mm, c + 1)
                A(sq_qk[:, c * CH:c * CH + n], PS[:, 4 + c % 4, 0:n], ACT.Sqrt, bias=eps, scale=1.0 / HD)\
                    .then_inc(S.qkn_ev, 1)
            act.wait_ge(S.h_ok, 1)
            with act.Fori(LOOP_A, LOOP_A + EARLY) as i:
                for t in range(4):
                    evac(4 * i + t, t)
                shift(2, i - LOOP_A)
            with act.Fori(LOOP_A + EARLY, NPIECE) as i:
                for t in range(4):
                    evac(4 * i + t, t)

            act.wait_ge(S.conv_out, 48)
            for n in range(16):
                j, m = n // 2, n % 2
                act.wait_ge(S.gate_mm, n + 1)
                dst = hT[:, j, :] if m == 0 else Z[:, ZX + j, :]
                c = FBA if m == 0 else FBX
                A(dst, PS[:, n % 8, 0:T], ACT.Sigmoid, bias=feat[:, j, c:c + 1]).then_inc(S.gate_ev, 1)
            act.wait_ge(S.lru_l, 1)
            A(xc[:, :, :], hT[:, :, :], ACT.Tanh, scale=-1.0).then_inc(S.lru_th, 1)
            act.wait_ge(S.ss_mm, 1)
            off = 0
            for g in range(NG):
                n = SKEYS[g]
                A(srow[:, off:off + n], PS[32 * g:32 * g + 32, 4, 0:n], ACT.Copy).then_inc(S.ss_ev, 1)
                off += n
            A(lt[:, :, :], hT[:, :, :], ACT.Exp, scale=2.0).then_inc(S.lru_e, 1)
            act.wait_ge(S.lru_e, 1)
            A(hT[:, :, :], hT[:, :, :], ACT.Exp).then_inc(S.lru_a, 1)
            act.wait_ge(S.sp_exp, 1)
            A(srow[:, 0:323], srow[:, 0:323], ACT.Exp, bias=sm[0:32, 1:2], scale=SCALE, accum_out=sm[0:32, 2:3])\
                .then_inc(S.sp_exp, 1)
            act.wait_ge(S.lru_c, 1)
            A(xc[:, :, :], xc[:, :, :], ACT.Sqrt).then_inc(S.lru_s, 1)

            def prompt_exp(it):
                n = 3 * P * (it % 2 + 1)
                act.wait_ge(S.at_nm, it + 1)
                A(sS[:, it % 2, 0:n], sS[:, it % 2, 0:n], ACT.Exp, bias=sm[:, 8 + it:9 + it], scale=SCALE,
                  accum_out=sm[:, 16 + it:17 + it]).then_inc(S.at_e, 1)

            def prompt_out(it):
                n = 3 * P * (it % 2 + 1)
                act.wait_ge(S.at_t, it + 1)
                if it >= 2:
                    act.wait_ge(S.at_pv, it - 1)
                A(sPT[:, it % 2, 0:n], PS[:, 4:6, :].rearrange("p a n -> p (a n)")[:, 0:n], ACT.Copy).then_inc(S.at_pt, 1)

            def prompt_att(it):
                act.wait_ge(S.at_pv, it + 1)
                A(attT[:, it // 2, (it % 2) * P:(it % 2 + 1) * P], PS[:, 6 + it % 2, 0:P], ACT.Copy).then_inc(S.at_ev, 1)

            prompt_exp(0)
            act.wait_ge(S.st_mm, 1)
            act.wait_ge(S.p_zero, 1)
            for g in range(NG):
                n = SKEYS[g]
                A(pdiag[g][0:n, ::33], PS[0:n, 6, g * 32:(g + 1) * 32], ACT.Copy).then_inc(S.st_ev, 1)
            act.wait_ge(S.sb_mm, 1)
            A(prod[:, :], PS[:, 7, 0:96], ACT.Copy).then_inc(S.sb_ev, 1)
            for it in range(8):
                prompt_out(it)
                if it + 1 < 8:
                    prompt_exp(it + 1)
                prompt_att(it)
                if it == 2:
                    act.wait_ge(S.spv_mm, 1)
                    A(pvrows[:, :], PS[0:96, 7, 256:384], ACT.Copy).then_inc(S.spv_ev, 1)
            A(Z[:, ZGA:ZGA + KT, :], Z[:, ZGA:ZGA + KT, :], ACT.Sigmoid).then_inc(S.sig_z, 1)
            A(Z[:, ZGR:ZGR + KT, :], Z[:, ZGR:ZGR + KT, :], ACT.Gelu_apprx_tanh).then_inc(S.gelu_z, 1)
            A(Z[:, ZGL:ZGL + KT, :], Z[:, ZGL:ZGL + KT, :], ACT.Sigmoid).then_inc(S.sig_z, 1)

            root(2, rstd[:, :], PS[:, 0, 0:T], 1.0 / D).then_inc(S.rms_ok, 1)
            for b in range(EARLY, NS):
                shift(2, b)
            for g in range(NG):
                shift_rest(g)
            for b, (t0, nt) in enumerate(BLK):
                act.wait_ge(S.ht_mm, b + 1)
                act.wait_ge(S.bl_ev, KT)
                A(hrow[0:nt, b, :], PS[:, 6:8, :].rearrange("p a n -> p (a n)")[0:nt, :], ACT.Copy).then_inc(S.ht_ev, 1)
            for m in range(KT):
                act.wait_ge(S.pl_mm, m + 1)
                A(plT[:, m, :], PS[:, 2 + m % 4, 0:T], ACT.Copy).then_inc(S.pl_ev, 1)
            act.wait_ge(S.rt_exp, 1)
            A(ge[:, :, :], ge[:, :, :], ACT.Exp).then_inc(S.rt_exp, 1)

            def tiles(bank):
                return PS[:, bank, :].rearrange("p (k n) -> p k n", k=4)

            def rows_copy(n):
                act.wait_ge(S.x_mm, n + 1)
                A(xg, PS[:, 5, :], ACT.Copy).then_inc(S.xg_ok, 1)

            def rows_T_copy(n):
                act.wait_ge(S.x_tr, n + 1)
                A(xgT, tiles(6), ACT.Copy).then_inc(S.xT_ok, 1)

            def block_(n, following=True):
                act.wait_ge(S.gmin, n + 1)
                A(ss_, sg, ACT.Sigmoid, scale=ALPHA).then_inc(S.sig, 1)
                if following:
                    rows_copy(n + 1)
                act.wait_ge(S.h_tr, n + 1)
                A(hmT, tiles(7), ACT.Copy).then_inc(S.hT_ok, 1)
                if following:
                    rows_T_copy(n + 1)
                act.wait_ge(S.go_mm, n + 1)
                A(gpickT, PS[:, 5, 0:T], ACT.Copy).then_inc(S.goT_ok, 1)

            rows_copy(0)
            rows_T_copy(0)
            with act.Fori(0, E - 1) as e:
                block_(e)
            block_(E - 1, following=False)
            act.wait_ge(S.cnt_ready, 1)

            def apart(e, n):
                rows_copy(n)
                rows_T_copy(n)
                block_(n, following=False)

            further(act, apart)

            root(3, rstd[:, :], PS[:, 4, 0:T], 1.0 / D).then_inc(S.rms_ok, 1)
            for m in range(KT):
                act.wait_ge(S.pg_ev, m + 1)
                A(sgp[:, m, :], sgp[:, m, :], ACT.Sigmoid).then_inc(S.pg_sig, 1)

        @block.vector
        def _(v):
            TT, TS, STT = nc.vector.tensor_tensor, nc.vector.tensor_scalar, nc.vector.scalar_tensor_tensor
            done = [0]

            def link(ins):
                ins.then_inc(S.dve, 1)
                done[0] = done[0] + 1
                v.wait_ge(S.dve, done[0])

            x0 = Z[:, ZGL:ZGL + KT, :]
            v.wait_ge(S.x_in, 32)
            TT(lt[:, :, :], x0, fv(FGM), ALU.mult).then_inc(S.xgain, 1)
            TT(hT[:, :, :], x0, x0, ALU.mult).then_inc(S.sq_ok, 1)
            v.wait_ge(S.rms_ok, 1)
            link(nc.vector.reciprocal(rstd[:, :], rstd[:, :]))
            v.wait_ge(S.xgain, 1)
            TT(hT[:, :, :], lt[:, :, :], over_tiles(rstd[:, :]), ALU.mult).then_inc(S.h_ok, 1)
            for n in range(4):
                v.wait_ge(S.z_done, n + 1)
                TT(Z[:, n, :], PS[:, n, 0:T], rstd[:, :], ALU.mult).then_inc(S.z_evac, 1)

            v.wait_ge(S.z_evac, 24)
            TT(sq_qk, Zb[:, 0:24 * T], Zb[:, 0:24 * T], ALU.mult).then_inc(S.sq_qk, 1)
            v.wait_ge(S.z_evac, ZX + KT)
            X = Z[:, ZX:ZX + KT, :]
            link(TT(xc[:, :, :], X, fv(FW + 3), ALU.mult))
            link(TT(xc[:, :, :], xc[:, :, :], fv(FCB), ALU.add))
            for back in (1, 2, 3):
                w = feat[:, :, FW + 3 - back:FW + 4 - back]
                n = NP - back
                link(TT(lt[:, :, 0:n], X[:, :, 0:n], w.to_broadcast([P, KT, n]), ALU.mult))
                link(TT(lt[:, :, NP:T], feat[:, :, FSC + (3 - back) * NS:FSC + (4 - back) * NS],
                        w.to_broadcast([P, KT, NS]), ALU.mult))
                link(TT(xc[:, :, back:NP], xc[:, :, back:NP], lt[:, :, 0:n], ALU.add))
                ins = TT(xc[:, :, NP:T], xc[:, :, NP:T], lt[:, :, NP:T], ALU.add)
                if back < 3:
                    link(ins)
            ins.then_inc(S.conv_done, 1)
            v.wait_ge(S.conv_done, 1)

            v.wait_ge(S.qkn_ev, 13)
            v.wait_ge(S.rope_in, 32)
            link(nc.vector.reciprocal(sq_qk, sq_qk))
            for m in range(2):
                zz = Zb[:, m * 12 * T:(m + 1) * 12 * T]
                ins = STT(zz, zz, gqk[:, m:m + 1], sq_qk[:, m * 12 * T:(m + 1) * 12 * T], ALU.mult, ALU.mult)
                if m == 0:
                    link(ins)
            ins.then_inc(S.qk_normed, 1)
            v.wait_ge(S.qk_normed, 1)
            v.wait_ge(S.rot_in, 32)
            zr = Z[0:32, 0:24, :]
            link(TT(rot, rot, over_tiles(rope[:, 1, :], 24), ALU.mult))
            link(TT(zr, zr, over_tiles(rope[:, 0, :], 24), ALU.mult))
            TT(zr, zr, rot, ALU.add).then_inc(S.roped, 1)
            v.wait_ge(S.roped, 1)
            TT(prod[:, :].rearrange("p (g b h) -> p g b h", g=NG, b=NS),
               Z[:, ZQ:ZQ + NHEAD, NP:T].rearrange("p (g h) b -> p g b h", g=NG),
               Z[:, ZK:ZK + NHEAD, NP:T].rearrange("p (g h) b -> p g b h", g=NG), ALU.mult).then_inc(S.ss_prod, 1)
            v.wait_ge(S.q_zero, 1)
            for g in range(NG):
                ins = nc.vector.tensor_copy(qdiag[g][:, ::33].rearrange("p (b h) -> p b h", b=NS),
                                            Z[:, ZQ + g * HPG:ZQ + (g + 1) * HPG, NP:T].rearrange("p h b -> p b h"))
            ins.then_inc(S.q_spread, 1)

            lam = feat[:, :, FLAM]
            v.wait_ge(S.nsp, 2)
            link(TS(nsp[:, 2, :], nsp[:, 0, :], 1.0, -1.0, ALU.add, ALU.add))
            link(TS(nsp[:, 3, :], nsp[:, 2, :], 1e-30, None, ALU.max))
            link(nc.vector.reciprocal(nsp[:, 3, :], nsp[:, 3, :]))
            link(TT(nsp[:, 1, :], nsp[:, 1, :], nsp[:, 3, :], ALU.mult))
            link(TS(nsp[:, 4, :], nsp[:, 2, :], 0.0, None, ALU.is_equal))
            link(TT(nsp[:, 1, :], nsp[:, 1, :], nsp[:, 4, :], ALU.add))
            link(TT(nsp[:, 1, :], nsp[:, 1, :], nsp[:, 0, :], ALU.mult))
            link(TS(nsp[:, 5, :], lam, -1.0, 0.0, ALU.mult, ALU.max))
            link(TT(nsp[:, 1, :], nsp[:, 1, :], nsp[:, 5, :], ALU.add))
            link(TS(nsp[:, 1, :], nsp[:, 1, :], -LRU_C, None, ALU.mult))
            v.wait_ge(S.gate_ev, 16)
            TT(X, X, xc[:, :, :], ALU.mult)
            TT(hT[:, :, :], hT[:, :, :], nsp[:, 1, :].unsqueeze(2).to_broadcast([P, KT, T]), ALU.mult)\
                .then_inc(S.lru_l, 1)

            def rows_out(kv):
                for b, (t0, nt) in enumerate(BLK):
                    direct = kv == 1 and b < 2
                    for g in range(NG):
                        n = 9 * kv + 3 * b + g
                        v.wait_ge(S.tk_mm, n + 1)
                        dst = vtok[:, b, g * CH:(g + 1) * CH] if direct else stages[kv][b][g][0:nt]
                        nc.vector.tensor_copy(dst, PS[0:nt, n % 4, :]).then_inc(S.tk_ev, 1)

            rows_out(0)
            v.wait_ge(S.ss_rows, 1)
            v.wait_ge(S.ss_ev, 3)
            link(nc.vector.tensor_copy(srow[:, 320:323], PS[0:32, 5, 0:3]))
            link(nc.vector.tensor_reduce(sm[0:32, 0:1], srow[:, 0:323], AX, ALU.max))
            TS(sm[0:32, 1:2], sm[0:32, 0:1], -SCALE, None, ALU.mult).then_inc(S.sp_exp, 1)
            v.wait_ge(S.lru_th, 1)
            v.wait_ge(S.lru_e, 1)
            STT(xc[:, :, :], lt[:, :, :], 1.0, xc[:, :, :], ALU.add, ALU.mult).then_inc(S.lru_c, 1)
            rows_out(1)
            v.wait_ge(S.sp_exp, 2)
            link(nc.vector.reciprocal(sm[0:32, 3:4], sm[0:32, 2:3]))
            TS(srow[:, 0:323], srow[:, 0:323], sm[0:32, 3:4], None, ALU.mult).then_inc(S.sp_ready, 1)
            v.wait_ge(S.sp_ready, 1)
            for g in range(NG):
                ins = TS(sdiag[:, g, :], ident[0:32, 0:32], srow[:, 320 + g:321 + g], None, ALU.mult)
            ins.then_inc(S.sd_ready, 1)

            def mask_max(it):
                h, qb = it // 2, it % 2
                n = 3 * P * (qb + 1)
                m = cst[:, C_MASK1:C_MASK1 + n] if qb else cst[:, C_MASK0:C_MASK0 + n]
                v.wait_ge(S.at_sc, it + 1)
                if it >= 2:
                    v.wait_ge(S.at_t, it - 1)
                ps = PS[:, 2 * (it % 2):2 * (it % 2) + 2, :].rearrange("p a n -> p (a n)")[:, 0:n]
                TT(sS[:, it % 2, 0:n], ps, m, ALU.add).then_inc(S.at_s, 1)
                v.wait_ge(S.at_s, it + 1)
                link(nc.vector.tensor_reduce(sm[:, 24:25], sS[:, it % 2, 0:n], AX, ALU.max))
                TS(sm[:, 8 + it:9 + it], sm[:, 24:25], -SCALE, None, ALU.mult).then_inc(S.at_nm, 1)

            def divide(it):
                n = 3 * P * (it % 2 + 1)
                v.wait_ge(S.at_e, it + 1)
                link(nc.vector.reciprocal(sm[:, 25:26], sm[:, 16 + it:17 + it]))
                TS(sS[:, it % 2, 0:n], sS[:, it % 2, 0:n], sm[:, 25:26], None, ALU.mult).then_inc(S.at_p, 1)

            v.wait_ge(S.tk_out, 16 * KV_STORES)
            mask_max(0)
            divide(0)
            mask_max(1)
            v.wait_ge(S.lru_s, 1)
            link(TT(X, X, xc[:, :, :], ALU.mult))
            v.wait_ge(S.lru_a, 1)
            for j in range(KT):
                nc.vector.tensor_tensor_scan(lt[:, j, 0:NP], hT[:, j, 0:NP], X[:, j, 0:NP], 0.0, ALU.mult, ALU.add)
            link(TT(lt[:, :, NP:T], hT[:, :, NP:T], feat[:, :, FSH:FSH + NS], ALU.mult))
            TT(lt[:, :, NP:T], lt[:, :, NP:T], X[:, :, NP:T], ALU.add).then_inc(S.lru_y, 1)
            for it in range(1, 8):
                divide(it)
                if it + 1 < 8:
                    mask_max(it + 1)
            v.wait_ge(S.sb_ev, 1)
            link(TT(prod[:, :].rearrange("p (g b h) -> p g b h", g=NG, b=NS),
                    prod[:, :].rearrange("p (g b h) -> p g b h", g=NG, b=NS),
                    Z[:, ZV:ZV + NHEAD, NP:T].rearrange("p (g h) b -> p g b h", g=NG), ALU.mult))
            link(TT(prod[:, 0:32], prod[:, 0:32], prod[:, 32:64], ALU.add))
            link(TT(prod[:, 0:32], prod[:, 0:32], prod[:, 64:96], ALU.add))
            v.wait_ge(S.spv_sum, 1)
            TT(attT[:, :, NP:T], PS[:, 0, 0:32].rearrange("p (b h) -> p h b", b=NS),
               prod[:, 0:32].rearrange("p (b h) -> p h b", b=NS), ALU.add).then_inc(S.satt, 1)

            v.wait_ge(S.sig_z, 1)
            for m in range(KT):
                if m == 4:
                    v.wait_ge(S.gelu_z, 1)
                    v.wait_ge(S.lru_y, 1)
                    TT(Z[:, ZGR:ZGR + KT, :], Z[:, ZGR:ZGR + KT, :], lt[:, :, :], ALU.mult).then_inc(S.lru_yg, 1)
                v.wait_ge(S.ba_mm, m + 1)
                TT(Z[:, ZGA + m, :], Z[:, ZGA + m, :], PS[:, 4 + m % 4, 0:T], ALU.mult).then_inc(S.ba_ev, 1)
            v.wait_ge(S.sig_z, 2)
            for m in range(KT):
                v.wait_ge(S.bl_mm, m + 1)
                TT(Z[:, ZGL + m, :], Z[:, ZGL + m, :], PS[:, m % 4, 0:T], ALU.mult).then_inc(S.bl_ev, 1)
            v.wait_ge(S.bl_ev, KT)
            v.wait_ge(S.ba_ev, KT)
            TT(hT[:, :, :], Z[:, ZGL:ZGL + KT, :], Z[:, ZGA:ZGA + KT, :], ALU.add).then_inc(S.merged, 1)
            v.wait_ge(S.res_in, 16)
            v.wait_ge(S.h_out, 32)
            for m in range(KT):
                v.wait_ge(S.wo_mm, m + 1)
                TT(xc[:, m, :], xc[:, m, :], PS[:, 4 + m % 4, 0:T], ALU.add).then_inc(S.wo_ev, 1)
                v.wait_ge(S.wo_ev, m + 1)
                TT(lt[:, m, :], xc[:, m, :], xc[:, m, :], ALU.mult).then_inc(S.sq_tile, 1)
                ins = TT(Z[:, m, :], xc[:, m, :], feat[:, m, FGF:FGF + 1].to_broadcast([P, T]), ALU.mult)
            link(ins)
            v.wait_ge(S.rms_ok, 2)
            link(nc.vector.reciprocal(rstd[:, :], rstd[:, :]))
            TT(hT[:, :, :], Z[:, 0:KT, :], over_tiles(rstd[:, :]), ALU.mult).then_inc(S.h_ok, 1)

            link(nc.vector.memset(logit[:, 2, :], 0.0))
            v.wait_ge(S.lg_mm, 1)
            nc.vector.tensor_copy(logit[:, 0:2, :].rearrange("p a n -> p (a n)"), PS[:, 0, 0:2 * E])
            link(nc.vector.tensor_copy(logit[0:NS, 2, :], PS[0:NS, 0, 2 * E:3 * E]))
            for b in range(3):
                ins = nc.vector.max(mx[:, b, :], logit[:, b, :])
            link(ins)
            for b in range(3):
                ins = nc.vector.max_index(mxi[:, b, :], mx[:, b, :], logit[:, b, :])
            link(ins)
            link(nc.vector.tensor_copy(mif[:, :, :], mxi[:, :, :]))
            iota = cst[:, C_IOTA:C_IOTA + E].unsqueeze(1).to_broadcast([P, 3, E])
            valid = cst[:, C_VALID:C_VALID + 3].unsqueeze(2).to_broadcast([P, 3, E])
            for k in range(TOPK):
                ins = TT(oh[k], iota, mif[:, :, k:k + 1].to_broadcast([P, 3, E]), ALU.is_equal)
            link(ins)
            TT(route, oh[0], oh[1], ALU.add)
            link(TT(rtmp, oh[2], oh[3], ALU.add))
            link(TT(route, route, rtmp, ALU.add))
            TT(route, route, valid, ALU.mult).then_inc(S.oh_ready, 1)
            TT(ge[:, :, :], mx[:, :, 0:TOPK], mx[:, :, 0:1].to_broadcast([P, 3, TOPK]), ALU.subtract).then_inc(S.rt_exp, 1)
            v.wait_ge(S.oh_ready, 1)
            v.wait_ge(S.rk_mm, 1)
            link(STT(rank, PS[:, 1, 0:3 * E].rearrange("p (b e) -> p b e", b=3), 1.0, route, ALU.add, ALU.mult))
            link(TS(rank, rank, -1.0, None, ALU.add))
            slots = cst[:, C_IOTA:C_IOTA + CAP].unsqueeze(1).to_broadcast([P, 3, CAP])

            def column(table, e):
                return table[:, :, e:e + 1] if isinstance(e, int) else table[:, :, bass.ds(e, 1)]

            def choose(e, n):
                if not (isinstance(n, int) and n == 0):
                    v.wait_ge(S.go_ok, n)
                    v.wait_ge(S.x_mm, n)
                TT(pick, slots, column(rank, e).to_broadcast([P, 3, CAP]), ALU.is_equal).then_inc(S.oh_ok, 1)

            def weigh_picks(e, n):
                v.wait_ge(S.oh_ok, n + 1)
                if not (isinstance(n, int) and n == 0):
                    v.wait_ge(S.go_mm, n)
                TT(gpick.rearrange("p b (h s) -> p b h s", h=2), pick.unsqueeze(2).to_broadcast([P, 3, 2, CAP]),
                   column(gate, e).unsqueeze(3).to_broadcast([P, 3, 2, CAP]), ALU.mult).then_inc(S.go_ok, 1)

            choose(0, 0)
            link(nc.vector.tensor_reduce(cmax, PS[0:1, 1, 3 * E:4 * E], AX, ALU.max))
            nc.vector.tensor_copy(most, cmax).then_inc(S.rt_ready, 1)
            v.wait_ge(S.rt_exp, 2)
            link(nc.vector.tensor_reduce(gs, ge, AX, ALU.add))
            link(nc.vector.reciprocal(gs, gs))
            link(TT(ge, ge, gs.unsqueeze(2).to_broadcast([P, 3, TOPK]), ALU.mult))
            link(TT(gate, oh[0], ge[:, :, 0:1].to_broadcast([P, 3, E]), ALU.mult))
            for k in range(1, TOPK):
                link(TT(rtmp, oh[k], ge[:, :, k:k + 1].to_broadcast([P, 3, E]), ALU.mult))
                link(TT(gate, gate, rtmp, ALU.add))
            v.wait_ge(S.rt_ready, 1)
            TS(sm[:, 26:27], ones[:, 0:1], 0.0, None, ALU.mult).then_inc(S.cnt_ready, 1)
            weigh_picks(0, 0)

            def add_spread(n, j):
                v.wait_ge(S.c_mm, 4 * n + j + 1)
                x = xc[:, :, :].rearrange("p (h k) t -> p h k t", h=2)[:, :, j, :]
                TT(x, x, PS[:, 2:4, 0:T], ALU.add).then_inc(S.added, 1)

            def block_(e, n, prev=True, following=True):
                first = isinstance(n, int) and n == 0
                if prev:
                    add_spread(n - 1, 0)
                if not first:
                    v.wait_ge(S.hid_ok, n)
                v.wait_ge(S.g1_mm, n + 1)
                TS(sg, PS[:, 0, :], LIMIT, None, ALU.min).then_inc(S.gmin, 1)
                v.wait_ge(S.sig, n + 1)
                TT(sg, sg, ss_, ALU.mult).then_inc(S.gated, 1)
                if following:
                    choose(e + 1, n + 1)
                if prev:
                    add_spread(n - 1, 1)
                    add_spread(n - 1, 2)
                v.wait_ge(S.u1_mm, n + 1)
                TS(su, PS[:, 1, :], LIMIT, -LIMIT, ALU.min, ALU.max).then_inc(S.u_rd, 1)
                v.wait_ge(S.gated, n + 1)
                v.wait_ge(S.u_rd, n + 1)
                if not first:
                    v.wait_ge(S.h_tr, n)
                STT(hm, su, 1.0, sg, ALU.add, ALU.mult).then_inc(S.hid_ok, 1)
                if prev:
                    add_spread(n - 1, 3)
                v.wait_ge(S.d1_mm, n + 1)
                nc.vector.tensor_copy(yb, PS[:, 4, :]).then_inc(S.y_ev, 1)
                if following:
                    weigh_picks(e + 1, n + 1)

            block_(0, 0, prev=False)
            with v.Fori(1, E - 1) as e:
                block_(e, e)
            block_(E - 1, E - 1, following=False)
            for j in range(4):
                add_spread(E - 1, j)

            def shift_ranks(c):
                v.wait_ge(S.added, 4 * c * E)
                TS(rank, rank, -float(CAP), None, ALU.add).then_inc(S.shifted, 1)
                v.wait_ge(S.shifted, c)

            def apart(e, n):
                choose(e, n)
                weigh_picks(e, n)
                block_(e, n, prev=False, following=False)
                for j in range(4):
                    add_spread(n, j)

            further(v, apart, before=shift_ranks, after=lambda n: v.wait_ge(S.added, 4 * n))
            v.wait_ge(S.added, 4 * E)
            TT(hT[:, :, :], xc[:, :, :], fv(FGP), ALU.mult).then_inc(S.h_ok, 1)
            TT(lt[:, :, :], xc[:, :, :], xc[:, :, :], ALU.mult).then_inc(S.sq_ok, 1)
            v.wait_ge(S.rms_ok, 3)
            link(nc.vector.reciprocal(rstd[:, :], rstd[:, :]))

            def ple_out(m):
                v.wait_ge(S.pg_sig, m + 1)
                TT(sgp[:, m, :], sgp[:, m, :], plT[:, m, :], ALU.mult).then_inc(S.gated_p, 1)
                v.wait_ge(S.gated_p, m + 1)
                TT(sgp[:, m, :], sgp[:, m, :], xc[:, m, :], ALU.add).then_inc(S.y_ok, 1)

            for m in range(KT):
                v.wait_ge(S.pg_mm, m + 1)
                TT(sgp[:, m, :], PS[:, m % 4, 0:T], rstd[:, :], ALU.mult).then_inc(S.pg_ev, 1)
                if m:
                    ple_out(m - 1)
            ple_out(KT - 1)

        @block.gpsimd
        def _(po):
            po.wait_ge(S.z_evac, ZX + KT)
            po.wait_ge(S.x_in, 32)
            po.dma_start(a["convp"], Z[:, ZX:ZX + KT, NP - 3:NP]).then_inc(S.conv_out, 16)
            po.dma_start(a["convs"][:, :, 0:2 * NS], feat[:, :, FSC + NS:FSC + 3 * NS]).then_inc(S.conv_out, 16)
            po.dma_start(a["convs"][:, :, 2 * NS:3 * NS], Z[:, ZX:ZX + KT, NP:T]).then_inc(S.conv_out, 16)
            po.wait_ge(S.qk_normed, 1)
            po.dma_start(rot[0:16, :, :], Z[16:32, 0:24, :]).then_inc(S.rot_in, 16)
            po.dma_start(rot[16:32, :, :], Z[0:16, 0:24, :]).then_inc(S.rot_in, 16)
            po.wait_ge(S.conv_done, 1)
            nc.gpsimd.memset(qdiag[2], 0.0)
            po.wait_ge(S.z_done, NZ)
            nc.gpsimd.memset(ring[:, 0, 2048:4096], 0.0).then_inc(S.q_zero, 1)
            po.wait_ge(S.ss_mm, 1)
            nc.gpsimd.memset(pdiag[2], 0.0).then_inc(S.p_zero, 1)
            for kv in range(2):
                for b, (t0, nt) in enumerate(BLK):
                    direct = kv == 1 and b < 2
                    po.wait_ge(S.tk_ev, 9 * kv + 3 * b + 3)
                    for g in range(NG):
                        src = vtok[:, b % 2, g * CH:(g + 1) * CH] if direct else stages[kv][b][g][0:nt]
                        if b == 2:
                            dst = a[f"kvs{g}"][:, WB[g] - 1, kv * CH:(kv + 1) * CH]
                        elif g == 0:
                            if b == 0:
                                continue
                            dst = a["kvp0"][:, kv * CH:(kv + 1) * CH]
                        else:
                            dst = a[f"kvp{g}"][t0:t0 + nt, kv * CH:(kv + 1) * CH]
                        po.dma_start(dst, src).then_inc(S.vt_out if kv else S.tk_out, 16)
            po.wait_ge(S.lru_y, 1)
            po.dma_start(a["hp"], lt[:, :, NP - 1:NP], allow_slow_non_contiguous=True).then_inc(S.h_out, 16)
            po.dma_start(a["hs"], lt[:, :, NP:T]).then_inc(S.h_out, 16)
            po.dma_start(xc[:, :, :], a["xT"]).then_inc(S.res_in, 16)


_OUTS = [("yT", (P, KT, T)), ("kvp0", (1, 1, 128, 2, HPG, HD)), ("kvp1", (1, 1, NP, 2, HPG, HD)),
         ("kvp2", (1, 1, NP, 2, HPG, HD)), ("convp", (P, KT, 3)), ("hp", (P, KT, 1)),
         ("kvs0", (1, NS, WB[0], 2, HPG, HD)), ("kvs1", (1, NS, WB[1], 2, HPG, HD)),
         ("kvs2", (1, NS, WB[2], 2, HPG, HD)), ("convs", (P, KT, 3 * NS)), ("hs", (P, KT, NS))]


def constants():
    import numpy as np
    c = np.zeros((P, NCST), np.float32)
    p = np.arange(P)
    c[:, C_ID:C_ID + P] = np.eye(P)
    c[:, C_ONE:C_ONE + P] = 1
    c[:, C_TRI:C_TRI + P] = p[:, None] < p[None, :]
    for qb, at in ((0, C_MASK0), (1, C_MASK1)):
        n = P * (qb + 1)
        rel = (qb * P + p)[:, None] - np.arange(n)[None, :]
        for g in range(NG):
            ok = (rel >= 0) & (rel % DIL[g] == 0) & (rel <= (128, 512, 2048)[g])
            c[:, at + g * n:at + (g + 1) * n] = np.where(ok, 0, -1e30)
    c[:, C_IOTA:C_IOTA + CAP] = np.arange(CAP)
    for b, (t0, nt) in enumerate(BLK):
        c[:, C_VALID + b] = p < nt
    c[:, C_EPS] = 1e-6
    half = HD // 8
    freqs = np.float32(500000.0) ** (-np.arange(half, dtype=np.float32) * np.float32(2.0 / (2 * half)))
    where = np.concatenate([np.arange(NP), np.full(NS, 1024)]).astype(np.float32)
    ang = (where[None, :] * freqs.astype(np.float32)[:, None]).astype(np.float32).astype(np.float64)
    cos, sin = np.cos(ang), np.sin(ang)
    rope = np.stack([np.concatenate([cos, cos]), np.concatenate([-sin, sin])], 1).astype(np.float32)
    return c, np.ascontiguousarray(rope)


def layout(i):
    import numpy as np
    i = {k: np.asarray(v) for k, v in i.items()}
    cst, rope = constants()

    def cols(v):
        v = np.moveaxis(v.reshape(-1, KT, P), 0, -1)
        return np.ascontiguousarray(v.transpose(1, 0, 2))

    order = [4, 5, 6, 7, 8, 9, 0, 1, 2, 3, 10, 11, 12, 13, 14, 15, 16]
    win = i["w_in"][0].reshape(KT, P, NPIECE, CH).transpose(2, 1, 0, 3)[order]
    sc = i["state_conv"][0].transpose(1, 0, 2).reshape(3 * NS, D)
    feat = np.concatenate([i["conv_w"][0], i["conv_b"], i["b_rg_a"], i["b_rg_x"], i["lru_lambda"], i["g_mix"],
                           i["g_ffn"], i["g_ple"], sc, i["state_h"][0]], 0)
    wrg = np.stack([i["w_rg_a"][0], i["w_rg_x"][0]]).reshape(2, 4, 2, P, 256).transpose(3, 0, 1, 2, 4)
    out = dict(
        cst=cst, rope=rope, feat=cols(feat),
        xT=cols(np.concatenate([i["x_prompt"][0], i["x_sample"][:, 0]], 0)),
        win=np.ascontiguousarray(win), gqk=np.ascontiguousarray(np.concatenate([i["g_q"], i["g_k"]], 0).T),
        wrg=np.ascontiguousarray(wrg.reshape(P, 4096)),
        w_router=i["w_router"][0], b_router=i["b_router"], w_br_lru=i["w_br_lru"][0], w_br_att=i["w_br_att"][0],
        w_out=i["w_out"][0], w_gu=i["w_gu"][0], w_down=i["w_down"][0], w_ple_gate=i["w_ple_gate"][0],
        w_ple=i["w_ple"][0])
    for g in range(NG):
        c = i[f"cache_kv_g{g}"][0]
        out[f"cache{g}"] = c.reshape(NS, WB[g], 2 * CH)
        out[f"kt{g}"] = np.ascontiguousarray(c[:, ::DIL[g], 0].transpose(3, 0, 2, 1)).reshape(P, -1)
    pp = np.concatenate([i["p_prompt"][0, 0], i["p_sample"][0, :, 0]], 0)
    out["pT"] = np.ascontiguousarray(pp.reshape(T, 2, P).transpose(2, 1, 0))
    b = i["b_gu"][0].reshape(E, 2, 2, CH).transpose(0, 2, 1, 3).reshape(E, 2 * D)
    out["bcat"] = np.concatenate([b, i["b_down"][0]], 1).reshape(E, 1, 3 * D)
    return out


def program(nc, arrays):
    a = {}
    for n, v in arrays.items():
        a[n] = nc.dram_tensor("in_" + n, v.shape, mybir.dt.from_np(v.dtype), kind="ExternalInput").ap()
    for n, s in _OUTS:
        ap = nc.dram_tensor("out_" + n, s, F32, kind="ExternalOutput").ap()
        if n.startswith("kvp"):
            ap = ap.rearrange("l o s c h d -> (l o s) (c h d)")
        elif n.startswith("kvs"):
            ap = ap.rearrange("l b s c h d -> (l b) s (c h d)")
        a[n] = ap
    for g in range(NG):
        n = SKEYS[g]
        a[f"kt{g}"] = a[f"kt{g}"].rearrange("p (s k) -> p s k", k=n)
    build(nc, a)


def kernel(**inputs):
    import numpy as np
    import concourse.bacc as bacc
    from concourse.bass_utils import run_bass_kernel_spmd

    arrays = layout(inputs)
    nc = bacc.Bacc("TRN2", target_bir_lowering=False, num_devices=1)
    program(nc, arrays)
    r = run_bass_kernel_spmd(nc, [{"in_" + n: v for n, v in arrays.items()}], core_ids=[0])
    return assemble({n: r.results[0]["out_" + n] for n, _ in _OUTS})


def assemble(o):
    import numpy as np

    def rows(v):
        return np.ascontiguousarray(v.transpose(2, 1, 0)).reshape(v.shape[2], D)

    y = rows(o["yT"])
    convs = rows(o["convs"]).reshape(3, NS, D).transpose(1, 0, 2)
    return (y[None, 0:NP], y[NP:T, None], o["kvp0"], o["kvp1"], o["kvp2"], rows(o["convp"])[None, None],
            rows(o["hp"])[None], o["kvs0"], o["kvs1"], o["kvs2"], np.ascontiguousarray(convs)[None],
            rows(o["hs"])[None])
```
